# Optimizing a Trainium2 kernel written in Bass

```python
import jax
import jax.numpy as jnp
from jax import lax
import numpy as np
import jax, jax.numpy as jnp

D_MODEL = 1024
BATCH = 1
SEQ = 512
DEPTH = 1

N_MEM = 256
EPS = 1e-6

GLA_HEADS = 4
GLA_DK = D_MODEL // 16
GLA_DV = D_MODEL // 8
GLA_RANK = 16
GLA_GATE_NORMALIZER = 16.0
GLA_CHUNK = 64

MOBA_HEADS = 4
MOBA_DH = D_MODEL // 16
MOBA_BLOCK = 256
MOBA_TOPK = 3
MOBA_QBLOCK = 128

MEM_HEADS = 4
MEM_DH = D_MODEL // 16

GLA_QK_W = GLA_HEADS * GLA_DK
GLA_V_W = GLA_HEADS * GLA_DV
MOBA_W = MOBA_HEADS * MOBA_DH
MEM_W = MEM_HEADS * MEM_DH
D_MIX = GLA_V_W + MOBA_W + MEM_W
IN_SPLITS = (GLA_QK_W, GLA_QK_W, GLA_V_W, GLA_V_W, GLA_RANK, MOBA_W, MOBA_W, MOBA_W, MEM_W)
D_IN = sum(IN_SPLITS)

N_GROUPS = 4
EXPERTS_PER_GROUP = 8
N_EXPERTS = N_GROUPS * EXPERTS_PER_GROUP
MOE_TOPK = 2
MOE_FF = D_MODEL // 2
MOE_BLOCK = 128


def rmsnorm(x, g):
    xf = x.astype(jnp.float32)
    y = xf * lax.rsqrt(jnp.mean(xf * xf, axis=-1, keepdims=True) + EPS)
    return (y * g.astype(jnp.float32)).astype(x.dtype)

def split_heads(t, n):
    b, s, w = t.shape
    return t.reshape(b, s, n, w // n).transpose(0, 2, 1, 3)

def merge_heads(t):
    b, n, s, d = t.shape
    return t.transpose(0, 2, 1, 3).reshape(b, s, n * d)

def alibi_slopes(n):
    return jnp.asarray(2.0 ** (-8.0 * np.arange(1, n + 1) / n), dtype=jnp.float32)

def gla_chunked(q, k, v, g):
    f32 = jnp.float32
    b, h, s, dk = q.shape
    dv = v.shape[-1]
    c = GLA_CHUNK
    n = s // c
    qf = q.astype(f32).reshape(b, h, n, c, dk) * (dk ** -0.5)
    kf = k.astype(f32).reshape(b, h, n, c, dk)
    vf = v.astype(f32).reshape(b, h, n, c, dv)
    cum = jnp.cumsum(g.astype(f32).reshape(b, h, n, c, dk), axis=3)
    cum_last = cum[:, :, :, -1:, :]
    q_dec = qf * jnp.exp(cum)
    k_inv = kf * jnp.exp(-cum)
    causal = jnp.tril(jnp.ones((c, c), dtype=bool))
    a_intra = jnp.where(causal, jnp.einsum('bhnik,bhnjk->bhnij', q_dec, k_inv), 0.0)
    o_intra = jnp.einsum('bhnij,bhnjv->bhniv', a_intra, vf)
    k_end = kf * jnp.exp(cum_last - cum)
    d_state = jnp.einsum('bhnck,bhncv->nbhkv', k_end, vf)
    chunk_decay = jnp.moveaxis(jnp.exp(cum_last[:, :, :, 0, :]), 2, 0)

    def step(state, inp):
        dec, ds = inp
        return state * dec[..., None] + ds, state

    _, s_prev = lax.scan(step, jnp.zeros((b, h, dk, dv), f32), (chunk_decay, d_state))
    o_inter = jnp.einsum('bhnck,nbhkv->bhncv', q_dec, s_prev)
    return (o_intra + o_inter).reshape(b, h, s, dv)

def moba_attention(q, k, v, slopes):
    f32 = jnp.float32
    b, h, s, d = q.shape
    nb = -(-s // MOBA_BLOCK)
    pad = nb * MOBA_BLOCK - s
    k_p = jnp.pad(k, ((0, 0), (0, 0), (0, pad), (0, 0)))
    v_p = jnp.pad(v, ((0, 0), (0, 0), (0, pad), (0, 0)))
    kb = k_p.reshape(b, h, nb, MOBA_BLOCK, d)
    vb = v_p.reshape(b, h, nb, MOBA_BLOCK, d)
    k_mean = jnp.mean(kb.astype(f32), axis=3)
    nb_gate = max(nb, MOBA_TOPK)
    scale = d ** -0.5
    bi = jnp.arange(b)[:, None, None, None]
    hi = jnp.arange(h)[None, :, None, None]
    blk_pos = jnp.arange(MOBA_BLOCK)
    m = slopes[None, :, None, None]
    n_sel = MOBA_TOPK * MOBA_BLOCK

    def query_block(qb):
        start = qb * MOBA_QBLOCK
        qc = lax.dynamic_slice_in_dim(q, start, MOBA_QBLOCK, axis=2)
        t = start + jnp.arange(MOBA_QBLOCK)
        own = start // MOBA_BLOCK
        gate = jnp.einsum('bhqd,bhnd->bhqn', qc.astype(f32), k_mean)
        gate = jnp.where(jnp.arange(nb) < own, gate, -jnp.inf)
        gate = jnp.pad(gate, ((0, 0), (0, 0), (0, 0), (0, nb_gate - nb)), constant_values=-jnp.inf)
        _, idx = lax.top_k(gate, MOBA_TOPK)
        idx = jnp.minimum(idx, nb - 1)
        valid = jnp.arange(MOBA_TOPK) < own
        k_sel = kb[bi, hi, idx]
        v_sel = vb[bi, hi, idx]
        s_sel = jnp.einsum('bhqd,bhqkjd->bhqkj', qc, k_sel, preferred_element_type=f32) * scale
        dist_sel = (t[:, None, None] - (idx[..., None] * MOBA_BLOCK + blk_pos)).astype(f32)
        s_sel = jnp.where(valid[:, None], s_sel - m[..., None] * dist_sel, -jnp.inf)
        k_own = lax.dynamic_slice_in_dim(k_p, own * MOBA_BLOCK, MOBA_BLOCK, axis=2)
        v_own = lax.dynamic_slice_in_dim(v_p, own * MOBA_BLOCK, MOBA_BLOCK, axis=2)
        dist_own = (t[:, None] - (own * MOBA_BLOCK + blk_pos)[None, :]).astype(f32)
        s_own = jnp.einsum('bhqd,bhjd->bhqj', qc, k_own, preferred_element_type=f32) * scale
        s_own = jnp.where(dist_own >= 0, s_own - m * dist_own, -jnp.inf)
        scores = jnp.concatenate([s_sel.reshape(b, h, MOBA_QBLOCK, n_sel), s_own], axis=-1)
        p = jax.nn.softmax(scores, axis=-1)
        p_sel = p[..., :n_sel].reshape(b, h, MOBA_QBLOCK, MOBA_TOPK, MOBA_BLOCK).astype(v.dtype)
        p_own = p[..., n_sel:].astype(v.dtype)
        o = (jnp.einsum('bhqkj,bhqkjd->bhqd', p_sel, v_sel, preferred_element_type=f32)
             + jnp.einsum('bhqj,bhjd->bhqd', p_own, v_own, preferred_element_type=f32))
        return o.astype(q.dtype)

    out = lax.map(query_block, jnp.arange(s // MOBA_QBLOCK))
    return out.transpose(1, 2, 0, 3, 4).reshape(b, h, s, d)

def memory_attention(q, mk, mv):
    f32 = jnp.float32
    scale = q.shape[-1] ** -0.5
    s = jnp.einsum('bhsd,bhmd->bhsm', q, mk, preferred_element_type=f32) * scale
    p = jax.nn.softmax(s, axis=-1).astype(mv.dtype)
    return jnp.einsum('bhsm,bhmd->bhsd', p, mv, preferred_element_type=f32).astype(q.dtype)

def hierarchical_moe(h, w_rg, b_rg, w_re, b_re, w_gate, w_up, w_down):
    f32 = jnp.float32
    b, s, d = h.shape
    t_tok = b * s
    xt = h.reshape(t_tok, d)
    lg = jnp.einsum('td,dg->tg', xt, w_rg).astype(f32) + b_rg.astype(f32)
    g_sel = jnp.argmax(lg, axis=-1)
    p_group = jnp.take_along_axis(jax.nn.softmax(lg, axis=-1), g_sel[:, None], axis=-1)
    le = jnp.einsum('td,gde->tge', xt, w_re).astype(f32) + b_re.astype(f32)
    le = jnp.take_along_axis(le, g_sel[:, None, None], axis=1)[:, 0]
    le_top, e_loc = lax.top_k(le, MOE_TOPK)
    gates = p_group * jax.nn.softmax(le_top, axis=-1)
    expert = (g_sel[:, None] * EXPERTS_PER_GROUP + e_loc).astype(jnp.int32)

    n_assign = t_tok * MOE_TOPK
    e_flat = expert.reshape(n_assign)
    t_flat = jnp.repeat(jnp.arange(t_tok, dtype=jnp.int32), MOE_TOPK)
    w_flat = gates.reshape(n_assign)
    order = jnp.argsort(e_flat)
    e_s, t_s, w_s = e_flat[order], t_flat[order], w_flat[order]
    counts = jax.ops.segment_sum(jnp.ones((n_assign,), jnp.int32), e_flat, num_segments=N_EXPERTS)
    padded = (counts + MOE_BLOCK - 1) // MOE_BLOCK * MOE_BLOCK
    starts = jnp.cumsum(counts) - counts
    pstarts = jnp.cumsum(padded) - padded
    dest = pstarts[e_s] + (jnp.arange(n_assign, dtype=jnp.int32) - starts[e_s])
    n_blocks = (n_assign + N_EXPERTS * (MOE_BLOCK - 1) + MOE_BLOCK - 1) // MOE_BLOCK
    n_rows = n_blocks * MOE_BLOCK
    tok_buf = jnp.full((n_rows,), t_tok, jnp.int32).at[dest].set(t_s)
    w_buf = jnp.zeros((n_rows,), f32).at[dest].set(w_s)
    block_start = jnp.arange(n_blocks, dtype=jnp.int32) * MOE_BLOCK
    block_expert = jnp.minimum(jnp.searchsorted(pstarts + padded, block_start, side='right'), N_EXPERTS - 1)
    x_pad = jnp.concatenate([xt, jnp.zeros((1, d), xt.dtype)], axis=0)

    def expert_block(args):
        toks, e = args
        xb = x_pad[toks]
        hid = jax.nn.silu(xb @ w_gate[e]) * (xb @ w_up[e])
        return hid @ w_down[e]

    y = lax.map(expert_block, (tok_buf.reshape(n_blocks, MOE_BLOCK), block_expert))
    y = y.reshape(n_rows, d) * w_buf[:, None].astype(y.dtype)
    out = jnp.zeros((t_tok + 1, d), y.dtype).at[tok_buf].add(y)[:t_tok]
    return out.reshape(b, s, d)

def first_inputs(seed: int = 0) -> dict:
    key = jax.random.key(seed)
    ks = jax.random.split(key, 24)
    L = DEPTH

    def nrm(k, shape, fan_in):
        return jax.random.normal(k, shape, jnp.float32) * fan_in ** -0.5

    def gain(k, shape):
        return 1.0 + 0.02 * jax.random.normal(k, shape, jnp.float32)

    return {
        'x': jax.random.normal(ks[0], (BATCH, SEQ, D_MODEL), jnp.float32),
        'mem': jax.random.normal(ks[1], (BATCH, N_MEM, D_MODEL), jnp.float32),
        'attn_norm_g': gain(ks[2], (L, D_MODEL)),
        'mem_norm_g': gain(ks[3], (L, D_MODEL)),
        'w_in': nrm(ks[4], (L, D_MODEL, D_IN), D_MODEL),
        'w_gla_gk': nrm(ks[5], (L, GLA_RANK, GLA_QK_W), GLA_RANK),
        'b_gla_gk': 0.1 * jax.random.normal(ks[6], (L, GLA_QK_W), jnp.float32),
        'gla_out_norm_g': gain(ks[7], (L, GLA_DV)),
        'moba_q_norm_g': gain(ks[8], (L, MOBA_DH)),
        'moba_k_norm_g': gain(ks[9], (L, MOBA_DH)),
        'w_mem_kv': nrm(ks[10], (L, D_MODEL, 2 * MEM_W), D_MODEL),
        'mem_q_norm_g': gain(ks[11], (L, MEM_DH)),
        'mem_k_norm_g': gain(ks[12], (L, MEM_DH)),
        'w_out': nrm(ks[13], (L, D_MIX, D_MODEL), D_MIX),
        'ffn_norm_g': gain(ks[14], (L, D_MODEL)),
        'w_router_group': nrm(ks[15], (L, D_MODEL, N_GROUPS), D_MODEL),
        'b_router_group': 0.01 * jax.random.normal(ks[16], (L, N_GROUPS), jnp.float32),
        'w_router_expert': nrm(ks[17], (L, N_GROUPS, D_MODEL, EXPERTS_PER_GROUP), D_MODEL),
        'b_router_expert': 0.01 * jax.random.normal(ks[18], (L, N_GROUPS, EXPERTS_PER_GROUP), jnp.float32),
        'w_gate': nrm(ks[19], (L, N_EXPERTS, D_MODEL, MOE_FF), D_MODEL),
        'w_up': nrm(ks[20], (L, N_EXPERTS, D_MODEL, MOE_FF), D_MODEL),
        'w_down': nrm(ks[21], (L, N_EXPERTS, MOE_FF, D_MODEL), MOE_FF),
    }

def first_block(x, mem, attn_norm_g, mem_norm_g, w_in, w_gla_gk, b_gla_gk, gla_out_norm_g,
              moba_q_norm_g, moba_k_norm_g, w_mem_kv, mem_q_norm_g, mem_k_norm_g, w_out,
              ffn_norm_g, w_router_group, b_router_group, w_router_expert, b_router_expert,
              w_gate, w_up, w_down):
    slopes = alibi_slopes(MOBA_HEADS)
    split_at = np.cumsum(IN_SPLITS)[:-1].tolist()
    for l in range(DEPTH):
        h = rmsnorm(x, attn_norm_g[l])
        proj = jnp.einsum('bsd,de->bse', h, w_in[l])
        gla_q, gla_k, gla_v, gla_r, gla_lr, mb_q, mb_k, mb_v, mem_q = jnp.split(proj, split_at, axis=-1)

        g_log = jax.nn.log_sigmoid((gla_lr @ w_gla_gk[l] + b_gla_gk[l]).astype(jnp.float32)) / GLA_GATE_NORMALIZER
        o_gla = gla_chunked(split_heads(gla_q, GLA_HEADS), split_heads(gla_k, GLA_HEADS),
                            split_heads(gla_v, GLA_HEADS), split_heads(g_log, GLA_HEADS))
        o_gla = rmsnorm(o_gla, gla_out_norm_g[l]).astype(x.dtype)
        o_gla = merge_heads(o_gla) * jax.nn.silu(gla_r)

        q_b = rmsnorm(split_heads(mb_q, MOBA_HEADS), moba_q_norm_g[l])
        k_b = rmsnorm(split_heads(mb_k, MOBA_HEADS), moba_k_norm_g[l])
        v_b = split_heads(mb_v, MOBA_HEADS)
        o_moba = merge_heads(moba_attention(q_b, k_b, v_b, slopes))

        mem_h = rmsnorm(mem, mem_norm_g[l])
        mem_k, mem_v = jnp.split(jnp.einsum('bmd,de->bme', mem_h, w_mem_kv[l]), 2, axis=-1)
        q_c = rmsnorm(split_heads(mem_q, MEM_HEADS), mem_q_norm_g[l])
        k_c = rmsnorm(split_heads(mem_k, MEM_HEADS), mem_k_norm_g[l])
        o_mem = merge_heads(memory_attention(q_c, k_c, split_heads(mem_v, MEM_HEADS)))

        mix = jnp.concatenate([o_gla, o_moba, o_mem], axis=-1)
        x = x + jnp.einsum('bse,ed->bsd', mix, w_out[l])

        x = x + hierarchical_moe(rmsnorm(x, ffn_norm_g[l]), w_router_group[l], b_router_group[l],
                                 w_router_expert[l], b_router_expert[l], w_gate[l], w_up[l], w_down[l])
    return x


LRU_WIDTH = D_MODEL
LRU_BLOCKS = 16
LRU_BLOCK_W = LRU_WIDTH // LRU_BLOCKS
LRU_C = 8.0
CONV_W = 4
ATT_HEADS = 16
ATT_HEAD_DIM = 64
ATT_WIDTH = ATT_HEADS * ATT_HEAD_DIM
Q_BLOCK = 128
D_FF = 4 * D_MODEL
PLE_DIM = 256
NORM_EPS = 1e-6

IN_SPLITS_2 = [LRU_WIDTH, LRU_WIDTH, ATT_WIDTH, ATT_WIDTH, ATT_WIDTH, D_MODEL, D_MODEL]
IN_WIDTH = sum(IN_SPLITS_2)


def rmsnorm_2(x, g):
    x32 = x.astype(jnp.float32)
    y = x32 * lax.rsqrt(jnp.mean(x32 * x32, axis=-1, keepdims=True) + NORM_EPS)
    return (y * g.astype(jnp.float32)).astype(x.dtype)

def causal_depthwise_conv(x, w, b):
    S = x.shape[1]
    xp = jnp.pad(x, ((0, 0), (CONV_W - 1, 0), (0, 0)))
    y = b
    for k in range(CONV_W):
        y = y + w[k] * xp[:, k:k + S]
    return y

def rg_lru(x, w_r, b_r, w_i, b_i, lam):
    B, S, W = x.shape
    xb = x.reshape(B, S, LRU_BLOCKS, LRU_BLOCK_W)
    r = jax.nn.sigmoid((jnp.einsum('bsnc,ncd->bsnd', xb, w_r).reshape(B, S, W) + b_r).astype(jnp.float32))
    i = jax.nn.sigmoid((jnp.einsum('bsnc,ncd->bsnd', xb, w_i).reshape(B, S, W) + b_i).astype(jnp.float32))
    log_a = -LRU_C * r * jax.nn.softplus(-lam.astype(jnp.float32))
    a = jnp.exp(log_a)
    mult = jnp.sqrt(-jnp.expm1(2.0 * log_a))
    u = mult * (i * x.astype(jnp.float32))

    def combine(left, right):
        a_l, u_l = left
        a_r, u_r = right
        return a_l * a_r, a_r * u_l + u_r

    _, h = lax.associative_scan(combine, (a, u), axis=1)
    return h.astype(x.dtype)

def stick_breaking_attention(q, k, v):
    B, H, S, Dh = q.shape
    n_blk = S // Q_BLOCK
    scale = Dh ** -0.5
    q_blocks = q.reshape(B, H, n_blk, Q_BLOCK, Dh).transpose(2, 0, 1, 3, 4)
    key_pos = jnp.arange(S)

    def one_block(args):
        q_blk, blk = args
        z = jnp.einsum('bhqd,bhkd->bhqk', q_blk, k).astype(jnp.float32) * scale
        q_pos = blk * Q_BLOCK + jnp.arange(Q_BLOCK)
        causal = key_pos[None, :] < q_pos[:, None]
        log_1m = jnp.where(causal, jax.nn.log_sigmoid(-z), 0.0)
        suffix = lax.cumsum(log_1m, axis=3, reverse=True) - log_1m
        att = jnp.where(causal, jnp.exp(jax.nn.log_sigmoid(z) + suffix), 0.0)
        return jnp.einsum('bhqk,bhkd->bhqd', att.astype(v.dtype), v)

    out = lax.map(one_block, (q_blocks, jnp.arange(n_blk)))
    return out.transpose(1, 2, 0, 3, 4).reshape(B, H, S, Dh)

def second_inputs(seed: int = 0) -> dict:
    key = jax.random.key(seed)
    ks = jax.random.split(key, 24)
    f32 = jnp.float32

    def nrm(k, shape, fan_in):
        return jax.random.normal(k, shape, f32) * (fan_in ** -0.5)

    def gain(k, shape):
        return 1.0 + 0.02 * jax.random.normal(k, shape, f32)

    u = jax.random.uniform(ks[10], (DEPTH, LRU_WIDTH), f32, 0.9, 0.999)
    a0 = u ** (1.0 / LRU_C)
    lam = jnp.log(a0) - jnp.log1p(-a0)
    return {
        'x': jax.random.normal(ks[0], (BATCH, SEQ, D_MODEL), f32),
        'p': jax.random.normal(ks[1], (DEPTH, BATCH, SEQ, PLE_DIM), f32),
        'norm_mix_g': gain(ks[2], (DEPTH, D_MODEL)),
        'w_in': nrm(ks[3], (DEPTH, D_MODEL, IN_WIDTH), D_MODEL),
        'conv_w': nrm(ks[4], (DEPTH, CONV_W, LRU_WIDTH), CONV_W),
        'conv_b': 0.02 * jax.random.normal(ks[5], (DEPTH, LRU_WIDTH), f32),
        'w_rgate': nrm(ks[6], (DEPTH, LRU_BLOCKS, LRU_BLOCK_W, LRU_BLOCK_W), LRU_BLOCK_W),
        'b_rgate': 0.02 * jax.random.normal(ks[7], (DEPTH, LRU_WIDTH), f32),
        'w_igate': nrm(ks[8], (DEPTH, LRU_BLOCKS, LRU_BLOCK_W, LRU_BLOCK_W), LRU_BLOCK_W),
        'b_igate': 0.02 * jax.random.normal(ks[9], (DEPTH, LRU_WIDTH), f32),
        'lru_lambda': lam,
        'w_br_lru': nrm(ks[11], (DEPTH, LRU_WIDTH, D_MODEL), LRU_WIDTH),
        'w_br_att': nrm(ks[12], (DEPTH, ATT_WIDTH, D_MODEL), ATT_WIDTH),
        'w_out': nrm(ks[13], (DEPTH, D_MODEL, D_MODEL), D_MODEL),
        'norm_mlp_g': gain(ks[14], (DEPTH, D_MODEL)),
        'w_mlp_up': nrm(ks[15], (DEPTH, D_MODEL, D_FF), D_MODEL),
        'w_mlp_down': nrm(ks[16], (DEPTH, D_FF, D_MODEL), D_FF),
        'norm_ple_g': gain(ks[17], (DEPTH, D_MODEL)),
        'w_ple_gate': nrm(ks[18], (DEPTH, D_MODEL, D_MODEL), D_MODEL),
        'w_ple': nrm(ks[19], (DEPTH, PLE_DIM, D_MODEL), PLE_DIM),
        'norm_final_g': gain(ks[20], (D_MODEL,)),
    }

def second_block(x, p, norm_mix_g, w_in, conv_w, conv_b, w_rgate, b_rgate, w_igate, b_igate,
              lru_lambda, w_br_lru, w_br_att, w_out, norm_mlp_g, w_mlp_up, w_mlp_down,
              norm_ple_g, w_ple_gate, w_ple, norm_final_g):
    B, S, _ = x.shape
    split_idx = [int(s) for s in np.cumsum(IN_SPLITS_2)[:-1]]
    for l in range(DEPTH):
        h = rmsnorm_2(x, norm_mix_g[l])
        proj = h @ w_in[l]
        u_x, u_g, q, k, v, g_lru, g_att = jnp.split(proj, split_idx, axis=-1)

        c = causal_depthwise_conv(u_x, conv_w[l], conv_b[l])
        y_lru = rg_lru(c, w_rgate[l], b_rgate[l], w_igate[l], b_igate[l], lru_lambda[l]) * jax.nn.gelu(u_g)

        to_heads = lambda t: t.reshape(B, S, ATT_HEADS, ATT_HEAD_DIM).transpose(0, 2, 1, 3)
        y_att = stick_breaking_attention(to_heads(q), to_heads(k), to_heads(v))
        y_att = y_att.transpose(0, 2, 1, 3).reshape(B, S, ATT_WIDTH)

        merged = jax.nn.sigmoid(g_lru) * (y_lru @ w_br_lru[l]) + jax.nn.sigmoid(g_att) * (y_att @ w_br_att[l])
        x = x + merged @ w_out[l]

        h2 = rmsnorm_2(x, norm_mlp_g[l])
        x = x + jnp.square(jax.nn.relu(h2 @ w_mlp_up[l])) @ w_mlp_down[l]

        h3 = rmsnorm_2(x, norm_ple_g[l])
        x = x + jax.nn.sigmoid(h3 @ w_ple_gate[l]) * (p[l] @ w_ple[l])
    return rmsnorm_2(x, norm_final_g)


def setup_inputs(seed=0):
    out = dict(first_inputs(seed))
    for name, value in second_inputs(seed + 1).items():
        if name != "x":
            out[name + "_2"] = value
    return out


def reference(
    x, mem, attn_norm_g, mem_norm_g, w_in, w_gla_gk, b_gla_gk, gla_out_norm_g, moba_q_norm_g,
    moba_k_norm_g, w_mem_kv, mem_q_norm_g, mem_k_norm_g, w_out, ffn_norm_g, w_router_group,
    b_router_group, w_router_expert, b_router_expert, w_gate, w_up, w_down, p_2, norm_mix_g_2,
    w_in_2, conv_w_2, conv_b_2, w_rgate_2, b_rgate_2, w_igate_2, b_igate_2, lru_lambda_2,
    w_br_lru_2, w_br_att_2, w_out_2, norm_mlp_g_2, w_mlp_up_2, w_mlp_down_2, norm_ple_g_2,
    w_ple_gate_2, w_ple_2, norm_final_g_2,
):
    x = first_block(
        x, mem, attn_norm_g, mem_norm_g, w_in, w_gla_gk, b_gla_gk, gla_out_norm_g,
        moba_q_norm_g, moba_k_norm_g, w_mem_kv, mem_q_norm_g, mem_k_norm_g, w_out, ffn_norm_g,
        w_router_group, b_router_group, w_router_expert, b_router_expert, w_gate, w_up, w_down,
    )
    return second_block(
        x, p_2, norm_mix_g_2, w_in_2, conv_w_2, conv_b_2, w_rgate_2, b_rgate_2, w_igate_2,
        b_igate_2, lru_lambda_2, w_br_lru_2, w_br_att_2, w_out_2, norm_mlp_g_2, w_mlp_up_2,
        w_mlp_down_2, norm_ple_g_2, w_ple_gate_2, w_ple_2, norm_final_g_2,
    )


_drawn_inputs = setup_inputs


def setup_inputs(seed=0):
    import zlib

    import numpy as np

    out = dict(_drawn_inputs(seed))
    spreads = {}
    factors = {'mem_norm_g': 8.0,
     'gla_out_norm_g': 9.52,
     'moba_q_norm_g': 8.0,
     'moba_k_norm_g': 8.0,
     'mem_q_norm_g': 8.0,
     'mem_k_norm_g': 8.0,
     'b_router_group': 25.015,
     'b_router_expert': 4.367,
     'norm_mix_g_2': 5.909,
     'b_rgate_2': 25.37,
     'b_igate_2': 21.732,
     'norm_mlp_g_2': 12.289,
     'norm_ple_g_2': 200.0,
     'norm_final_g_2': 22.829,
     'ffn_norm_g': 3.431,
     'conv_b_2': 3.933,
     'w_ple_gate_2': 21.968,
     'p_2': 8.0,
     'w_ple_2': 8.0}
    for name, (base, spread) in spreads.items():
        noise = np.random.default_rng([zlib.crc32(name.encode()), seed]).standard_normal(out[name].shape)
        drawn = base * np.exp(spread * noise) if base else spread * noise
        out[name] = jnp.asarray(drawn.astype(out[name].dtype))
    for name, factor in factors.items():
        out[name] = (out[name] * factor).astype(out[name].dtype)
    return out
```

```python
import math
from contextlib import ExitStack

import concourse.bass as bass
from concourse import mybir
import numpy as np

F32 = mybir.dt.float32
I32 = mybir.dt.int32
ALU = mybir.AluOpType
ACT = mybir.ActivationFunctionType
AX = mybir.AxisListType.X

P = 128
S = 512
D = 1024
KD = D // P
TT = S // P
NM = 256
MT = NM // P
PAN = KD * 512
RANK = 16
CH = 64
NE, FF = 32, 512
CAP = 64
NOVER = 2 * S // CAP - 1
NROWS = (NE + NOVER) * CAP
EPS = 1e-6
BIG = 1e30
JB = 7
HB = 16


def columns(widths):
    at, out = 0, {}
    for name, w in widths:
        out[name] = (at, at + w)
        at += w
    return out, at


CONST, NCONST = columns([
    ("ident", P), ("ones", P), ("blk", P), ("before", P), ("chunkmask", P), ("negtri", P), ("negones", P),
    ("stickbias", P), ("alibi", S), ("reset", S), ("half", 2), ("thresholds", 7), ("first32", 32), ("first4", 4),
    ("expert", 32), ("overblock", NOVER), ("token", TT), ("eps", 1), ("one", 1)])

GAINS, NGAIN = columns([
    ("attn_norm_g", 8), ("mem_norm_g", 8), ("ffn_norm_g", 8), ("norm_mix_g_2", 8), ("norm_mlp_g_2", 8),
    ("norm_ple_g_2", 8), ("norm_final_g_2", 8), ("b_gla_gk", 2), ("gla_out_norm_g", 1), ("moba_q_norm_g", 1),
    ("moba_k_norm_g", 1), ("mem_q_norm_g", 1), ("mem_k_norm_g", 1), ("conv_w_2", 32), ("conv_b_2", 8),
    ("b_rgate_2", 8), ("b_igate_2", 8), ("lru_lambda_2", 8), ("router_bias", 36)])


def plan():
    steps, jobs = [], []

    def step(kind, *args):
        steps.append((kind, *args))

    def job(kind, *args):
        jobs.append((kind, *args))
        steps.append((kind, *args))

    def attention(which, fill):
        units = [(which, pr, qt, hh) for pr in range(2) for qt in range(TT) for hh in range(2)]
        fill = list(fill)
        for u in range(len(units) + 3):
            if u < len(units):
                job("score", *units[u])
            if u >= 3 and (u - 3) % 2 == 1:
                job("values", *units[u - 3][:3])
            if 2 <= u < len(units) + 2:
                job("turn", *units[u - 2])
            if fill and u % 2 == 0:
                for f in fill.pop(0):
                    emit(f)
            if u < len(units):
                step("softmax", *units[u])
        if (len(units) - 1) % 2 == 1 and ("values", *units[-1][:3]) not in jobs:
            job("values", *units[-1][:3])
        for fs in fill:
            for f in fs:
                emit(f)

    def emit(f):
        (step if f[0] in STEPS_ONLY else job)(*f)
        if f[0] == "proj" and f[1] in ("mq", "mk", "cq", "ck"):
            job("headsum", f[1], f[2])

    step("mem_norm")
    step("norm", 0)
    for n in range(2):
        emit(("proj", "ck", n))
    for n in range(MT):
        emit(("proj", "cv", n))
    for n in range(2):
        emit(("proj", "cq", n))
    attention("mem", [[("proj", "mv", t)] for t in range(TT)] + [[("proj", "mq", n)] for n in range(2)]
              + [[("proj", "mk", n)] for n in range(2)])
    attention("moba", [[("proj", "gq", 0)], [("proj", "gq", 1)], [("proj", "gk", 0)], [("proj", "gk", 1)],
                       [("proj", "lr", 0), ("gate", 0), ("gate", 1)]] + [[("proj", "gv", t)] for t in range(TT)])
    step("gla_begin")
    step("decay", 0)
    job("proj", "r", 0)
    job("proj", "r", 1)
    for pr in range(2):
        job("turn_keys", pr)
        for hh in range(2):
            job("intra", pr, hh)
        for g in range(4):
            job("chunk_state", pr, g)
        if pr == 0:
            job("proj", "r", 2)
            job("proj", "r", 3)
        for hh in range(2):
            job("gla_out", pr, hh)
            job("gla_sum", pr, hh)
        if pr == 0:
            step("decay", 1)
    for n in range(KD):
        job("proj", "out", n)
        step("square", 1, n)
    step("norm", 1)
    job("router")
    for t in range(TT):
        for half in range(2):
            job("turn_h", t, half)
    step("route")
    job("rank")
    step("place")
    step("moe")
    for t in range(TT):
        for half in range(2):
            job("turn_y", t, half)
    step("norm", 2)
    for n in range(KD):
        job("proj", "ux", n)
        if n % 2:
            step("conv", n // 2)
            for m in (n - 1, n):
                job("lru_gate", "r", m)
                job("lru_gate", "i", m)
            step("lru", n // 2)
    for n in range(KD):
        job("proj", "ug", n)
    for name in ("q2", "k2"):
        for n in range(KD):
            job("proj", name, n)
    for half in range(2):
        for t in range(TT):
            job("proj", "v2", half * TT + t)
    step("stick")
    for name, br in (("gl", "bl"), ("ga", "ba")):
        for half in range(2):
            for n in range(4 * half, 4 * half + 4):
                job("proj", name, n)
            for n in range(4 * half, 4 * half + 4):
                job("proj", br, n)
    for n in range(KD):
        job("proj", "out2", n)
        step("square", 3, n)
    step("norm", 3)
    for n in range(4 * KD):
        job("proj", "up", n)
    for half in range(2):
        step("down", half)
        for n in range(4 * half, 4 * half + 4):
            jobs.append(("proj", "down", n))
            steps.append(("downed", n))
            step("square", 4, n)
    step("norm", 4)
    for half in range(2):
        for n in range(4 * half, 4 * half + 4):
            job("proj", "pg", n)
    for n in range(KD):
        job("proj", "ple", n)
        step("square", 5, n)
    step("norm", 5)
    return steps, jobs


STEPS_ONLY = ("softmax",)

PANELS1 = ["memkv", "mvcq", "mqk", "gqk", "gv", "r", "out0", "out1"]
PANELS2 = (["ux0", "ux1", "ug0", "ug1", "q20", "q21", "k20", "k21", "v20", "v21", "gl0", "bl0", "gl1", "bl1",
            "ga0", "ba0", "ga1", "ba1", "out20", "out21"] + [f"up{i}" for i in range(8)]
           + [f"down{i}" for i in range(8)] + ["pg0", "pg1", "ple"])
SLOTS1, SLOTS2 = 4, 5


def build(nc, a, out):
    steps, jobs = plan()
    J = {name: n for n, name in enumerate(jobs)}
    hn_index = {n[1:]: i for i, n in enumerate(x for x in jobs if x[0] == "headsum")}
    unit_index = {n[1:]: i for i, n in enumerate(x for x in steps if x[0] == "softmax")}

    with ExitStack() as ctx:
        def sb(name, n, dt=F32):
            return ctx.enter_context(nc.sbuf_tensor("sb_" + name, [P, n], dt))

        def sem(name):
            return ctx.enter_context(nc.semaphore(name))

        def dram(name, shape, dt):
            return nc.dram_tensor(name, shape, dt, kind="Internal").ap()

        slot = [sb(f"slot{i}", PAN) for i in range(6)]
        xT_ = sb("xT", KD * S)
        hT_ = sb("hT", KD * S)
        R = sb("R", 4 * KD * S)
        F = sb("F", 1280)
        cst = sb("cst", NCONST)
        prm = sb("prm", NGAIN)
        small = sb("small", 288)
        table_i = sb("table_i", 32, I32)
        ps_ = ctx.enter_context(nc.psum_tensor("ps", [P, 8, 512], F32))

        def C(name):
            lo, hi = CONST[name]
            return cst[:, lo:hi]

        def G(name, i=0):
            lo = GAINS[name][0] + i
            return prm[:, lo:lo + 1]

        def view(t, at, *dims):
            n = int(np.prod(dims))
            v = t[:, at:at + n]
            if len(dims) == 2:
                return v.rearrange("p (a b) -> p a b", a=dims[0])
            if len(dims) == 3:
                return v.rearrange("p (a b c) -> p a b c", a=dims[0], b=dims[1])
            return v

        xT, hT = view(xT_, 0, KD, S), view(hT_, 0, KD, S)
        sqb = view(F, 0, 2, S)
        std = view(F, 0, S)
        mixT = view(R, 0, KD, S)
        qpad = view(R, 4096, 4, S)
        kn = view(R, 6144, 2, S)
        vpad = view(R, 7168, TT, 4, P)
        cqpad = view(R, 9216, 4, S)
        ckn = view(R, 11264, 2, NM)
        cvpad = view(R, 11776, MT, 4, P)
        s_sb = view(R, 13312, 2, S)
        p_sb = view(R, 14336, 2, S)
        pT = view(R, 15360, 2, TT, P)
        memT = view(slot[5], 0, KD, NM)
        memh = view(slot[5], 2048, KD, NM)
        hn_raw = view(slot[5], 0, 2, S)
        hn_sq = view(slot[5], 1024, 2, S)
        gq = view(slot[4], 0, 2, S)
        gk = view(slot[4], 1024, 2, S)
        lrT = view(slot[4], 2048, S)
        zb = view(slot[4], 2560, 2, S)
        slope_b = view(slot[4], 3584, S)
        gv = view(R, 9216, TT, S)
        rs = view(R, 11264, 4, S)
        t1 = view(R, 4096, S)
        cum = view(R, 4608, S)
        ecum = view(R, 5120, S)
        einv = view(R, 5632, S)
        eend = view(R, 6144, S)
        kend_f = view(R, 6656, S)
        kend = view(R, 7168, 2, TT, P)
        osq = view(R, 8192, S)
        ogn = view(R, 8704, S)
        qdec = view(R, 13312, 2, S)
        ostd = view(R, 14336, S)
        at_sb = view(R, 14848, 2, TT, P)
        kinv = view(slot[5], 0, 4, S)
        state = view(slot[5], 2048, 8, 2 * P)
        htok = view(R, 0, TT, D)
        xg = [view(R, 4096 + 1024 * b, D) for b in range(2)]
        yout = [view(R, 6144 + 1024 * b, D) for b in range(2)]
        xgT = [view(R, 8192 + 512 * b, KD, CAP) for b in range(2)]
        sg = [view(R, 9216 + 256 * b, 4, CAP) for b in range(2)]
        hid = [view(R, 9728 + 256 * b, 4, CAP) for b in range(2)]
        lg = view(R, 10240, TT, 36)
        wk32 = view(R, 10400, TT, 32)
        wk32b = view(R, 10528, TT, 32)
        oh = [view(R, 10656 + 128 * k, TT, 32) for k in range(2)]
        M = view(R, 10912, TT, 32)
        dest = view(R, 11040, TT, 32)
        w4 = view(R, 11168, TT, 4)
        w4b = view(R, 11184, TT, 4)
        cmp = view(R, 11200, 32, 7)
        cmp2 = view(R, 11424, NOVER, 32)
        cnt, nb, obend, dd = (view(R, 11904 + 32 * i, 32) for i in range(4))
        otab = view(R, 12032, NOVER)
        w_router = view(R, 15872, KD, 36)
        col = [view(R, 12600 + 4 * i, TT) for i in range(12)]
        gate_w = view(small, 0, 2, TT)
        dest_i = table_i[:, 0:8]
        token_i = table_i[:, 8:12]
        over_i = table_i[:, 12:12 + NOVER + 1]
        idx = [sb(f"idx{b}", 1, I32) for b in range(2)]
        zeros_i = sb("zeros_i", NROWS // CAP, I32)
        yg = [view(R, 1024 * i, D) for i in range(2 * TT)]
        q2, k2, v2, yl = (view(R, 4096 * i, KD, S) for i in range(4))
        v2 = view(R, 8192, TT, D)
        lc, lr_, li, la = (view(R, 8192 + 1024 * i, 2, S) for i in range(4))
        uxp = view(slot[5], 0, 2, S + 4)
        lt = view(slot[5], 1032, 2, S)
        lh = view(slot[5], 2056, S)
        sp8 = view(small, 16, KD)
        nsp8 = view(small, 24, KD)
        lw = [view(small, 32 + 8 * i, KD) for i in range(6)]
        row_max, row_neg, row_sum, row_inv = (view(small, 96 + 2 * i, 2) for i in range(4))
        dec = [view(small, 112 + 8 * i, 8) for i in range(2)]
        w_lr = view(R, 0, KD * RANK)
        w_gk = view(R, 128, 2 * P)
        w_bd = view(F, 1024, 2, P)
        SEG = [(0, 512), (512, 384), (1024, 256), (896, 128)]
        Lb = [view(slot[5], 0, 1280), view(slot[5], 1280, 1280)]
        att = [view(slot[5], 2560, 1280), F[:, :]]
        merged = view(R, 4096, KD, S)
        sgate = [view(slot[5], 512 * i, S) for i in range(4)]
        prod = view(slot[5], 2048, S)
        hidden = view(R, 0, 4 * KD, S)
        pgs = view(R, 0, KD, S)
        pT2 = view(R, 4096, 2, S)

        h_dram = dram("h_rows", (S, D), F32)
        y_dram = dram("y_rows", (NROWS, D), F32)
        slot_dram = dram("row_tokens", (NROWS, 1), I32)

        pe_done = sem("pe_done")
        bank_free = [sem(f"bank_free{b}") for b in range(JB)]
        ld = {n: sem(f"ld_{n}") for n in ("cst", "prm", "mem", "x", "wlr", "wgk", "router", "p")}
        ld_bd = [sem(f"ld_bd{j}") for j in range(2)]
        pan1 = [sem(f"pan1_{i}") for i in range(SLOTS1)]
        pan2 = [sem(f"pan2_{i}") for i in range(SLOTS2)]
        act_chain, dve_chain, pool_chain = sem("act_chain"), sem("dve_chain"), sem("pool_chain")
        mem_sq, mem_sum, mem_std, mem_h = sem("mem_sq"), sem("mem_sum"), sem("mem_std"), sem("mem_h")
        squared, summed, std_done, h_ready = sem("squared"), sem("summed"), sem("std_done"), sem("h_ready")
        x_new, relu_done, gla_o = sem("x_new"), sem("relu_done"), sem("gla_o")
        zeroed = sem("zeroed")
        hn_in, hn_std, hn_done = sem("hn_in"), sem("hn_std"), sem("hn_done")
        slope_ok = sem("slope_ok")
        s_ready, neg_ready, exp_done, p_ready = sem("s_ready"), sem("neg_ready"), sem("exp_done"), sem("p_ready")
        gla_go, state_zero = sem("gla_go"), sem("state_zero")
        lsig, cum_done, dec_exp, qk_ready = sem("lsig"), sem("cum_done"), sem("dec_exp"), sem("qk_ready")
        st_done = sem("st_done")
        o_sq, o_std, o_done = sem("o_sq"), sem("o_std"), sem("o_done")
        r_exp, r_gd, r_m, r_dest = sem("r_exp"), sem("r_gd"), sem("r_m"), sem("r_dest")
        r_e2in, r_e2 = sem("r_e2in"), sem("r_e2")
        h_stored, zeros_set, zeros_stored, tokens_stored = (
            sem("h_stored"), sem("zeros_set"), sem("zeros_stored"), sem("tokens_stored"))
        m_w = [sem(f"m_w{i}") for i in range(6)]
        m_idx, m_x, m_turned, m_xT, m_gu, m_silu, m_hid, m_down, m_y, m_st = (
            [sem(f"{n}{b}") for b in range(2)] for n in
            ("m_idx", "m_x", "m_turned", "m_xT", "m_gu", "m_silu", "m_hid", "m_down", "m_y", "m_st"))
        o_w = sem("o_w")
        o_idx, o_x, o_turned, o_xT, o_gu, o_silu, o_hid, o_down, o_y, o_st = (
            sem(n) for n in ("o_idx", "o_x", "o_turned", "o_xT", "o_gu", "o_silu", "o_hid", "o_down", "o_y", "o_st"))
        y_got, y_mixed = [sem(f"y_got{t}") for t in range(TT)], sem("y_mixed")
        pad_zero, conv_done, gates_done, lru_exp, lru_m2, lru_mult, lru_done = (
            sem(n) for n in ("pad_zero", "conv_done", "gates_done", "lru_exp", "lru_m2", "lru_mult", "lru_done"))
        lam_exp, lam_done = sem("lam_exp"), sem("lam_done")
        gelu_done, yl_done = sem("gelu_done"), sem("yl_done")
        z_done, sp_log, sp_done, tri_done, att_done, pv_done, pv_out = (
            sem(n) for n in ("z_done", "sp_log", "sp_done", "tri_done", "att_done", "pv_done", "pv_out"))
        sig_done, sig_used, merge_done = sem("sig_done"), sem("sig_used"), sem("merge_done")
        hid_done = sem("hid_done")
        stored = sem("stored")
        passed = {e: sem(f"passed_{e}") for e in ("pool", "pe", "sp")}

        def bank(name):
            return ps_[:, J[name] % JB, :]

        def finished(eng, name):
            eng.wait_ge(pe_done, J[name] + 1)

        def taken(eng, name):
            eng.wait_ge(bank_free[J[name] % JB], J[name] // JB + 1)

        def frees(ins, name):
            return ins.then_inc(bank_free[J[name] % JB], 1)

        w_in, w_in2 = a["w_in"], a["w_in_2"]

        def panel_src(name):
            def cols(w, lo):
                return w[0, :, lo:lo + 512].rearrange("(k p) n -> p k n", p=P)
            if name == "memkv":
                return cols(a["w_mem_kv"], 0)
            if name in ("gqk", "gv", "r", "mqk", "mvcq"):
                return cols(w_in, {"gqk": 0, "gv": 512, "r": 1024, "mqk": 1552, "mvcq": 2064}[name])
            if name in ("out0", "out1"):
                return cols(a["w_out"], 512 * int(name[-1]))
            base, n = name[:-1], name[-1]
            if base in ("ux", "ug", "q2", "k2", "v2", "gl", "ga"):
                return cols(w_in2, ["ux", "ug", "q2", "k2", "v2", "gl", "ga"].index(base) * D + 512 * int(n))
            if base in ("bl", "ba", "out2", "up", "pg"):
                w = a[{"bl": "w_br_lru_2", "ba": "w_br_att_2", "out2": "w_out_2", "up": "w_mlp_up_2",
                       "pg": "w_ple_gate_2"}[base]]
                return cols(w, 512 * int(n))
            if base == "down":
                half, kp = int(n) // 4, int(n) % 4
                return a["w_mlp_down_2"][0, D * kp:D * kp + D, 512 * half:512 * half + 512].rearrange(
                    "(k p) n -> p k n", p=P)
            return a["w_ple_2"][0].rearrange("(k p) n -> p k n", p=P)

        def where(name, n):
            if name in ("ck", "cv"):
                return "memkv", (0 if name == "ck" else 256)
            if name in ("cq", "mv"):
                return "mvcq", (256 if name == "cq" else 0)
            if name in ("mq", "mk"):
                return "mqk", (0 if name == "mq" else 256)
            if name in ("gq", "gk"):
                return "gqk", (0 if name == "gq" else 256)
            if name in ("gv", "r"):
                return name, 0
            if name in ("v2",):
                return f"v2{n // TT}", 0
            if name in ("out", "ux", "ug", "q2", "k2", "gl", "bl", "ga", "ba", "out2", "pg", "up"):
                return f"{name}{n // 4}", 0
            return name, 0

        def last_use(panel):
            for nm in reversed(jobs):
                if nm[0] == "proj":
                    if nm[1] == "down" and panel.startswith("down"):
                        half = int(panel[-1]) // 4
                        return ("proj", "down", 4 * half + 3)
                    if nm[1] not in ("down", "lr") and where(nm[1], nm[2])[0] == panel:
                        return nm
            raise KeyError(panel)

        down_read = sem("down_read")

        def panel_at(name):
            if name in PANELS1:
                n = PANELS1.index(name)
                return slot[n % SLOTS1], pan1[n % SLOTS1], 16 * (n // SLOTS1 + 1)
            n = PANELS2.index(name)
            return slot[n % SLOTS2], pan2[n % SLOTS2], 16 * (n // SLOTS2 + 1)

        def expert_src(name, e):
            w = a[name][0, e]
            return w.rearrange("(k p) n -> p k n", p=P)

        def pairs(eng, body):
            body(0)
            with eng.Fori(1, NE // 2) as i:
                body(i)

        def overflow(eng, n_over, body):
            with eng.If(n_over > 0):
                body(0)
                with eng.Fori(1, NOVER) as i:
                    with eng.If(i < n_over):
                        body(i)

        def free(eng, s, v):
            if type(v) is not int or v > 0:
                eng.wait_ge(s, v)

        def prev_unit(u):
            return next(n for n, i in unit_index.items() if i == u)

        def flat(h):
            b0 = 3 * (h % 2)
            return ps_[:, b0:b0 + 3, :].rearrange("p a b -> p (a b)")[:, 0:1280]

        GU = ("w_gate", "w_up")
        block = ctx.enter_context(nc.Block())

        @block.sync
        def _(sp):
            def load(dst, src, s):
                sp.dma_start(dst, src).then_inc(s, 16)

            load(cst[:, :], a["consts"], ld["cst"])
            load(prm[:, :], a["gains"], ld["prm"])
            load(memT, a["memT"].rearrange("(k p) n -> p k n", p=P), ld["mem"])
            load(slot[0][:, :].rearrange("p (k n) -> p k n", k=KD), panel_src("memkv"), pan1[0])
            load(xT, a["xT"].rearrange("(k p) n -> p k n", p=P), ld["x"])
            load(w_lr.rearrange("p (k n) -> p k n", k=KD),
                 w_in[0, :, 1536:1536 + RANK].rearrange("(k p) n -> p k n", p=P), ld["wlr"])
            load(w_gk[0:RANK, :], a["w_gla_gk"][0], ld["wgk"])
            for n, name in enumerate(PANELS1):
                if n == 0:
                    continue
                if n >= SLOTS1:
                    finished(sp, last_use(PANELS1[n - SLOTS1]))
                load(slot[n % SLOTS1][:, :].rearrange("p (k n) -> p k n", k=KD), panel_src(name), pan1[n % SLOTS1])

            def pair_load(e, b, part):
                if part == "gu":
                    for j in range(2):
                        load(slot[2 * b + j][:, :].rearrange("p (k n) -> p k n", k=KD), expert_src(GU[j], e),
                             m_w[2 * b + j])
                else:
                    load(slot[4 + b][:, :].rearrange("p (k n) -> p k n", k=4), expert_src("w_down", e), m_w[4 + b])

            finished(sp, ("gla_sum", 1, 1))
            sp.wait_ge(st_done, 14 * 2)
            sp.wait_ge(qk_ready, 2)
            load(w_router, a["w_router"], ld["router"])
            pair_load(0, 0, "down")
            pair_load(1, 1, "down")
            for n in (4, 5):
                finished(sp, last_use(PANELS1[n]))
            pair_load(0, 0, "gu")
            for n in (6, 7):
                finished(sp, last_use(PANELS1[n]))
            pair_load(1, 1, "gu")
            with sp.Fori(1, NE // 2) as i:
                for b in range(2):
                    sp.wait_ge(m_gu[b], i)
                    pair_load(2 * i + b, b, "gu")
                for b in range(2):
                    sp.wait_ge(m_down[b], i)
                    pair_load(2 * i + b, b, "down")
            for b in range(2):
                sp.wait_ge(m_gu[b], NE // 2)
                sp.wait_ge(m_down[b], NE // 2)
            sp.wait_ge(r_dest, 1)
            n_over = sp.value_load(over_i[0:1, NOVER:NOVER + 1], min_val=0, max_val=NOVER)

            def over_load(i):
                e = sp.value_load(over_i[0:1, bass.ds(i, 1)], min_val=0, max_val=NE - 1)
                for j in range(2):
                    load(slot[j][:, :].rearrange("p (k n) -> p k n", k=KD), expert_src(GU[j], e), o_w)
                load(slot[4][:, :].rearrange("p (k n) -> p k n", k=4), expert_src("w_down", e), o_w)
                sp.wait_ge(o_st, 16 * i + 16)
                sp.sem_inc(passed["sp"], 1)

            overflow(sp, n_over, over_load)
            for n, name in enumerate(PANELS2):
                if n >= SLOTS2:
                    prev = PANELS2[n - SLOTS2]
                    if prev.startswith("down") and int(prev[-1]) % 4 < 3:
                        sp.wait_ge(down_read, 3 * (int(prev[-1]) // 4) + int(prev[-1]) % 4 + 1)
                    else:
                        finished(sp, last_use(prev))
                dst = slot[n % SLOTS2]
                if name == "ple":
                    finished(sp, ("proj", "down", 7))
                    load(pT2, a["pT"].rearrange("(k p) n -> p k n", p=P), ld["p"])
                    load(dst[:, 0:2 * D].rearrange("p (k n) -> p k n", k=2), panel_src(name), pan2[n % SLOTS2])
                else:
                    load(dst[:, :].rearrange("p (k n) -> p k n", k=KD), panel_src(name), pan2[n % SLOTS2])
            for k in range(KD):
                sp.wait_ge(h_ready, 8 * 5 + k + 1)
                sp.dma_start(out[k * P:(k + 1) * P, :], hT[:, k, :]).then_inc(stored, 16)
            sp.wait_ge(stored, 16 * KD)

        @block.gpsimd
        def _(pool):
            chain = [0]

            def link(ins):
                chain[0] += 1
                ins.then_inc(pool_chain, 1)
                pool.wait_ge(pool_chain, chain[0])

            nc.gpsimd.memset(R[:, 4096:6144], 0.0).then_inc(zeroed, 1)
            nc.gpsimd.memset(R[:, 7168:11264], 0.0).then_inc(zeroed, 1)
            nc.gpsimd.memset(R[:, 11776:12800], 0.0).then_inc(zeroed, 1)
            nc.gpsimd.memset(zeros_i[0:CAP, :], 0).then_inc(zeros_set, 1)
            pool.wait_ge(zeros_set, 1)
            pool.dma_start(slot_dram.rearrange("(b s) o -> b (s o)", b=CAP), zeros_i[0:CAP, :]).then_inc(zeros_stored, 16)
            nc.gpsimd.memset(R[:, 12800:13312], 0.0).then_inc(zeros_set, 1)
            pool.wait_ge(zeros_set, 2)
            zp = NOVER * CAP // 8
            pool.dma_start(y_dram[NE * CAP:NROWS, :].rearrange("(z r) (c n) -> z (r c) n", z=zp, c=2),
                           R[0:zp, 12800:13312].unsqueeze(1).to_broadcast([zp, 16, 512])).then_inc(zeros_stored, 16)
            pool.wait_ge(ld["cst"], 16)
            link(nc.gpsimd.tensor_copy(token_i, C("token")))
            finished(pool, ("values", "moba", 1, TT - 1))
            pool.wait_ge(hn_done, 8)
            nc.gpsimd.memset(slot[5][:, :], 0.0).then_inc(state_zero, 1)
            pool.wait_ge(zeros_stored, 32)
            pool.wait_ge(r_dest, 1)
            for k in range(2):
                for t in range(TT):
                    nc.gpsimd.indirect_dma_start(
                        slot_dram, bass.IndirectOffsetOnAxis(ap=dest_i[:, k * TT + t:k * TT + t + 1], axis=0),
                        token_i[:, t:t + 1], None).then_inc(tokens_stored, 16)
            pool.wait_ge(tokens_stored, 16 * 2 * TT)
            pool.wait_ge(h_stored, 16 * TT)

            def fetch(first, b, i, s_idx, s_x, s_free):
                free(pool, s_free, i)
                pool.dma_start(idx[b][0:CAP, :], slot_dram[bass.ds(first, CAP), :]).then_inc(s_idx, 16)
                pool.wait_ge(s_idx, 16 * i + 16)
                pool.sem_inc(passed["pool"], 1)
                nc.gpsimd.indirect_dma_start(
                    xg[b][0:CAP, :], None, h_dram,
                    bass.IndirectOffsetOnAxis(ap=idx[b][0:CAP, :], axis=0)).then_inc(s_x, 16)
                pool.wait_ge(s_x, 16 * i + 16)

            pairs(pool, lambda i: [fetch((2 * i + b) * CAP, b, i, m_idx[b], m_x[b], m_turned[b]) for b in range(2)])
            for b in range(2):
                pool.wait_ge(m_st[b], 16 * (NE // 2))
            n_over = nc.gpsimd.value_load(over_i[0:1, NOVER:NOVER + 1], min_val=0, max_val=NOVER)

            def over_fetch(i):
                fetch((NE + i) * CAP, 0, i, o_idx, o_x, o_turned)
                pool.wait_ge(o_st, 16 * i + 16)

            overflow(pool, n_over, over_fetch)
            for t in range(TT):
                for k in range(2):
                    nc.gpsimd.indirect_dma_start(
                        yg[2 * t + k], None, y_dram,
                        bass.IndirectOffsetOnAxis(ap=dest_i[:, k * TT + t:k * TT + t + 1], axis=0)
                    ).then_inc(y_got[t], 16)
            for n in range(KD):
                for j, which in enumerate("ri"):
                    if n:
                        finished(pool, ("lru_gate", which, n - 1))
                    else:
                        finished(pool, ("turn_y", TT - 1, 1))
                        pool.wait_ge(h_ready, 8 * 2)
                    pool.dma_start(w_bd[:, j, :], a["gate_blocks"][2 * n + j]).then_inc(ld_bd[j], 16)

        @block.tensor
        def _(pe):
            def begin(name):
                n = J[name]
                if n >= JB:
                    pe.wait_ge(bank_free[n % JB], n // JB)
                return bank(name)

            def end(ins):
                ins.then_inc(pe_done, 1)

            def panel(name):
                t, s, v = panel_at(name)
                pe.wait_ge(s, v)
                return t[:, :].rearrange("p (k n) -> p k n", k=KD)

            def h_wait(name, k):
                norm = (0 if name in ("cq", "mq", "mk", "mv", "gq", "gk", "lr", "gv", "r") else
                        2 if name in ("ux", "ug", "q2", "k2", "v2", "gl", "ga") else
                        3 if name == "up" else 4 if name == "pg" else None)
                if norm is not None:
                    pe.wait_ge(h_ready, 8 * norm + k + 1)

            tok_major = ("mv", "cv", "gv", "v2")

            def project(name, n):
                o = begin(("proj", name, n))
                if name == "lr":
                    pe.wait_ge(ld["wlr"], 16)
                    w = w_lr.rearrange("p (k n) -> p k n", k=KD)
                    for k in range(KD):
                        ins = nc.tensor.matmul(o[0:RANK, :], w[:, k, :], hT[:, k, :], start=(k == 0), stop=(k == KD - 1))
                    end(ins)
                    return
                pn, off = where(name, n)
                w = panel(pn)
                if name == "ple":
                    w = panel_at(pn)[0][:, 0:2 * D].rearrange("p (k n) -> p k n", k=2)
                    pe.wait_ge(ld["p"], 16)
                    for k in range(2):
                        ins = nc.tensor.matmul(o, w[:, k, n * P:(n + 1) * P], pT2[:, k, :], start=(k == 0), stop=(k == 1))
                    end(ins)
                    return
                src = hT
                if name in ("ck", "cv"):
                    src = memh
                elif name == "out":
                    src = mixT
                elif name == "bl":
                    src = yl
                elif name == "ba":
                    src = q2
                elif name == "out2":
                    src = merged
                for k in range(KD):
                    if name in ("ck", "cv"):
                        pe.wait_ge(mem_h, k + 1)
                    elif name == "bl":
                        pe.wait_ge(yl_done, k + 1)
                    elif name == "ba":
                        pe.wait_ge(pv_out, HB)
                    elif name == "out2":
                        pe.wait_ge(merge_done, k + 1)
                    elif name == "out" and k < 4:
                        pe.wait_ge(o_done, k + 1)
                    elif name == "out":
                        if k == 4 and n == 0:
                            for w_ in ("mem", "moba"):
                                for pr in range(2):
                                    for qt in range(TT):
                                        taken(pe, ("values", w_, pr, qt))
                    else:
                        h_wait(name, k)
                    if name in tok_major:
                        t = n % TT
                        width = {"mv": 256, "cv": 256, "gv": 512, "v2": 512}[name]
                        ins = nc.tensor.matmul(o[:, 0:width], src[:, k, t * P:(t + 1) * P], w[:, k, off:off + width],
                                               start=(k == 0), stop=(k == KD - 1))
                    else:
                        c = off + (n % 4) * P
                        width = NM if name == "ck" else S
                        ins = nc.tensor.matmul(o[:, 0:width], w[:, k, c:c + P], src[:, k, :],
                                               start=(k == 0), stop=(k == KD - 1))
                end(ins)

            def norm_sum(norm, n):
                if n == 0 and norm > 0:
                    pe.wait_ge(std_done, norm)
                if n == 0 and norm == 0:
                    pe.wait_ge(mem_std, 1)
                pe.wait_ge(squared, 8 * norm + n + 1)
                ins = nc.tensor.matmul(ps_[:, 7, :], C("ones"), (hT[:, n, :] if norm == 0 else sqb[:, n % 2, :]),
                                       start=(n == 0), stop=(n == KD - 1), skip_group_check=True)
                ins.then_inc(summed, 1)

            for st in steps:
                kind, arg = st[0], st[1:]
                if kind == "mem_norm":
                    pe.wait_ge(ld["cst"], 16)
                    pe.wait_ge(mem_sq, 1)
                    for k in range(KD):
                        ins = nc.tensor.matmul(ps_[:, 7, 0:NM], C("ones"), memh[:, k, :], start=(k == 0), stop=(k == KD - 1))
                    ins.then_inc(mem_sum, 1)
                elif kind == "norm":
                    norm = arg[0]
                    if norm == 0:
                        for n in range(KD):
                            norm_sum(0, n)
                elif kind == "square":
                    norm_sum(*arg)
                elif kind == "proj":
                    project(*arg)
                elif kind == "headsum":
                    o = begin(st)
                    i = hn_index[arg]
                    pe.wait_ge(hn_in, i + 1)
                    width = NM if arg[0] == "ck" else S
                    end(nc.tensor.matmul(o[:, 0:width], C("blk"), hn_sq[:, i % 2, 0:width], start=True, stop=True))
                elif kind == "score":
                    which, pr, qt, hh = arg
                    o = begin(st)
                    h = 2 * pr + hh
                    if which == "mem":
                        pe.wait_ge(hn_done, 4)
                        end(nc.tensor.matmul(o[:, 0:NM], cqpad[:, h, qt * P:(qt + 1) * P], ckn[:, pr, :], start=True, stop=True))
                    else:
                        pe.wait_ge(hn_done, 8)
                        w_ = P * (qt + 1)
                        end(nc.tensor.matmul(o[:, 0:w_], qpad[:, h, qt * P:(qt + 1) * P], kn[:, pr, 0:w_], start=True, stop=True))
                elif kind == "turn":
                    which, pr, qt, hh = arg
                    u = unit_index[arg]
                    o = begin(st)
                    pe.wait_ge(p_ready, u + 1)
                    for kt in range(MT if which == "mem" else qt + 1):
                        ins = nc.tensor.transpose(o[:, kt * P:(kt + 1) * P], p_sb[:, u % 2, kt * P:(kt + 1) * P], C("ident"))
                    end(ins)
                elif kind == "values":
                    which, pr, qt = arg
                    o = begin(st)
                    nk = MT if which == "mem" else qt + 1
                    if which == "mem":
                        for t in range(MT):
                            taken(pe, ("proj", "cv", t))
                    else:
                        for t in range(qt + 1):
                            taken(pe, ("proj", "mv", t))
                    for hh in range(2):
                        taken(pe, ("turn", which, pr, qt, hh))
                        for kt in range(nk):
                            v = (cvpad if which == "mem" else vpad)[:, kt, 2 * pr + hh, :]
                            ins = nc.tensor.matmul(o[:, 0:P], v, pT[:, hh, kt, :], start=(hh == 0 and kt == 0),
                                                   stop=(hh == 1 and kt == nk - 1))
                    end(ins)
                elif kind == "gate":
                    pr = arg[0]
                    o = begin(st)
                    pe.wait_ge(ld["wgk"], 16)
                    taken(pe, ("proj", "lr", 0))
                    end(nc.tensor.matmul(o, w_gk[0:RANK, pr * P:(pr + 1) * P], lrT[0:RANK, :], start=True, stop=True))
                elif kind == "turn_keys":
                    pr = arg[0]
                    o = begin(st)
                    pe.wait_ge(qk_ready, pr + 1)
                    for t in range(TT):
                        ins = nc.tensor.transpose(o[:, t * P:(t + 1) * P], kend_f[:, t * P:(t + 1) * P], C("ident"))
                    end(ins)
                elif kind == "intra":
                    pr, hh = arg
                    o = begin(st)
                    for t in range(TT):
                        ins = nc.tensor.matmul(o[:, t * P:(t + 1) * P], kinv[:, 2 * pr + hh, t * P:(t + 1) * P],
                                               qdec[:, pr, t * P:(t + 1) * P], start=True, stop=True)
                    end(ins)
                elif kind == "chunk_state":
                    pr, g = arg
                    o = begin(st)
                    taken(pe, ("turn_keys", pr))
                    taken(pe, ("proj", "gv", g))
                    for s_ in range(2):
                        ins = nc.tensor.matmul(o[:, s_ * 256:s_ * 256 + 256], kend[:, s_, g, :],
                                               gv[:, g, pr * 256:pr * 256 + 256], start=True, stop=True)
                    end(ins)
                elif kind == "gla_out":
                    pr, hh = arg
                    o = begin(st)
                    h = 2 * pr + hh
                    taken(pe, ("intra", pr, hh))
                    for t in range(TT):
                        ins = nc.tensor.matmul(o[:, t * P:(t + 1) * P], gv[:, t, h * P:(h + 1) * P], at_sb[:, hh, t, :],
                                               start=True, stop=False, skip_group_check=True)
                        for c in (2 * t, 2 * t + 1):
                            if c:
                                pe.wait_ge(st_done, 14 * pr + 2 * c)
                                ins = nc.tensor.matmul(o[:, c * CH:(c + 1) * CH], state[:, c, hh * P:(hh + 1) * P],
                                                       qdec[:, pr, c * CH:(c + 1) * CH], start=False, stop=True,
                                                       skip_group_check=True)
                    end(ins)
                elif kind == "gla_sum":
                    o = begin(st)
                    taken(pe, ("gla_out", *arg))
                    end(nc.tensor.matmul(o, C("ones"), osq, start=True, stop=True))
                elif kind == "router":
                    o = begin(st)
                    pe.wait_ge(ld["router"], 16)
                    for t in range(TT):
                        for k in range(KD):
                            pe.wait_ge(h_ready, 8 + k + 1)
                            ins = nc.tensor.matmul(o[:, t * 36:(t + 1) * 36], hT[:, k, t * P:(t + 1) * P], w_router[:, k, :],
                                                   start=(k == 0), stop=(k == KD - 1))
                    end(ins)
                elif kind == "turn_h":
                    t, half = arg
                    o = begin(st)
                    for j in range(4):
                        ins = nc.tensor.transpose(o[:, j * P:(j + 1) * P], hT[:, 4 * half + j, t * P:(t + 1) * P], C("ident"))
                    end(ins)
                elif kind == "rank":
                    o = begin(st)
                    pe.wait_ge(r_m, 1)
                    for t in range(TT):
                        for u in range(t + 1):
                            nc.tensor.matmul(o[:, t * 32:(t + 1) * 32], C("before") if u == t else C("ones"), M[:, u, :],
                                             start=(u == 0), stop=(u == t))
                    for u in range(TT):
                        ins = nc.tensor.matmul(o[:, P:P + 32], C("ones"), M[:, u, :], start=(u == 0), stop=(u == TT - 1))
                    end(ins)
                elif kind == "moe":
                    taken(pe, ("rank",))
                    for t in range(TT):
                        for half in range(2):
                            taken(pe, ("turn_h", t, half))
                    pe.wait_ge(std_done, 2)

                    def turn(b, s):
                        pe.sem_inc(passed["pe"], 1)
                        for k in range(KD):
                            ins = nc.tensor.transpose(ps_[:, 4 * b, k * CAP:(k + 1) * CAP], xg[b][0:CAP, k * P:(k + 1) * P],
                                                      C("ident")[0:CAP, 0:CAP])
                        ins.then_inc(s, 1)

                    def gate_up(b, s):
                        for j in range(2):
                            w = slot[2 * b + j][:, :].rearrange("p (k n) -> p k n", k=KD)
                            for f in range(4):
                                for k in range(KD):
                                    ins = nc.tensor.matmul(
                                        ps_[:, 4 * b + 1, j * 256 + f * CAP:j * 256 + (f + 1) * CAP],
                                        w[:, k, f * P:(f + 1) * P], xgT[b][:, k, :], start=(k == 0), stop=(k == KD - 1))
                        ins.then_inc(s, 1)

                    def down(b, s):
                        w = slot[4 + b][:, :].rearrange("p (k n) -> p k n", k=4)
                        for half in range(2):
                            for k in range(4):
                                ins = nc.tensor.matmul(ps_[0:CAP, 4 * b + 2 + half, :], hid[b][:, k, :],
                                                       w[:, k, half * 512:(half + 1) * 512], start=(k == 0), stop=(k == 3))
                        ins.then_inc(s, 1)

                    def pair(i):
                        for b in range(2):
                            pe.wait_ge(m_x[b], 16 * i + 16)
                            free(pe, m_xT[b], i)
                            turn(b, m_turned[b])
                        for b in range(2):
                            pe.wait_ge(m_xT[b], i + 1)
                            free(pe, m_hid[b], i)
                            pe.wait_ge(m_w[2 * b], 16 * i + 16)
                            pe.wait_ge(m_w[2 * b + 1], 16 * i + 16)
                            gate_up(b, m_gu[b])
                        for b in range(2):
                            pe.wait_ge(m_hid[b], i + 1)
                            free(pe, m_y[b], i)
                            pe.wait_ge(m_w[4 + b], 16 * i + 16)
                            down(b, m_down[b])

                    def over(i):
                        pe.wait_ge(o_x, 16 * i + 16)
                        turn(0, o_turned)
                        pe.wait_ge(o_xT, i + 1)
                        pe.wait_ge(o_w, 48 * i + 48)
                        gate_up(0, o_gu)
                        pe.wait_ge(o_hid, i + 1)
                        down(0, o_down)
                        pe.wait_ge(o_st, 16 * i + 16)

                    pairs(pe, pair)
                    for b in range(2):
                        pe.wait_ge(m_y[b], NE // 2)
                    pe.wait_ge(r_dest, 1)
                    n_over = nc.tensor.value_load(over_i[0:1, NOVER:NOVER + 1], min_val=0, max_val=NOVER)
                    overflow(pe, n_over, over)
                elif kind == "turn_y":
                    t, half = arg
                    o = begin(st)
                    pe.wait_ge(y_mixed, t + 1)
                    for j in range(4):
                        ins = nc.tensor.transpose(o[:, j * P:(j + 1) * P],
                                                  yg[2 * t][:, (4 * half + j) * P:(4 * half + j + 1) * P], C("ident"))
                    end(ins)
                    if t == TT - 1 and half == 1:
                        for n in range(KD):
                            norm_sum(2, n)
                elif kind == "lru_gate":
                    which, n = arg
                    o = begin(st)
                    pe.wait_ge(conv_done, n + 1)
                    j = int(which == "i")
                    pe.wait_ge(ld_bd[j], 16 * (n + 1))
                    end(nc.tensor.matmul(o, w_bd[:, j, :], lc[:, n % 2, :], start=True, stop=True))
                elif kind == "stick":
                    for name in jobs[J[("proj", "v2", 7)] - 6:J[("proj", "v2", 7)] + 1]:
                        taken(pe, name)
                    pe.wait_ge(std_done, 3)

                    def scores(h):
                        pr, lo = h // 2, CH * (h % 2)
                        b0 = 3 * (h % 2)
                        if h >= 2:
                            pe.wait_ge(att_done, h - 1)
                        for kt, (c, w_) in enumerate(SEG):
                            o = ps_[:, b0 + c // 512, c % 512:c % 512 + w_]
                            nc.tensor.matmul(o, k2[lo:lo + CH, pr, kt * P:(kt + 1) * P], q2[lo:lo + CH, pr, kt * P:S],
                                             start=(kt != 3), stop=False, skip_group_check=True)
                            ins = nc.tensor.matmul(ps_[:, b0 + c // 512, c % 512:c % 512 + P], C("ident"), C("stickbias"),
                                                   start=False, stop=False, skip_group_check=True)
                        ins.then_inc(z_done, 1)

                    def suffix(h):
                        b0 = 3 * (h % 2)
                        pe.wait_ge(sp_done, h + 1)
                        for jt, (c, w_) in enumerate(SEG):
                            for kt in range(jt, TT):
                                ck_, wk = SEG[kt]
                                o = c + (kt - jt) * P
                                ins = nc.tensor.matmul(ps_[:, b0 + o // 512, o % 512:o % 512 + wk],
                                                       C("negtri") if kt == jt else C("negones"), Lb[h % 2][:, ck_:ck_ + wk],
                                                       start=False, stop=False, skip_group_check=True)
                        ins.then_inc(tri_done, 1)

                    def head_values(h):
                        pr = h // 2
                        pe.wait_ge(att_done, h + 1)
                        if h >= 2:
                            pe.wait_ge(pv_out, h - 1)
                        for kt, (c, w_) in enumerate(SEG):
                            ins = nc.tensor.matmul(ps_[:, 6 + h % 2, kt * P:S], v2[:, kt, pr * P:(pr + 1) * P],
                                                   att[h % 2][:, c:c + w_], start=(kt == 0), stop=(kt == TT - 1),
                                                   skip_group_check=True)
                        ins.then_inc(pv_done, 1)

                    scores(0)
                    scores(1)
                    for h in range(HB + 1):
                        if h < HB:
                            suffix(h)
                        if h >= 1:
                            head_values(h - 1)
                        if h + 2 < HB:
                            scores(h + 2)
                    pe.wait_ge(att_done, HB)
                    pe.wait_ge(pv_out, HB)
                elif kind == "down":
                    half = arg[0]
                    names = [("proj", "down", n) for n in range(4 * half, 4 * half + 4)]
                    outs = [begin(nm) for nm in names]
                    for kp in range(4):
                        w = panel(f"down{4 * half + kp}")
                        pe.wait_ge(hid_done, 8 * kp + 8)
                        for j in range(4):
                            for k in range(KD):
                                ins = nc.tensor.matmul(outs[j], w[:, k, j * P:(j + 1) * P], hidden[:, kp * KD + k, :],
                                                       start=(kp == 0 and k == 0), stop=(kp == 3 and k == KD - 1),
                                                       skip_group_check=True)
                            if kp == 3:
                                end(ins)
                            elif j == 3:
                                ins.then_inc(down_read, 1)


        @block.scalar
        def _(act):
            chain = [0]

            def link(ins):
                chain[0] += 1
                ins.then_inc(act_chain, 1)
                act.wait_ge(act_chain, chain[0])

            one, eps = C("one"), C("eps")

            def fn(dst, src, f, **kw):
                return nc.scalar.activation(dst, src, f, **kw)

            act.wait_ge(ld["cst"], 16)
            act.wait_ge(ld["prm"], 16)
            for st in steps:
                kind, arg = st[0], st[1:]
                if kind == "mem_norm":
                    act.wait_ge(mem_sum, 1)
                    fn(std[:, 0:NM], ps_[:, 7, 0:NM], ACT.Sqrt, scale=1.0 / D, bias=eps).then_inc(mem_std, 1)
                    link(fn(lw[0], prm[:, GAINS["lru_lambda_2"][0]:GAINS["lru_lambda_2"][1]], ACT.Abs))
                    fn(lw[1], lw[0], ACT.Exp, scale=-1.0).then_inc(lam_exp, 1)
                    act.wait_ge(ld["x"], 16)
                    for n in range(KD):
                        fn(hT[:, n, :], xT[:, n, :], ACT.Square).then_inc(squared, 1)
                elif kind in ("square", "norm"):
                    norm = arg[0]
                    if kind == "square" or norm == 2:
                        for n in ([arg[1]] if kind == "square" else range(KD)):
                            if norm == 2 and n == 0:
                                for t in range(TT):
                                    for half in range(2):
                                        taken(act, ("turn_y", t, half))
                            elif norm == 1:
                                taken(act, ("proj", "out", n))
                            elif norm == 3:
                                taken(act, ("proj", "out2", n))
                            elif norm == 4:
                                taken(act, ("proj", "down", n))
                            elif norm == 5:
                                act.wait_ge(x_new, n + 1)
                            if n < 2:
                                act.wait_ge(h_ready, 8 * norm)
                            else:
                                act.wait_ge(summed, 8 * norm + n - 1)
                            fn(sqb[:, n % 2, :], xT[:, n, :], ACT.Square).then_inc(squared, 1)
                    if kind == "norm":
                        act.wait_ge(summed, 8 * norm + 8)
                        if norm == 0:
                            act.wait_ge(mem_h, 8)
                        fn(std, ps_[:, 7, :], ACT.Sqrt, scale=1.0 / D, bias=eps).then_inc(std_done, 1)
                elif kind == "proj":
                    name, n = arg
                    job = st
                    o = None if name in ("out", "bl", "ba", "out2", "down", "ple") else bank(job)
                    if o is not None:
                        finished(act, job)
                    if name in ("ck", "cq", "mq", "mk"):
                        i = hn_index[arg]
                        w_ = NM if name == "ck" else S
                        if i == 0:
                            act.wait_ge(mem_h, 8)
                        if i >= 2:
                            act.wait_ge(hn_done, i - 1)
                        fn(hn_raw[:, i % 2, 0:w_], o[:, 0:w_], ACT.Copy)
                        link(fn(hn_sq[:, i % 2, 0:w_], o[:, 0:w_], ACT.Square))
                        act.sem_inc(hn_in, 1)
                        act.sem_inc(bank_free[J[job] % JB], 1)
                    elif name in ("cv", "mv"):
                        dst = (cvpad if name == "cv" else vpad)[:, n, :, :]
                        act.wait_ge(zeroed, 3)
                        src = o[:, 0:256].rearrange("p (a b d) -> p a b d", a=2, b=2)
                        d4 = dst.rearrange("p (a b) d -> p a b d", a=2)
                        fn(d4[:, :, 0, 0:CH], src[:, :, 0, :], ACT.Copy)
                        frees(fn(d4[:, :, 1, CH:P], src[:, :, 1, :], ACT.Copy), job)
                    elif name in ("gq", "gk"):
                        frees(fn((gq if name == "gq" else gk)[:, n, :], o, ACT.Copy), job)
                    elif name == "lr":
                        frees(fn(lrT[0:RANK, :], o[0:RANK, :], ACT.Copy), job)
                    elif name == "gv":
                        frees(fn(gv[:, n, :], o, ACT.Copy), job)
                    elif name == "r":
                        act.wait_ge(zeros_stored, 32)
                        frees(fn(rs[:, n, :], o, ACT.Silu), job)
                    elif name == "ux":
                        if n == 0:
                            act.wait_ge(pad_zero, 1)
                        if n >= 2:
                            act.wait_ge(conv_done, n - 1)
                        frees(fn(uxp[:, n % 2, 3:3 + S], o, ACT.Copy), job)
                    elif name == "ug":
                        if n >= 2:
                            act.wait_ge(yl_done, n - 1)
                        elif n == 0:
                            act.wait_ge(lru_done, KD)
                        frees(fn(lt[:, n % 2, :], o, ACT.Gelu_apprx_tanh), job)
                    elif name == "q2":
                        frees(fn(q2[:, n, :], o, ACT.Copy, scale=0.125), job)
                    elif name == "k2":
                        frees(fn(k2[:, n, :], o, ACT.Copy), job)
                    elif name == "v2":
                        half, t = n // TT, n % TT
                        if n == 0:
                            act.wait_ge(lru_done, KD)
                        frees(fn(v2[:, t, half * 512:half * 512 + 512], o, ACT.Copy), job)
                    elif name in ("gl", "ga"):
                        if name == "gl" and n == 0:
                            act.wait_ge(pv_done, HB)
                        j = (0 if name == "gl" else 8) + n
                        if j >= 4:
                            pj = j - 4
                            taken(act, ("proj", "bl" if pj < 8 else "ba", pj % 8))
                        frees(fn(sgate[n % 4], o, ACT.Sigmoid), job)
                    elif name == "up":
                        if n == 0:
                            finished(act, ("proj", "out2", 7))
                        frees(fn(hidden[:, n, :], o, ACT.Relu), job)
                    elif name == "pg":
                        if n == 0:
                            finished(act, ("proj", "down", 7))
                        frees(fn(pgs[:, n, :], o, ACT.Sigmoid), job)
                elif kind == "headsum":
                    i = hn_index[arg]
                    w_ = NM if arg[0] == "ck" else S
                    finished(act, st)
                    frees(fn(hn_sq[:, i % 2, 0:w_], bank(st)[:, 0:w_], ACT.Sqrt, scale=1.0 / CH, bias=eps), st)
                elif kind == "softmax":
                    u = unit_index[arg]
                    which, pr, qt, hh = arg
                    act.wait_ge(neg_ready, u + 1)
                    if u >= 2:
                        finished(act, ("turn", *prev_unit(u - 2)))
                    if which == "mem":
                        ins = fn(p_sb[:, u % 2, 0:NM], bank(("score", *arg))[:, 0:NM], ACT.Exp, scale=0.125,
                                 bias=row_neg[:, u % 2:u % 2 + 1], accum_out=row_sum[:, u % 2:u % 2 + 1])
                    else:
                        w_ = P * (qt + 1)
                        ins = fn(p_sb[:, u % 2, 0:w_], s_sb[:, u % 2, 0:w_], ACT.Exp,
                                 bias=row_neg[:, u % 2:u % 2 + 1], accum_out=row_sum[:, u % 2:u % 2 + 1])
                    ins.then_inc(exp_done, 1)
                elif kind == "turn":
                    which, pr, qt, hh = arg
                    finished(act, st)
                    nk = MT if which == "mem" else qt + 1
                    first = unit_index[arg]
                    if first >= 2:
                        pu = prev_unit(2 * (first // 2) - 2)
                        finished(act, ("values", *pu[:3]))
                    frees(fn(pT[:, hh, 0:nk, :], bank(st)[:, 0:nk * P].rearrange("p (k q) -> p k q", q=P), ACT.Copy), st)
                elif kind == "values":
                    which, pr, qt = arg
                    finished(act, st)
                    tile = (6 if which == "mem" else 4) + pr
                    frees(fn(mixT[:, tile, qt * P:(qt + 1) * P], bank(st)[:, 0:P], ACT.Copy), st)
                elif kind == "gate":
                    pr = arg[0]
                    finished(act, st)
                    frees(fn(zb[:, pr, :], bank(st), ACT.Identity, bias=G("b_gla_gk", pr)), st)
                elif kind == "gla_begin":
                    finished(act, ("values", "moba", 1, TT - 1))
                    act.wait_ge(exp_done, 32)
                elif kind == "decay":
                    pr = arg[0]
                    if pr:
                        act.wait_ge(qk_ready, pr)
                    taken(act, ("gate", pr))
                    link(fn(t1, zb[:, pr, :], ACT.Abs))
                    link(fn(t1, t1, ACT.Exp, scale=-1.0))
                    fn(t1, t1, ACT.Ln, bias=one).then_inc(lsig, 1)
                    act.wait_ge(cum_done, 2 * pr + 2)
                    i16 = 1.0 / 16.0
                    fn(ecum, cum, ACT.Exp, scale=i16)
                    fn(einv, cum, ACT.Exp, scale=-i16)
                    fn(eend, t1, ACT.Exp, scale=i16)
                    fn(dec[pr], cum.rearrange("p (c l) -> p c l", l=CH)[:, :, CH - 1], ACT.Exp, scale=i16).then_inc(dec_exp, 1)
                elif kind == "gla_out":
                    h = 2 * arg[0] + arg[1]
                    finished(act, st)
                    if h:
                        act.wait_ge(o_done, h)
                        finished(act, ("gla_sum", (h - 1) // 2, (h - 1) % 2))
                    fn(ogn, bank(st), ACT.Copy)
                    frees(fn(osq, bank(st), ACT.Square), st)
                elif kind == "gla_sum":
                    finished(act, st)
                    frees(fn(ostd, bank(st), ACT.Sqrt, scale=1.0 / P, bias=eps), st)
                elif kind == "turn_h":
                    t, half = arg
                    finished(act, st)
                    frees(fn(htok[:, t, half * 512:half * 512 + 512], bank(st), ACT.Copy), st)
                    if half == 1:
                        taken(act, st)
                        act.dma_start(h_dram[t * P:(t + 1) * P, :], htok[:, t, :]).then_inc(h_stored, 16)
                elif kind == "route":
                    act.wait_ge(r_gd, 1)
                    fn(w4b, w4, ACT.Exp).then_inc(r_exp, 1)
                    act.wait_ge(r_e2in, 1)
                    fn(col[5], col[4], ACT.Exp).then_inc(r_e2, 1)
                elif kind == "moe":
                    def silu(b, s_gu, s_silu, i):
                        act.wait_ge(s_gu, i + 1)
                        fn(sg[b], ps_[:, 4 * b + 1, 0:256].rearrange("p (f c) -> p f c", c=CAP), ACT.Silu).then_inc(s_silu, 1)

                    def rows_out(b, first, s_down, s_y, s_st, i):
                        act.wait_ge(s_down, i + 1)
                        free(act, s_st, 16 * i)
                        fn(yout[b][0:CAP, :], ps_[0:CAP, 4 * b + 2:4 * b + 4, :].rearrange("p a n -> p (a n)"),
                           ACT.Copy).then_inc(s_y, 1)
                        act.wait_ge(s_y, i + 1)
                        act.dma_start(y_dram[bass.ds(first, CAP), :], yout[b][0:CAP, :]).then_inc(s_st, 16)

                    def pair(i):
                        for b in range(2):
                            free(act, m_hid[b], i)
                            silu(b, m_gu[b], m_silu[b], i)
                        for b in range(2):
                            rows_out(b, (2 * i + b) * CAP, m_down[b], m_y[b], m_st[b], i)

                    def over(i):
                        silu(0, o_gu, o_silu, i)
                        rows_out(0, (NE + i) * CAP, o_down, o_y, o_st, i)

                    pairs(act, pair)
                    for b in range(2):
                        act.wait_ge(m_st[b], 16 * (NE // 2))
                    act.wait_ge(r_dest, 1)
                    n_over = nc.scalar.value_load(over_i[0:1, NOVER:NOVER + 1], min_val=0, max_val=NOVER)
                    overflow(act, n_over, over)
                elif kind == "lru_gate":
                    which, n = arg
                    if n >= 2:
                        act.wait_ge(lru_done, n - n % 2)
                    finished(act, st)
                    dst, b_ = (lr_, "b_rgate_2") if which == "r" else (li, "b_igate_2")
                    frees(fn(dst[:, n % 2, :], bank(st), ACT.Sigmoid, bias=G(b_, n)), st)
                elif kind == "lru":
                    g = arg[0]
                    if g == 0:
                        act.wait_ge(lam_done, 1)
                    taken(act, ("lru_gate", "r", 2 * g))
                    taken(act, ("lru_gate", "r", 2 * g + 1))
                    for m in (2 * g, 2 * g + 1):
                        fn(la[:, m % 2, :], lr_[:, m % 2, :], ACT.Exp, scale=nsp8[:, m:m + 1])
                        ins = fn(lt[:, m % 2, :], lr_[:, m % 2, :], ACT.Tanh, scale=sp8[:, m:m + 1])
                    ins.then_inc(lru_exp, 1)
                    act.wait_ge(lru_m2, g + 1)
                    fn(lt, lt, ACT.Sqrt).then_inc(lru_mult, 1)
                elif kind == "stick":
                    act.wait_ge(yl_done, KD)

                    def softplus(h):
                        act.wait_ge(z_done, h + 1)
                        if h >= 2:
                            act.wait_ge(tri_done, h - 1)
                        link(fn(Lb[h % 2], flat(h), ACT.Abs))
                        link(fn(Lb[h % 2], Lb[h % 2], ACT.Exp, scale=-1.0))
                        fn(Lb[h % 2], Lb[h % 2], ACT.Ln, bias=one).then_inc(sp_log, 1)

                    def weights(h):
                        act.wait_ge(tri_done, h + 1)
                        if h >= 2:
                            act.wait_ge(pv_done, h - 1)
                        else:
                            act.wait_ge(h_ready, 8 * 3)
                            finished(act, ("lru_gate", "i", KD - 1))
                        fn(att[h % 2], flat(h), ACT.Exp).then_inc(att_done, 1)

                    softplus(0)
                    softplus(1)
                    for h in range(HB):
                        weights(h)
                        if h + 2 < HB:
                            softplus(h + 2)

        @block.vector
        def _(dve):
            chain = [0]

            def link(ins):
                chain[0] += 1
                ins.then_inc(dve_chain, 1)
                dve.wait_ge(dve_chain, chain[0])

            v = nc.vector
            dve.wait_ge(ld["cst"], 16)
            dve.wait_ge(ld["prm"], 16)
            lam = prm[:, GAINS["lru_lambda_2"][0]:GAINS["lru_lambda_2"][1]]
            dve.wait_ge(ld["mem"], 16)
            v.tensor_tensor(memh, memT, memT, ALU.mult).then_inc(mem_sq, 1)
            dve.wait_ge(lam_exp, 1)
            link(v.tensor_scalar(lw[2], lw[1], 2.0, None, ALU.add))
            link(v.reciprocal(lw[2], lw[2]))
            link(v.tensor_tensor(lw[3], lw[1], lw[2], ALU.mult))
            link(v.tensor_tensor(lw[4], lw[3], lw[3], ALU.mult))
            link(v.tensor_scalar(lw[5], lw[4], 1.0 / 17, 1.0 / 15, ALU.mult, ALU.add))
            for d in (13, 11, 9, 7, 5, 3, 1):
                link(v.tensor_tensor(lw[5], lw[5], lw[4], ALU.mult))
                link(v.tensor_scalar(lw[5], lw[5], 1.0 / d, None, ALU.add))
            link(v.scalar_tensor_tensor(out=lw[5], in0=lw[5], scalar=2.0, in1=lw[3], op0=ALU.mult, op1=ALU.mult))
            link(v.tensor_scalar(lw[0], lam, -1.0, 0.0, ALU.mult, ALU.max))
            link(v.tensor_tensor(lw[5], lw[5], lw[0], ALU.add))
            v.tensor_scalar(nsp8, lw[5], -8.0, None, ALU.mult)
            v.tensor_scalar(sp8, lw[5], 8.0, None, ALU.mult).then_inc(lam_done, 1)

            def add_x(n, job):
                finished(dve, job)
                frees(v.tensor_tensor(xT[:, n, :], bank(job), xT[:, n, :], ALU.add), job)

            def pick_first(dst, cond, first, tmp, mx):
                link(v.tensor_tensor(tmp, cond, first, ALU.mult))
                link(v.tensor_reduce(mx, tmp, AX, ALU.max))
                link(v.tensor_tensor(dst, tmp, mx.unsqueeze(2).to_broadcast(list(tmp.shape)), ALU.is_equal))

            def rows(x):
                return x.unsqueeze(1).to_broadcast([P, TT, x.shape[1]])

            def each(x, n):
                return x.unsqueeze(2).to_broadcast([P, x.shape[1], n])

            for st in steps:
                kind, arg = st[0], st[1:]
                if kind == "mem_norm":
                    dve.wait_ge(mem_std, 1)
                    link(v.reciprocal(std[:, 0:NM], std[:, 0:NM]))
                    for k in range(KD):
                        v.scalar_tensor_tensor(out=memh[:, k, :], in0=memT[:, k, :], scalar=G("mem_norm_g", k),
                                               in1=std[:, 0:NM], op0=ALU.mult, op1=ALU.mult).then_inc(mem_h, 1)
                elif kind == "norm":
                    norm = arg[0]
                    gain = ["attn_norm_g", "ffn_norm_g", "norm_mix_g_2", "norm_mlp_g_2", "norm_ple_g_2",
                            "norm_final_g_2"][norm]
                    old = {1: ("proj", "r", 3), 2: ("turn_h", TT - 1, 1), 3: ("proj", "ga", 7), 4: ("proj", "up", 31),
                           5: ("proj", "pg", 7)}
                    if norm in old:
                        finished(dve, old[norm])
                    dve.wait_ge(std_done, norm + 1)
                    link(v.reciprocal(std, std))
                    for k in range(KD):
                        v.scalar_tensor_tensor(out=hT[:, k, :], in0=xT[:, k, :], scalar=G(gain, k), in1=std,
                                               op0=ALU.mult, op1=ALU.mult).then_inc(h_ready, 1)
                    if norm == 2:
                        v.memset(uxp[:, :, 0:3], 0.0).then_inc(pad_zero, 1)
                elif kind == "proj":
                    name, n = arg
                    if name in ("out", "out2"):
                        add_x(n, st)
                    elif name == "ug":
                        taken(dve, st)
                        v.tensor_tensor(yl[:, n, :], yl[:, n, :], lt[:, n % 2, :], ALU.mult).then_inc(yl_done, 1)
                    elif name in ("bl", "ba"):
                        taken(dve, ("proj", "gl" if name == "bl" else "ga", n))
                        finished(dve, st)
                        if name == "bl":
                            frees(v.tensor_tensor(merged[:, n, :], bank(st), sgate[n % 4], ALU.mult), st)
                        else:
                            frees(v.tensor_tensor(prod, bank(st), sgate[n % 4], ALU.mult), st)
                            taken(dve, st)
                            v.tensor_tensor(merged[:, n, :], merged[:, n, :], prod, ALU.add).then_inc(merge_done, 1)
                            dve.wait_ge(merge_done, n + 1)
                    elif name == "up":
                        taken(dve, st)
                        v.tensor_tensor(hidden[:, n, :], hidden[:, n, :], hidden[:, n, :], ALU.mult).then_inc(hid_done, 1)
                    elif name == "ple":
                        taken(dve, ("proj", "pg", n))
                        finished(dve, st)
                        frees(v.tensor_tensor(prod, bank(st), pgs[:, n, :], ALU.mult), st)
                        taken(dve, st)
                        v.tensor_tensor(xT[:, n, :], xT[:, n, :], prod, ALU.add).then_inc(x_new, 1)
                        dve.wait_ge(x_new, n + 1)
                elif kind == "downed":
                    add_x(arg[0], ("proj", "down", arg[0]))
                elif kind == "headsum":
                    name, n = arg
                    i = hn_index[arg]
                    w_ = NM if name == "ck" else S
                    taken(dve, st)
                    dve.wait_ge(hn_in, i + 1)
                    dve.wait_ge(zeroed, 3)
                    inv = hn_sq[:, i % 2, 0:w_]
                    link(v.reciprocal(inv, inv))
                    gain = G({"mq": "moba_q_norm_g", "mk": "moba_k_norm_g", "cq": "mem_q_norm_g", "ck": "mem_k_norm_g"}[name])
                    parts = [(0, P, {"mk": kn, "ck": ckn}[name][:, n, :])] if name in ("mk", "ck") else [
                        (lo, lo + CH, {"mq": qpad, "cq": cqpad}[name][lo:lo + CH, 2 * n + lo // CH, :]) for lo in (0, CH)]
                    for lo, hi, dst in parts:
                        ins = v.scalar_tensor_tensor(out=dst, in0=hn_raw[lo:hi, i % 2, 0:w_], scalar=gain[lo:hi, :],
                                                     in1=hn_sq[lo:hi, i % 2, 0:w_], op0=ALU.mult, op1=ALU.mult)
                    ins.then_inc(hn_done, 1)
                elif kind == "softmax":
                    u = unit_index[arg]
                    which, pr, qt, hh = arg
                    j = u % 2
                    h = 2 * pr + hh
                    finished(dve, ("score", *arg))
                    if u >= 2:
                        dve.wait_ge(exp_done, u - 1)
                    o = bank(("score", *arg))
                    if which == "mem":
                        w_ = NM
                        link(v.tensor_reduce(row_max[:, j:j + 1], o[:, 0:w_], AX, ALU.max))
                        v.tensor_scalar(row_neg[:, j:j + 1], row_max[:, j:j + 1], -0.125, None, ALU.mult).then_inc(neg_ready, 1)
                    else:
                        w_ = P * (qt + 1)
                        link(v.tensor_scalar(slope_b[:, 0:w_], C("alibi")[:, S - w_:S], 2.0 ** (-2 * (h + 1)), None, ALU.mult))
                        link(v.scalar_tensor_tensor(out=s_sb[:, j, 0:w_], in0=o[:, 0:w_], scalar=0.125,
                                                    in1=slope_b[:, 0:w_], op0=ALU.mult, op1=ALU.add))
                        link(v.tensor_reduce(row_max[:, j:j + 1], s_sb[:, j, 0:w_], AX, ALU.max))
                        v.tensor_scalar(row_neg[:, j:j + 1], row_max[:, j:j + 1], -1.0, None, ALU.mult).then_inc(neg_ready, 1)
                    dve.wait_ge(exp_done, u + 1)
                    dve.sem_inc(bank_free[J[("score", *arg)] % JB], 1)
                    link(v.reciprocal(row_inv[:, j:j + 1], row_sum[:, j:j + 1]))
                    v.tensor_scalar(p_sb[:, j, 0:w_], p_sb[:, j, 0:w_], row_inv[:, j:j + 1], None, ALU.mult).then_inc(p_ready, 1)
                elif kind == "gla_begin":
                    finished(dve, ("values", "moba", 1, TT - 1))
                    dve.wait_ge(state_zero, 1)
                elif kind == "decay":
                    pr = arg[0]
                    for nm in ("gq", "gk"):
                        taken(dve, ("proj", nm, pr))
                    dve.wait_ge(lsig, pr + 1)
                    if pr:
                        dve.wait_ge(dec_exp, pr)
                    link(v.scalar_tensor_tensor(out=t1, in0=zb[:, pr, :], scalar=0.0, in1=t1, op0=ALU.min, op1=ALU.subtract))
                    v.tensor_tensor_scan(cum, C("reset"), t1, 0.0, ALU.mult, ALU.add).then_inc(cum_done, 1)
                    dve.wait_ge(cum_done, 2 * pr + 1)
                    c3 = cum.rearrange("p (c l) -> p c l", l=CH)
                    v.tensor_tensor(t1.rearrange("p (c l) -> p c l", l=CH), c3[:, :, CH - 1:CH].to_broadcast([P, 8, CH]), c3,
                                    ALU.subtract).then_inc(cum_done, 1)
                    dve.wait_ge(dec_exp, pr + 1)
                    if pr:
                        finished(dve, ("turn_keys", pr - 1))
                    v.scalar_tensor_tensor(out=qdec[:, pr, :], in0=gq[:, pr, :], scalar=0.125, in1=ecum, op0=ALU.mult, op1=ALU.mult)
                    for lo in (0, CH):
                        v.tensor_tensor(kinv[lo:lo + CH, 2 * pr + lo // CH, :], gk[lo:lo + CH, pr, :], einv[lo:lo + CH, :], ALU.mult)
                    v.tensor_tensor(kend_f, gk[:, pr, :], eend, ALU.mult).then_inc(qk_ready, 1)
                elif kind == "turn_keys":
                    pr = arg[0]
                    finished(dve, st)
                    if pr:
                        finished(dve, ("chunk_state", pr - 1, 3))
                    for s_ in range(2):
                        ins = v.tensor_scalar(kend[:, s_, :, :], bank(st).rearrange("p (t f) -> p t f", t=TT),
                                              C("half")[:, s_:s_ + 1], None, ALU.mult)
                    frees(ins, st)
                elif kind == "intra":
                    pr, hh = arg
                    finished(dve, st)
                    if pr:
                        finished(dve, ("gla_out", pr - 1, hh))
                    frees(v.tensor_tensor(at_sb[:, hh, :, :], bank(st).rearrange("p (t f) -> p t f", t=TT),
                                          C("chunkmask").unsqueeze(1).to_broadcast([P, TT, P]), ALU.mult), st)
                elif kind == "chunk_state":
                    pr, g = arg
                    finished(dve, st)
                    if pr and g == 0:
                        finished(dve, ("gla_out", pr - 1, 1))
                    for s_ in range(2):
                        c = 2 * g + s_
                        if c == 7:
                            break
                        if c:
                            dve.wait_ge(st_done, 14 * pr + 2 * c)
                        for lo in (0, CH):
                            cs = slice(lo // CH * P, lo // CH * P + P)
                            d_ = state[lo:lo + CH, c + 1, cs]
                            u_ = bank(st)[lo:lo + CH, s_ * 256 + cs.start:s_ * 256 + cs.stop]
                            if c == 0:
                                v.tensor_copy(d_, u_).then_inc(st_done, 1)
                            else:
                                v.scalar_tensor_tensor(out=d_, in0=state[lo:lo + CH, c, cs], scalar=dec[pr][lo:lo + CH, c:c + 1],
                                                       in1=u_, op0=ALU.mult, op1=ALU.add).then_inc(st_done, 1)
                    dve.wait_ge(st_done, 14 * pr + 2 * min(2 * g + 2, 7))
                    dve.sem_inc(bank_free[J[st] % JB], 1)
                elif kind == "gla_sum":
                    h = 2 * arg[0] + arg[1]
                    taken(dve, st)
                    link(v.reciprocal(ostd, ostd))
                    link(v.scalar_tensor_tensor(out=ogn, in0=ogn, scalar=G("gla_out_norm_g"), in1=ostd, op0=ALU.mult, op1=ALU.mult))
                    taken(dve, ("proj", "r", h))
                    v.tensor_tensor(mixT[:, h, :], ogn, rs[:, h, :], ALU.mult).then_inc(o_done, 1)
                    dve.wait_ge(o_done, h + 1)
                elif kind == "router":
                    finished(dve, st)
                    lo, hi = GAINS["router_bias"]
                    frees(v.tensor_tensor(lg, bank(st)[:, 0:TT * 36].rearrange("p (t n) -> p t n", t=TT),
                                          rows(prm[:, lo:hi]), ALU.add), st)
                    taken(dve, st)
                elif kind == "route":
                    link(v.tensor_reduce(col[0], lg[:, :, 0:4], AX, ALU.max))
                    v.tensor_tensor(w4, lg[:, :, 0:4], each(col[0], 4), ALU.subtract).then_inc(r_gd, 1)
                    dve.wait_ge(r_exp, 1)
                    link(v.tensor_reduce(col[1], w4b, AX, ALU.add))
                    link(v.reciprocal(col[1], col[1]))
                    link(v.tensor_scalar(w4, w4, 0.0, None, ALU.is_ge))
                    pick_first(w4b, w4, rows(C("first4")), w4, col[2])
                    link(v.tensor_scalar(w4b, w4b, -1.0, BIG, ALU.add, ALU.mult))
                    link(v.tensor_tensor(wk32.rearrange("p t (g e) -> p t g e", g=4),
                                         lg[:, :, 4:36].rearrange("p t (g e) -> p t g e", g=4),
                                         w4b.unsqueeze(3).to_broadcast([P, TT, 4, 8]), ALU.add))
                    for k in range(2):
                        link(v.tensor_reduce(col[2 + k], wk32, AX, ALU.max))
                        link(v.tensor_tensor(wk32b, wk32, each(col[2 + k], 32), ALU.is_ge))
                        pick_first(oh[k], wk32b, rows(C("first32")), wk32b, col[6])
                        if k == 0:
                            link(v.scalar_tensor_tensor(out=wk32, in0=oh[0], scalar=-100.0 * BIG, in1=wk32, op0=ALU.mult, op1=ALU.add))
                    v.tensor_tensor(M, oh[0], oh[1], ALU.add).then_inc(r_m, 1)
                    v.tensor_tensor(col[4], col[3], col[2], ALU.subtract).then_inc(r_e2in, 1)
                    dve.wait_ge(r_e2, 1)
                    link(v.tensor_scalar(col[7], col[5], 1.0, None, ALU.add))
                    link(v.reciprocal(col[7], col[7]))
                    link(v.tensor_tensor(gate_w[:, 0, :], col[7], col[1], ALU.mult))
                    link(v.tensor_tensor(gate_w[:, 1, :], gate_w[:, 0, :], col[5], ALU.mult))
                elif kind == "place":
                    rk = ("rank",)
                    finished(dve, rk)
                    o = bank(rk)
                    link(v.tensor_copy(cnt, o[:, P:P + 32]))
                    link(v.tensor_tensor(cmp, cnt.unsqueeze(2).to_broadcast([P, 32, 7]),
                                         C("thresholds").unsqueeze(1).to_broadcast([P, 32, 7]), ALU.is_gt))
                    link(v.tensor_reduce(nb, cmp, AX, ALU.add))
                    link(v.tensor_tensor_scan(obend, C("ones")[:, 0:32], nb, 0.0, ALU.mult, ALU.add))
                    link(v.tensor_tensor(dd, obend, nb, ALU.subtract))
                    link(v.tensor_tensor(dd, dd, C("expert"), ALU.subtract))
                    link(v.tensor_scalar(dd, dd, float(CAP), float((NE - 1) * CAP), ALU.mult, ALU.add))
                    rank = o[:, 0:P].rearrange("p (t e) -> p t e", t=TT)
                    link(v.tensor_scalar(wk32, rank, float(CAP), None, ALU.is_ge))
                    link(v.tensor_tensor(wk32, wk32, rows(dd), ALU.mult))
                    link(v.tensor_tensor(wk32, wk32, rank, ALU.add))
                    link(v.tensor_scalar(dd, C("expert"), float(CAP), None, ALU.mult))
                    link(v.tensor_tensor(dest, wk32, rows(dd), ALU.add))
                    for k in range(2):
                        link(v.tensor_tensor(wk32, dest, oh[k], ALU.mult))
                        link(v.tensor_reduce(col[8 + k], wk32, AX, ALU.add))
                        link(v.tensor_copy(dest_i[:, k * TT:(k + 1) * TT], col[8 + k]))
                    link(v.tensor_tensor(cmp2, obend.unsqueeze(1).to_broadcast([P, NOVER, 32]),
                                         C("overblock").unsqueeze(2).to_broadcast([P, NOVER, 32]), ALU.is_le))
                    link(v.tensor_reduce(otab, cmp2, AX, ALU.add))
                    link(v.tensor_scalar(otab, otab, float(NE - 1), None, ALU.min))
                    link(v.tensor_copy(over_i[:, 0:NOVER], otab))
                    link(v.tensor_copy(over_i[:, NOVER:NOVER + 1], obend[:, 31:32]))
                    dve.sem_inc(r_dest, 1)
                    dve.sem_inc(bank_free[J[rk] % JB], 1)
                elif kind == "moe":
                    def rows_in(b, s_turned, s_xT, i):
                        dve.wait_ge(s_turned, i + 1)
                        v.tensor_copy(xgT[b], ps_[:, 4 * b, :].rearrange("p (k c) -> p k c", k=KD)).then_inc(s_xT, 1)

                    def gated(b, s_silu, s_hid, i):
                        dve.wait_ge(s_silu, i + 1)
                        v.tensor_tensor(hid[b], ps_[:, 4 * b + 1, 256:512].rearrange("p (f c) -> p f c", c=CAP), sg[b],
                                        ALU.mult).then_inc(s_hid, 1)

                    def pair(i):
                        for b in range(2):
                            free(dve, m_gu[b], i)
                            rows_in(b, m_turned[b], m_xT[b], i)
                        for b in range(2):
                            free(dve, m_down[b], i)
                            gated(b, m_silu[b], m_hid[b], i)

                    def over(i):
                        free(dve, o_st, 16 * i)
                        rows_in(0, o_turned, o_xT, i)
                        gated(0, o_silu, o_hid, i)

                    pairs(dve, pair)
                    for b in range(2):
                        dve.wait_ge(m_st[b], 16 * (NE // 2))
                    n_over = nc.vector.value_load(over_i[0:1, NOVER:NOVER + 1], min_val=0, max_val=NOVER)
                    overflow(dve, n_over, over)
                    for t in range(TT):
                        dve.wait_ge(y_got[t], 32)
                        link(v.tensor_scalar(yg[2 * t], yg[2 * t], gate_w[:, 0, t:t + 1], None, ALU.mult))
                        v.scalar_tensor_tensor(out=yg[2 * t], in0=yg[2 * t + 1], scalar=gate_w[:, 1, t:t + 1], in1=yg[2 * t],
                                               op0=ALU.mult, op1=ALU.add).then_inc(y_mixed, 1)
                elif kind == "turn_y":
                    t, half = arg
                    finished(dve, st)
                    xs = xT[:, 4 * half:4 * half + 4, t * P:(t + 1) * P]
                    frees(v.tensor_tensor(xs, bank(st).rearrange("p (k q) -> p k q", q=P), xs, ALU.add), st)
                elif kind == "conv":
                    g = arg[0]
                    for m in (2 * g, 2 * g + 1):
                        taken(dve, ("proj", "ux", m))
                        dve.wait_ge(pad_zero, 1)
                        c_, u_ = lc[:, m % 2, :], uxp[:, m % 2, :]
                        link(v.tensor_scalar(c_, u_[:, 3:3 + S], G("conv_w_2", 24 + m), G("conv_b_2", m), ALU.mult, ALU.add))
                        for tap in (2, 1, 0):
                            ins = v.scalar_tensor_tensor(out=c_, in0=u_[:, tap:tap + S], scalar=G("conv_w_2", 8 * tap + m), in1=c_,
                                                         op0=ALU.mult, op1=ALU.add)
                            if tap:
                                link(ins)
                        ins.then_inc(conv_done, 1)
                elif kind == "lru":
                    g = arg[0]
                    dve.wait_ge(lru_exp, g + 1)
                    taken(dve, ("lru_gate", "i", 2 * g))
                    taken(dve, ("lru_gate", "i", 2 * g + 1))
                    dve.wait_ge(conv_done, 2 * g + 2)
                    link(v.tensor_scalar(lr_, lt, 1.0, None, ALU.add))
                    link(v.reciprocal(lr_, lr_))
                    v.scalar_tensor_tensor(out=lt, in0=lt, scalar=2.0, in1=lr_, op0=ALU.mult, op1=ALU.mult).then_inc(lru_m2, 1)
                    link(v.tensor_tensor(li, li, lc, ALU.mult))
                    dve.wait_ge(lru_mult, g + 1)
                    link(v.tensor_tensor(lt, lt, li, ALU.mult))
                    for m in (2 * g, 2 * g + 1):
                        v.tensor_tensor_scan(yl[:, m, :], la[:, m % 2, :], lt[:, m % 2, :], 0.0, ALU.mult, ALU.add).then_inc(lru_done, 1)
                    dve.wait_ge(lru_done, 2 * g + 2)
                elif kind == "stick":
                    def log_sum(h):
                        dve.wait_ge(sp_log, h + 1)
                        v.scalar_tensor_tensor(out=Lb[h % 2], in0=flat(h), scalar=0.0, in1=Lb[h % 2], op0=ALU.max,
                                               op1=ALU.add).then_inc(sp_done, 1)

                    dve.wait_ge(yl_done, KD)
                    log_sum(0)
                    log_sum(1)
                    for h in range(HB + 1):
                        if h >= 1:
                            lo = CH * ((h - 1) % 2)
                            dve.wait_ge(pv_done, h)
                            v.tensor_copy(q2[lo:lo + CH, (h - 1) // 2, :], ps_[lo:lo + CH, 6 + (h - 1) % 2, :]).then_inc(pv_out, 1)
                        if h + 2 < HB:
                            log_sum(h + 2)


def constants():
    c = np.zeros((P, NCONST), np.float32)

    def put(name, x):
        lo, hi = CONST[name]
        c[:, lo:hi] = x

    r, q = np.arange(P)[:, None], np.arange(P)[None, :]
    put("ident", r == q)
    put("ones", 1)
    put("blk", r // 64 == q // 64)
    put("before", r < q)
    put("chunkmask", (r // CH == q // CH) & (r <= q))
    put("negtri", -1.0 * (r >= q))
    put("negones", -1)
    put("stickbias", np.where(r >= q, -BIG, 0))
    dist = r + (S - P) - np.arange(S)[None, :]
    put("alibi", np.where(dist >= 0, -dist, -BIG))
    put("reset", (np.arange(S) % CH != 0)[None, :])
    put("half", np.arange(P)[:, None] // CH == np.arange(2)[None, :])
    put("thresholds", CAP * np.arange(1, 8)[None, :])
    put("first32", 32 - np.arange(32)[None, :])
    put("first4", 4 - np.arange(4)[None, :])
    put("expert", np.arange(32)[None, :])
    put("overblock", np.arange(NOVER)[None, :])
    put("token", np.arange(TT)[None, :] * P + r)
    put("eps", EPS)
    put("one", 1)
    return c


def gains(x):
    g = np.zeros((P, NGAIN), np.float32)
    for name, (lo, hi) in GAINS.items():
        if name == "router_bias":
            g[:, lo:hi] = np.concatenate([x["b_router_group"][0], x["b_router_expert"][0].reshape(-1)])[None, :]
            continue
        w = np.asarray(x[name]).reshape(-1)
        if w.size == 64:
            w = np.concatenate([w, w])
        g[:, lo:hi] = w.reshape(hi - lo, P).T
    return g


BIGS = ["w_in", "w_gla_gk", "w_mem_kv", "w_out", "w_gate", "w_up", "w_down", "w_in_2", "w_br_lru_2", "w_br_att_2",
        "w_out_2", "w_mlp_up_2", "w_mlp_down_2", "w_ple_gate_2", "w_ple_2"]


def kernel(**inputs):
    import concourse.bacc as bacc
    from concourse.bass_utils import run_bass_kernel_spmd

    x = {k: np.asarray(v) for k, v in inputs.items()}
    arrays = {k: np.ascontiguousarray(x[k]) for k in BIGS}
    arrays["xT"] = np.ascontiguousarray(x["x"][0].T)
    arrays["memT"] = np.ascontiguousarray(x["mem"][0].T)
    arrays["pT"] = np.ascontiguousarray(x["p_2"][0, 0].T)
    arrays["consts"] = constants()
    arrays["gains"] = gains(x)
    router = np.concatenate([x["w_router_group"][0], x["w_router_expert"][0].transpose(1, 0, 2).reshape(D, 32)], axis=1)
    arrays["w_router"] = np.ascontiguousarray(router.reshape(KD, P, 36).transpose(1, 0, 2))
    blocks = np.zeros((2 * KD, P, P), np.float32)
    for j, name in enumerate(("w_rgate_2", "w_igate_2")):
        for n in range(2 * KD):
            lo = 64 * (n % 2)
            blocks[2 * (n // 2) + j, lo:lo + 64, lo:lo + 64] = x[name][0, n]
    arrays["gate_blocks"] = blocks
    nc = bacc.Bacc("TRN2", target_bir_lowering=False, num_devices=1)
    a = {k: nc.dram_tensor(k, v.shape, mybir.dt.from_np(v.dtype), kind="ExternalInput").ap() for k, v in arrays.items()}
    out = nc.dram_tensor("outT", (D, S), F32, kind="ExternalOutput").ap()
    build(nc, a, out)
    r = run_bass_kernel_spmd(nc, [arrays], core_ids=[0])
    return np.ascontiguousarray(r.results[0]["outT"].T)[None]
```

```python
import math
from contextlib import ExitStack

import concourse.bass as bass
from concourse import mybir
import numpy as np

F32 = mybir.dt.float32
F32R = mybir.dt.float32r
I32 = mybir.dt.int32
ALU = mybir.AluOpType
ACT = mybir.ActivationFunctionType
AX = mybir.AxisListType.X

P = 128
S = 512
D = 1024
KD = D // P
TT = S // P
NM = 256
MT = NM // P
PAN = KD * 512
RANK = 16
CH = 64
NE, FF = 32, 512
CAP = 64
NOVER = 2 * S // CAP - 1
NROWS = (NE + NOVER) * CAP
EPS = 1e-6
BIG = 1e30
JB = 7
HB = 16


def columns(widths):
    at, out = 0, {}
    for name, w in widths:
        out[name] = (at, at + w)
        at += w
    return out, at


CONST, NCONST = columns([
    ("ident", P), ("ones", P), ("blk", P), ("before", P), ("chunkmask", P), ("negtri", P), ("negones", P),
    ("stickbias", P), ("alibi", S), ("reset", S), ("half", 2), ("thresholds", 7), ("first32", 32), ("first4", 4),
    ("expert", 32), ("overblock", NOVER), ("token", TT), ("eps", 1), ("one", 1)])

GAINS, NGAIN = columns([
    ("attn_norm_g", 8), ("mem_norm_g", 8), ("ffn_norm_g", 8), ("norm_mix_g_2", 8), ("norm_mlp_g_2", 8),
    ("norm_ple_g_2", 8), ("norm_final_g_2", 8), ("b_gla_gk", 2), ("gla_out_norm_g", 1), ("moba_q_norm_g", 1),
    ("moba_k_norm_g", 1), ("mem_q_norm_g", 1), ("mem_k_norm_g", 1), ("conv_w_2", 32), ("conv_b_2", 8),
    ("b_rgate_2", 8), ("b_igate_2", 8), ("lru_lambda_2", 8), ("router_bias", 36)])


def plan():
    steps, jobs = [], []

    def step(kind, *args):
        steps.append((kind, *args))

    def job(kind, *args):
        jobs.append((kind, *args))
        steps.append((kind, *args))

    def attention(which, fill):
        units = [(which, pr, qt, hh) for pr in range(2) for qt in range(TT) for hh in range(2)]
        fill = list(fill)
        for u in range(len(units) + 3):
            if u < len(units):
                job("score", *units[u])
            if u >= 3 and (u - 3) % 2 == 1:
                job("values", *units[u - 3][:3])
            if 2 <= u < len(units) + 2:
                job("turn", *units[u - 2])
            if fill and u % 2 == 0:
                for f in fill.pop(0):
                    emit(f)
            if u < len(units):
                step("softmax", *units[u])
        if (len(units) - 1) % 2 == 1 and ("values", *units[-1][:3]) not in jobs:
            job("values", *units[-1][:3])
        for fs in fill:
            for f in fs:
                emit(f)

    def emit(f):
        (step if f[0] in STEPS_ONLY else job)(*f)
        if f[0] == "proj" and f[1] in ("mq", "mk", "cq", "ck"):
            job("headsum", f[1], f[2])

    step("mem_norm")
    step("norm", 0)
    for n in range(2):
        emit(("proj", "ck", n))
    for n in range(MT):
        emit(("proj", "cv", n))
    for n in range(2):
        emit(("proj", "cq", n))
    attention("mem", [[("proj", "mv", t)] for t in range(TT)] + [[("proj", "mq", n)] for n in range(2)]
              + [[("proj", "mk", n)] for n in range(2)])
    attention("moba", [[("proj", "gq", 0)], [("proj", "gq", 1)], [("proj", "gk", 0)], [("proj", "gk", 1)],
                       [("proj", "lr", 0), ("gate", 0), ("gate", 1)]] + [[("proj", "gv", t)] for t in range(TT)])
    step("gla_begin")
    step("decay", 0)
    job("proj", "r", 0)
    job("proj", "r", 1)
    for pr in range(2):
        job("turn_keys", pr)
        for hh in range(2):
            job("intra", pr, hh)
        for g in range(4):
            job("chunk_state", pr, g)
        if pr == 0:
            job("proj", "r", 2)
            job("proj", "r", 3)
        for hh in range(2):
            job("gla_out", pr, hh)
            job("gla_sum", pr, hh)
        if pr == 0:
            step("decay", 1)
    for n in range(KD):
        job("proj", "out", n)
        step("square", 1, n)
    step("norm", 1)
    job("router")
    for t in range(TT):
        for half in range(2):
            job("turn_h", t, half)
    step("route")
    job("rank")
    step("place")
    step("moe")
    for t in range(TT):
        for half in range(2):
            job("turn_y", t, half)
        if t:
            step("y_square", t - 1)
    step("y_square", TT - 1)
    step("norm", 2)
    step("split", 0)

    halves = [(name, h) for name in PANELS2[:-1] for h in range(2)]
    ahead = [0]

    def half_jobs(g):
        name, h = halves[g]
        while ahead[0] <= min(g + 1, len(halves) - 1):
            if ahead[0] > g and name == "v21" and h == 1:
                break
            step("weights", ahead[0])
            ahead[0] += 1
        base, n = name[:-1], int(name[-1])
        if base == "v2":
            return [("proj", "v2", (2 * n + h) * TT + t) for t in range(TT)]
        return [("proj", base, 4 * n + 2 * h + j) for j in range(2)]

    for g, (name, h) in enumerate(halves):
        if (name, h) == ("gl0", 0):
            step("stick")
        if (name, h) == ("bl0", 0):
            step("split", 1)
        if (name, h) == ("ba0", 0):
            step("split", 2)
        if (name, h) == ("out20", 0):
            step("split", 3)
        if (name, h) == ("up0", 0):
            step("norm", 3)
            step("split", 4)
        if (name, h) == ("pg0", 0):
            step("norm", 4)
            step("split", 5)
        for jb in half_jobs(g):
            job(*jb)
            n = jb[2]
            if jb[1] == "ux" and n % 2:
                step("conv", n // 2)
                for m in (n - 1, n):
                    job("lru_gate", "r", m)
                    job("lru_gate", "i", m)
                step("lru", n // 2)
            if jb[1] == "out2":
                step("square", 3, n)
            if jb[1] == "dn" and n >= 3 * KD:
                step("square", 4, n - 3 * KD)
    for n in range(KD):
        job("proj", "ple", n)
        step("square", 5, n)
    step("norm", 5)
    return steps, jobs


SQUARED = (1, 3, 4, 5)
STICK_HALVES = (20, 21)
STEPS_ONLY = ("softmax",)
PHASE2 = ("ux", "ug", "q2", "k2", "v2", "gl", "ga", "bl", "ba", "out2", "up", "dn", "pg")

PANELS1 = ["memkv", "mvcq", "mqk", "gqk", "gv", "r", "out0", "out1"]
PANELS2 = ["ux0", "ux1", "ug0", "ug1", "q20", "q21", "k20", "k21", "v20", "v21", "gl0", "gl1", "ga0", "ga1",
           "bl0", "bl1", "ba0", "ba1", "out20", "out21", "up0", "up1", "up2", "up3", "dn0", "dn1", "up4", "up5",
           "dn2", "dn3", "up6", "up7", "dn4", "dn5", "dn6", "dn7", "pg0", "pg1", "ple"]
SLOTS1, SLOTS2 = 4, 3
SPLITS = ("mixed input", "lru", "attention", "merged", "mlp input", "ple input")


def build(nc, a, out):
    steps, jobs = plan()
    J = {name: n for n, name in enumerate(jobs)}
    hn_index = {n[1:]: i for i, n in enumerate(x for x in jobs if x[0] == "headsum")}
    unit_index = {n[1:]: i for i, n in enumerate(x for x in steps if x[0] == "softmax")}

    with ExitStack() as ctx:
        def sb(name, n, dt=F32):
            return ctx.enter_context(nc.sbuf_tensor("sb_" + name, [P, n], dt))

        def sem(name):
            return ctx.enter_context(nc.semaphore(name))

        def dram(name, shape, dt):
            return nc.dram_tensor(name, shape, dt, kind="Internal").ap()

        slot = [sb(f"slot{i}", PAN) for i in range(3)]
        xT_ = sb("xT", KD * S)
        F = sb("F", 1280)
        cst = sb("cst", NCONST)
        prm = sb("prm", NGAIN)
        small = sb("small", 288)
        table_i = sb("table_i", 32, I32)
        idx = [sb(f"idx{b}", 1, I32) for b in range(2)]
        zeros_i = sb("zeros_i", NROWS // CAP, I32)
        with ExitStack() as first:
            def fb(name, n):
                return first.enter_context(nc.sbuf_tensor("sb_" + name, [P, n], F32))

            slot += [fb(f"slot{i}", PAN) for i in range(3, 6)]
            hT_ = fb("hT", KD * S)
            R = fb("R", 4 * KD * S)
        WH = [sb(f"w_high{i}", PAN // 2, F32R) for i in range(2)]
        WL = [sb(f"w_low{i}", PAN // 2, F32R) for i in range(2)]
        HH_, HL_ = sb("h_high", KD * S, F32R), sb("h_low", KD * S, F32R)
        HC_ = [[sb(f"hidden_{part}{i}", KD * S, F32R) for part in ("high", "low")] for i in range(2)]
        ps_ = ctx.enter_context(nc.psum_tensor("ps", [P, 8, 512], F32))

        def C(name):
            lo, hi = CONST[name]
            return cst[:, lo:hi]

        def G(name, i=0):
            lo = GAINS[name][0] + i
            return prm[:, lo:lo + 1]

        def view(t, at, *dims):
            n = int(np.prod(dims))
            v = t[:, at:at + n]
            if len(dims) == 2:
                return v.rearrange("p (a b) -> p a b", a=dims[0])
            if len(dims) == 3:
                return v.rearrange("p (a b c) -> p a b c", a=dims[0], b=dims[1])
            return v

        xT, hT = view(xT_, 0, KD, S), view(hT_, 0, KD, S)
        acc = view(F, 0, S)
        sq = view(F, 512, S)
        std = view(F, 512, S)
        mixT = view(R, 0, KD, S)
        qpad = view(R, 4096, 4, S)
        kn = view(R, 6144, 2, S)
        vpad = view(R, 7168, TT, 4, P)
        cqpad = view(R, 9216, 4, S)
        ckn = view(R, 11264, 2, NM)
        cvpad = view(R, 11776, MT, 4, P)
        s_sb = view(R, 13312, 2, S)
        p_sb = view(R, 14336, 2, S)
        pT = view(R, 15360, 2, TT, P)
        memT = view(slot[5], 0, KD, NM)
        memh = view(slot[5], 2048, KD, NM)
        hn_raw = view(slot[5], 0, 2, S)
        hn_sq = view(slot[5], 1024, 2, S)
        gq = view(slot[4], 0, 2, S)
        gk = view(slot[4], 1024, 2, S)
        lrT = view(slot[4], 2048, S)
        zb = view(slot[4], 2560, 2, S)
        slope_b = view(slot[4], 3584, S)
        gv = view(R, 9216, TT, S)
        rs = view(R, 11264, 4, S)
        t1 = view(R, 4096, S)
        cum = view(R, 4608, S)
        ecum = view(R, 5120, S)
        einv = view(R, 5632, S)
        eend = view(R, 6144, S)
        kend_f = view(R, 6656, S)
        kend = view(R, 7168, 2, TT, P)
        osq = view(R, 8192, S)
        ogn = view(R, 8704, S)
        qdec = view(R, 13312, 2, S)
        ostd = view(R, 14336, S)
        at_sb = view(R, 14848, 2, TT, P)
        kinv = view(slot[5], 0, 4, S)
        state = view(slot[5], 2048, 8, 2 * P)
        htok = view(R, 0, TT, D)
        xg = [view(R, 4096 + 1024 * b, D) for b in range(2)]
        yout = [view(R, 6144 + 1024 * b, D) for b in range(2)]
        xgT = [view(R, 8192 + 512 * b, KD, CAP) for b in range(2)]
        sg = [view(R, 9216 + 256 * b, 4, CAP) for b in range(2)]
        hid = [view(R, 9728 + 256 * b, 4, CAP) for b in range(2)]
        lg = view(R, 10240, TT, 36)
        wk32 = view(R, 10400, TT, 32)
        wk32b = view(R, 10528, TT, 32)
        oh = [view(R, 10656 + 128 * k, TT, 32) for k in range(2)]
        M = view(R, 10912, TT, 32)
        dest = view(R, 11040, TT, 32)
        w4 = view(R, 11168, TT, 4)
        w4b = view(R, 11184, TT, 4)
        cmp = view(R, 11200, 32, 7)
        cmp2 = view(R, 11424, NOVER, 32)
        cnt, nb, obend, dd = (view(R, 11904 + 32 * i, 32) for i in range(4))
        otab = view(R, 12032, NOVER)
        w_router = view(R, 15872, KD, 36)
        col = [view(R, 12600 + 4 * i, TT) for i in range(12)]
        gate_w = view(small, 0, 2, TT)
        dest_i = table_i[:, 0:8]
        token_i = table_i[:, 8:12]
        over_i = table_i[:, 12:12 + NOVER + 1]
        yg = [view(R, 1024 * i, D) for i in range(2 * TT)]
        q2, k2, v2, yl = (view(R, 4096 * i, KD, S) for i in range(4))
        v2 = view(R, 8192, TT, D)
        lc, lr_, li, la = (view(R, 8192 + 1024 * i, 2, S) for i in range(4))
        uxp = view(R, 4096, 2, S + 4)
        lt = view(R, 5136, 2, S)
        sp8 = view(small, 16, KD)
        nsp8 = view(small, 24, KD)
        lw = [view(small, 32 + 8 * i, KD) for i in range(6)]
        row_max, row_neg, row_sum, row_inv = (view(small, 96 + 2 * i, 2) for i in range(4))
        dec = [view(small, 112 + 8 * i, 8) for i in range(2)]
        w_lr = view(R, 0, KD * RANK)
        w_gk = view(R, 128, 2 * P)
        w_bd = view(F, 1024, 2, P)
        SEG = [(0, 512), (512, 384), (1024, 256), (896, 128)]
        Lb = [view(slot[3], 0, 1280), view(slot[3], 1280, 1280)]
        att = [view(slot[3], 2560, 1280), view(slot[4], 0, 1280)]
        WH = [w[:, :].rearrange("p (k n) -> p k n", k=KD) for w in WH]
        WL = [w[:, :].rearrange("p (k n) -> p k n", k=KD) for w in WL]
        HH, HL = (w[:, :].rearrange("p (k n) -> p k n", k=KD) for w in (HH_, HL_))
        HC = [[w[:, :].rearrange("p (k n) -> p k n", k=KD) for w in pair] for pair in HC_]
        tmp = view(R, 8192, 4, S)
        relu = view(F, 0, 2, S)
        sig = {"gl": view(R, 4096, KD, S), "ga": view(R, 8192, KD, S)}
        merged = yl
        prod = {"ba": view(F, 0, S), "ple": view(R, 5120, S)}
        pgs = view(R, 0, KD, S)
        pT2 = view(R, 4096, 2, S)

        h_dram = dram("h_rows", (S, D), F32)
        y_dram = dram("y_rows", (NROWS, D), F32)
        slot_dram = dram("row_tokens", (NROWS, 1), I32)

        pe_done = sem("pe_done")
        bank_free = [sem(f"bank_free{b}") for b in range(JB)]
        ld = {n: sem(f"ld_{n}") for n in ("cst", "prm", "mem", "x", "wlr", "wgk", "router", "p")}
        ld_bd = [sem(f"ld_bd{j}") for j in range(2)]
        pan1 = [sem(f"pan1_{i}") for i in range(SLOTS1)]
        pan2 = [sem(f"pan2_{i}") for i in range(SLOTS2)]
        act_chain, dve_chain, pool_chain = sem("act_chain"), sem("dve_chain"), sem("pool_chain")
        mem_sq, mem_sum, mem_std, mem_h = sem("mem_sq"), sem("mem_sum"), sem("mem_std"), sem("mem_h")
        squared, summed, std_done, h_ready = sem("squared"), sem("summed"), sem("std_done"), sem("h_ready")
        x_new, acc_done, tmp_done = sem("x_new"), sem("acc_done"), sem("tmp_done")
        high_done, low_done, w_high, w_low = sem("high_done"), sem("low_done"), sem("w_high"), sem("w_low")
        relu_sq, hid_high, hid_low = sem("relu_sq"), sem("hid_high"), sem("hid_low")
        zeroed = sem("zeroed")
        hn_in, hn_std, hn_done = sem("hn_in"), sem("hn_std"), sem("hn_done")
        slope_ok = sem("slope_ok")
        s_ready, neg_ready, exp_done, p_ready = sem("s_ready"), sem("neg_ready"), sem("exp_done"), sem("p_ready")
        gla_go, state_zero = sem("gla_go"), sem("state_zero")
        lsig, cum_done, dec_exp, qk_ready = sem("lsig"), sem("cum_done"), sem("dec_exp"), sem("qk_ready")
        st_done = sem("st_done")
        o_sq, o_std, o_done = sem("o_sq"), sem("o_std"), sem("o_done")
        r_exp, r_gd, r_m, r_dest = sem("r_exp"), sem("r_gd"), sem("r_m"), sem("r_dest")
        r_e2in, r_e2 = sem("r_e2in"), sem("r_e2")
        h_stored, zeros_set, zeros_stored, tokens_stored = (
            sem("h_stored"), sem("zeros_set"), sem("zeros_stored"), sem("tokens_stored"))
        m_w = [sem(f"m_w{i}") for i in range(6)]
        m_idx, m_x, m_turned, m_xT, m_gu, m_silu, m_hid, m_down, m_y, m_st = (
            [sem(f"{n}{b}") for b in range(2)] for n in
            ("m_idx", "m_x", "m_turned", "m_xT", "m_gu", "m_silu", "m_hid", "m_down", "m_y", "m_st"))
        o_w = sem("o_w")
        o_idx, o_x, o_turned, o_xT, o_gu, o_silu, o_hid, o_down, o_y, o_st = (
            sem(n) for n in ("o_idx", "o_x", "o_turned", "o_xT", "o_gu", "o_silu", "o_hid", "o_down", "o_y", "o_st"))
        y_squared = sem("y_squared")
        y_got, y_mixed = [sem(f"y_got{t}") for t in range(TT)], sem("y_mixed")
        pad_zero, conv_done, gates_done, lru_exp, lru_m2, lru_mult, lru_done = (
            sem(n) for n in ("pad_zero", "conv_done", "gates_done", "lru_exp", "lru_m2", "lru_mult", "lru_done"))
        lam_exp, lam_done = sem("lam_exp"), sem("lam_done")
        gelu_done, yl_done = sem("gelu_done"), sem("yl_done")
        z_done, sp_log, sp_done, tri_done, att_done, pv_done, pv_out = (
            sem(n) for n in ("z_done", "sp_log", "sp_done", "tri_done", "att_done", "pv_done", "pv_out"))
        merge_done = sem("merge_done")
        stored = sem("stored")
        passed = {e: sem(f"passed_{e}") for e in ("pool", "pe", "sp")}

        def bank(name):
            return ps_[:, J[name] % JB, :]

        def finished(eng, name):
            eng.wait_ge(pe_done, J[name] + 1)

        def taken(eng, name):
            eng.wait_ge(bank_free[J[name] % JB], J[name] // JB + 1)

        def frees(ins, name):
            return ins.then_inc(bank_free[J[name] % JB], 1)

        w_in, w_in2 = a["w_in"], a["w_in_2"]

        def panel_src(name):
            def cols(w, lo):
                return w[0, :, lo:lo + 512].rearrange("(k p) n -> p k n", p=P)
            if name == "memkv":
                return cols(a["w_mem_kv"], 0)
            if name in ("gqk", "gv", "r", "mqk", "mvcq"):
                return cols(w_in, {"gqk": 0, "gv": 512, "r": 1024, "mqk": 1552, "mvcq": 2064}[name])
            if name in ("out0", "out1"):
                return cols(a["w_out"], 512 * int(name[-1]))
            base, n = name[:-1], name[-1]
            if base in ("ux", "ug", "q2", "k2", "v2", "gl", "ga"):
                return cols(w_in2, ["ux", "ug", "q2", "k2", "v2", "gl", "ga"].index(base) * D + 512 * int(n))
            if base in ("bl", "ba", "out2", "up", "pg"):
                w = a[{"bl": "w_br_lru_2", "ba": "w_br_att_2", "out2": "w_out_2", "up": "w_mlp_up_2",
                       "pg": "w_ple_gate_2"}[base]]
                return cols(w, 512 * int(n))
            if base == "dn":
                c, half = int(n) // 2, int(n) % 2
                return a["w_mlp_down_2"][0, D * c:D * c + D, 512 * half:512 * half + 512].rearrange(
                    "(k p) n -> p k n", p=P)
            return a["w_ple_2"][0].rearrange("(k p) n -> p k n", p=P)

        def where(name, n):
            if name in ("ck", "cv"):
                return "memkv", (0 if name == "ck" else 256)
            if name in ("cq", "mv"):
                return "mvcq", (256 if name == "cq" else 0)
            if name in ("mq", "mk"):
                return "mqk", (0 if name == "mq" else 256)
            if name in ("gq", "gk"):
                return "gqk", (0 if name == "gq" else 256)
            if name in ("gv", "r"):
                return name, 0
            if name == "out":
                return f"{name}{n // 4}", 0
            return name, 0

        def last_use(panel):
            return next(nm for nm in reversed(jobs) if nm[0] == "proj" and nm[1] not in PHASE2 + ("lr",)
                        and where(nm[1], nm[2])[0] == panel)

        def half_of(name, n):
            p, h = (n // 8, n // 4 % 2) if name == "v2" else (n // 4, n % 4 // 2)
            return 2 * PANELS2.index(f"{name}{p}") + h

        half_last = {}
        for nm in jobs:
            if nm[0] == "proj" and nm[1] in PHASE2:
                half_last[half_of(*nm[1:])] = nm

        def half_free(eng, g):
            if g >= 2:
                finished(eng, half_last[g - 2])

        def split_src(s, k):
            return {1: yl, 2: q2, 3: merged}[s][:, k, :] if s in (1, 2, 3) else tmp[:, k % 4, :]

        split_old = {1: ("proj", "ga", 7), 2: ("proj", "bl", 7), 3: ("proj", "ba", 7), 4: ("proj", "out2", 7),
                     5: ("proj", "up", 31)}

        def norm_used(eng, norm):
            if norm <= 2:
                eng.wait_ge(h_ready, 8 * norm)
            else:
                eng.wait_ge(tmp_done, 8 * (norm - 2))

        def panel_at(name):
            if name in PANELS1:
                n = PANELS1.index(name)
                return slot[n % SLOTS1], pan1[n % SLOTS1], 16 * (n // SLOTS1 + 1)
            n = PANELS2.index(name)
            return slot[n % SLOTS2], pan2[n % SLOTS2], 16 * (n // SLOTS2 + 1)

        def raw_half(g):
            t = panel_at(PANELS2[g // 2])[0][:, :].rearrange("p (k n) -> p k n", k=KD)
            return t[:, :, 256 * (g % 2):256 * (g % 2) + 256]

        def expert_src(name, e):
            w = a[name][0, e]
            return w.rearrange("(k p) n -> p k n", p=P)

        def pairs(eng, body):
            body(0)
            with eng.Fori(1, NE // 2) as i:
                body(i)

        def overflow(eng, n_over, body):
            with eng.If(n_over > 0):
                body(0)
                with eng.Fori(1, NOVER) as i:
                    with eng.If(i < n_over):
                        body(i)

        def free(eng, s, v):
            if type(v) is not int or v > 0:
                eng.wait_ge(s, v)

        def prev_unit(u):
            return next(n for n, i in unit_index.items() if i == u)

        def flat(h):
            b0 = 3 * (h % 2)
            return ps_[:, b0:b0 + 3, :].rearrange("p a b -> p (a b)")[:, 0:1280]

        GU = ("w_gate", "w_up")
        block = ctx.enter_context(nc.Block())

        @block.sync
        def _(sp):
            def load(dst, src, s):
                sp.dma_start(dst, src).then_inc(s, 16)

            load(cst[:, :], a["consts"], ld["cst"])
            load(prm[:, :], a["gains"], ld["prm"])
            load(memT, a["memT"].rearrange("(k p) n -> p k n", p=P), ld["mem"])
            load(slot[0][:, :].rearrange("p (k n) -> p k n", k=KD), panel_src("memkv"), pan1[0])
            load(xT, a["xT"].rearrange("(k p) n -> p k n", p=P), ld["x"])
            load(w_lr.rearrange("p (k n) -> p k n", k=KD),
                 w_in[0, :, 1536:1536 + RANK].rearrange("(k p) n -> p k n", p=P), ld["wlr"])
            load(w_gk[0:RANK, :], a["w_gla_gk"][0], ld["wgk"])
            for n, name in enumerate(PANELS1):
                if n == 0:
                    continue
                if n >= SLOTS1:
                    finished(sp, last_use(PANELS1[n - SLOTS1]))
                load(slot[n % SLOTS1][:, :].rearrange("p (k n) -> p k n", k=KD), panel_src(name), pan1[n % SLOTS1])

            def pair_load(e, b, part):
                if part == "gu":
                    for j in range(2):
                        load(slot[2 * b + j][:, :].rearrange("p (k n) -> p k n", k=KD), expert_src(GU[j], e),
                             m_w[2 * b + j])
                else:
                    load(slot[4 + b][:, :].rearrange("p (k n) -> p k n", k=4), expert_src("w_down", e), m_w[4 + b])

            finished(sp, ("gla_sum", 1, 1))
            sp.wait_ge(st_done, 14 * 2)
            sp.wait_ge(qk_ready, 2)
            load(w_router, a["w_router"], ld["router"])
            pair_load(0, 0, "down")
            pair_load(1, 1, "down")
            for n in (4, 5):
                finished(sp, last_use(PANELS1[n]))
            pair_load(0, 0, "gu")
            for n in (6, 7):
                finished(sp, last_use(PANELS1[n]))
            pair_load(1, 1, "gu")
            with sp.Fori(1, NE // 2) as i:
                for b in range(2):
                    sp.wait_ge(m_gu[b], i)
                    pair_load(2 * i + b, b, "gu")
                for b in range(2):
                    sp.wait_ge(m_down[b], i)
                    pair_load(2 * i + b, b, "down")
            for b in range(2):
                sp.wait_ge(m_gu[b], NE // 2)
                sp.wait_ge(m_down[b], NE // 2)
            sp.wait_ge(r_dest, 1)
            n_over = sp.value_load(over_i[0:1, NOVER:NOVER + 1], min_val=0, max_val=NOVER)

            def over_load(i):
                e = sp.value_load(over_i[0:1, bass.ds(i, 1)], min_val=0, max_val=NE - 1)
                for j in range(2):
                    load(slot[j][:, :].rearrange("p (k n) -> p k n", k=KD), expert_src(GU[j], e), o_w)
                load(slot[4][:, :].rearrange("p (k n) -> p k n", k=4), expert_src("w_down", e), o_w)
                sp.wait_ge(o_st, 16 * i + 16)
                sp.sem_inc(passed["sp"], 1)

            overflow(sp, n_over, over_load)
            for n, name in enumerate(PANELS2):
                if n >= SLOTS2:
                    sp.wait_ge(w_low, 2 * (n - SLOTS2) + 2)
                dst = slot[n % SLOTS2]
                if name == "ple":
                    finished(sp, ("proj", "dn", 31))
                    load(pT2, a["pT"].rearrange("(k p) n -> p k n", p=P), ld["p"])
                    load(dst[:, 0:2 * D].rearrange("p (k n) -> p k n", k=2), panel_src(name), pan2[n % SLOTS2])
                else:
                    load(dst[:, :].rearrange("p (k n) -> p k n", k=KD), panel_src(name), pan2[n % SLOTS2])
            for k in range(KD):
                sp.wait_ge(h_ready, 8 * 2 + k + 1)
                sp.dma_start(out[k * P:(k + 1) * P, :], hT[:, k, :]).then_inc(stored, 16)
            sp.wait_ge(stored, 16 * KD)

        @block.gpsimd
        def _(pool):
            chain = [0]

            def link(ins):
                chain[0] += 1
                ins.then_inc(pool_chain, 1)
                pool.wait_ge(pool_chain, chain[0])

            nc.gpsimd.memset(R[:, 4096:6144], 0.0).then_inc(zeroed, 1)
            nc.gpsimd.memset(R[:, 7168:11264], 0.0).then_inc(zeroed, 1)
            nc.gpsimd.memset(R[:, 11776:12800], 0.0).then_inc(zeroed, 1)
            nc.gpsimd.memset(zeros_i[0:CAP, :], 0).then_inc(zeros_set, 1)
            pool.wait_ge(zeros_set, 1)
            pool.dma_start(slot_dram.rearrange("(b s) o -> b (s o)", b=CAP), zeros_i[0:CAP, :]).then_inc(zeros_stored, 16)
            nc.gpsimd.memset(R[:, 12800:13312], 0.0).then_inc(zeros_set, 1)
            pool.wait_ge(zeros_set, 2)
            zp = NOVER * CAP // 8
            pool.dma_start(y_dram[NE * CAP:NROWS, :].rearrange("(z r) (c n) -> z (r c) n", z=zp, c=2),
                           R[0:zp, 12800:13312].unsqueeze(1).to_broadcast([zp, 16, 512])).then_inc(zeros_stored, 16)
            pool.wait_ge(ld["cst"], 16)
            link(nc.gpsimd.tensor_copy(token_i, C("token")))
            finished(pool, ("values", "moba", 1, TT - 1))
            pool.wait_ge(hn_done, 8)
            nc.gpsimd.memset(slot[5][:, :], 0.0).then_inc(state_zero, 1)
            pool.wait_ge(zeros_stored, 32)
            pool.wait_ge(r_dest, 1)
            for k in range(2):
                for t in range(TT):
                    nc.gpsimd.indirect_dma_start(
                        slot_dram, bass.IndirectOffsetOnAxis(ap=dest_i[:, k * TT + t:k * TT + t + 1], axis=0),
                        token_i[:, t:t + 1], None).then_inc(tokens_stored, 16)
            pool.wait_ge(tokens_stored, 16 * 2 * TT)
            pool.wait_ge(h_stored, 16 * TT)

            def fetch(first, b, i, s_idx, s_x, s_free):
                free(pool, s_free, i)
                pool.dma_start(idx[b][0:CAP, :], slot_dram[bass.ds(first, CAP), :]).then_inc(s_idx, 16)
                pool.wait_ge(s_idx, 16 * i + 16)
                pool.sem_inc(passed["pool"], 1)
                nc.gpsimd.indirect_dma_start(
                    xg[b][0:CAP, :], None, h_dram,
                    bass.IndirectOffsetOnAxis(ap=idx[b][0:CAP, :], axis=0)).then_inc(s_x, 16)
                pool.wait_ge(s_x, 16 * i + 16)

            pairs(pool, lambda i: [fetch((2 * i + b) * CAP, b, i, m_idx[b], m_x[b], m_turned[b]) for b in range(2)])
            for b in range(2):
                pool.wait_ge(m_st[b], 16 * (NE // 2))
            n_over = nc.gpsimd.value_load(over_i[0:1, NOVER:NOVER + 1], min_val=0, max_val=NOVER)

            def over_fetch(i):
                fetch((NE + i) * CAP, 0, i, o_idx, o_x, o_turned)
                pool.wait_ge(o_st, 16 * i + 16)

            overflow(pool, n_over, over_fetch)
            for t in range(TT):
                for k in range(2):
                    nc.gpsimd.indirect_dma_start(
                        yg[2 * t + k], None, y_dram,
                        bass.IndirectOffsetOnAxis(ap=dest_i[:, k * TT + t:k * TT + t + 1], axis=0)
                    ).then_inc(y_got[t], 16)
            for n in range(KD):
                for j, which in enumerate("ri"):
                    if n:
                        finished(pool, ("lru_gate", which, n - 1))
                    else:
                        finished(pool, ("turn_y", TT - 1, 1))
                    pool.dma_start(w_bd[:, j, :], a["gate_blocks"][2 * n + j]).then_inc(ld_bd[j], 16)

        @block.tensor
        def _(pe):
            def begin(name):
                n = J[name]
                if n >= JB:
                    pe.wait_ge(bank_free[n % JB], n // JB)
                return bank(name)

            def end(ins):
                ins.then_inc(pe_done, 1)

            def panel(name):
                t, s, v = panel_at(name)
                pe.wait_ge(s, v)
                return t[:, :].rearrange("p (k n) -> p k n", k=KD)

            tok_major = ("mv", "cv", "gv")

            def project2(name, n):
                o = begin(("proj", name, n))
                g = half_of(name, n)
                if name == "dn":
                    c = n // KD
                    high, low = HC[c % 2]
                else:
                    s = {"bl": 1, "ba": 2, "out2": 3, "up": 4, "pg": 5}.get(name, 0)
                    high, low = HH, HL
                for i, (w, h) in enumerate(((WH, high), (WL, high), (WH, low))):
                    if i < 2:
                        pe.wait_ge(w_low if i else w_high, g + 1)
                    for k in range(KD):
                        if i != 1:
                            if name == "dn":
                                pe.wait_ge(hid_low if i else hid_high, c * KD + k + 1)
                            else:
                                pe.wait_ge(low_done if i else high_done, KD * s + k + 1)
                        first, last = i == 0 and k == 0, i == 2 and k == KD - 1
                        if name == "v2":
                            t = n % TT
                            ins = nc.tensor.matmul(o[:, 0:256], h[:, k, t * P:(t + 1) * P], w[g % 2][:, k, :], start=first, stop=last)
                        else:
                            ins = nc.tensor.matmul(o, w[g % 2][:, k, n % 2 * P:(n % 2 + 1) * P], h[:, k, :], start=first, stop=last)
                end(ins)

            def project(name, n):
                if name in PHASE2:
                    return project2(name, n)
                o = begin(("proj", name, n))
                if name == "lr":
                    pe.wait_ge(ld["wlr"], 16)
                    w = w_lr.rearrange("p (k n) -> p k n", k=KD)
                    for k in range(KD):
                        ins = nc.tensor.matmul(o[0:RANK, :], w[:, k, :], hT[:, k, :], start=(k == 0), stop=(k == KD - 1))
                    end(ins)
                    return
                pn, off = where(name, n)
                w = panel(pn)
                if name == "ple":
                    w = panel_at(pn)[0][:, 0:2 * D].rearrange("p (k n) -> p k n", k=2)
                    pe.wait_ge(ld["p"], 16)
                    for k in range(2):
                        ins = nc.tensor.matmul(o, w[:, k, n * P:(n + 1) * P], pT2[:, k, :], start=(k == 0), stop=(k == 1))
                    end(ins)
                    return
                src = hT
                if name in ("ck", "cv"):
                    src = memh
                elif name == "out":
                    src = mixT
                for k in range(KD):
                    if name in ("ck", "cv"):
                        pe.wait_ge(mem_h, k + 1)
                    elif name == "out" and k < 4:
                        pe.wait_ge(o_done, k + 1)
                    elif name == "out":
                        if k == 4 and n == 0:
                            for w_ in ("mem", "moba"):
                                for pr in range(2):
                                    for qt in range(TT):
                                        taken(pe, ("values", w_, pr, qt))
                    elif name != "out":
                        pe.wait_ge(h_ready, k + 1)
                    if name in tok_major:
                        t = n % TT
                        width = {"mv": 256, "cv": 256, "gv": 512}[name]
                        ins = nc.tensor.matmul(o[:, 0:width], src[:, k, t * P:(t + 1) * P], w[:, k, off:off + width],
                                               start=(k == 0), stop=(k == KD - 1))
                    else:
                        c = off + (n % 4) * P
                        width = NM if name == "ck" else S
                        ins = nc.tensor.matmul(o[:, 0:width], w[:, k, c:c + P], src[:, k, :],
                                               start=(k == 0), stop=(k == KD - 1))
                end(ins)

            def norm_sum(norm):
                pe.wait_ge(std_done, norm)
                pe.wait_ge(acc_done, 7 * SQUARED.index(norm) + 7)
                nc.tensor.matmul(ps_[:, 7, :], C("ones"), acc, start=True, stop=True).then_inc(summed, 1)

            for st in steps:
                kind, arg = st[0], st[1:]
                if kind == "mem_norm":
                    pe.wait_ge(ld["cst"], 16)
                    pe.wait_ge(mem_sq, 1)
                    for k in range(KD):
                        ins = nc.tensor.matmul(ps_[:, 7, 0:NM], C("ones"), memh[:, k, :], start=(k == 0), stop=(k == KD - 1))
                    ins.then_inc(mem_sum, 1)
                elif kind == "norm":
                    norm = arg[0]
                    if norm == 0:
                        pe.wait_ge(mem_std, 1)
                        for n in range(KD):
                            pe.wait_ge(squared, n + 1)
                            ins = nc.tensor.matmul(ps_[:, 7, :], C("ones"), hT[:, n, :], start=(n == 0), stop=(n == KD - 1))
                        ins.then_inc(summed, 1)
                    elif norm != 2:
                        norm_sum(norm)
                elif kind == "y_square":
                    t = arg[0]
                    pe.wait_ge(std_done, 2)
                    pe.wait_ge(y_squared, t + 1)
                    for k in range(KD):
                        ins = nc.tensor.matmul(ps_[:, 7, t * P:(t + 1) * P], C("ones"), hT[:, k, t * P:(t + 1) * P],
                                               start=(k == 0), stop=(k == KD - 1))
                    if t == TT - 1:
                        ins.then_inc(summed, 1)
                elif kind == "proj":
                    project(*arg)
                elif kind == "headsum":
                    o = begin(st)
                    i = hn_index[arg]
                    pe.wait_ge(hn_in, i + 1)
                    width = NM if arg[0] == "ck" else S
                    end(nc.tensor.matmul(o[:, 0:width], C("blk"), hn_sq[:, i % 2, 0:width], start=True, stop=True))
                elif kind == "score":
                    which, pr, qt, hh = arg
                    o = begin(st)
                    h = 2 * pr + hh
                    if which == "mem":
                        pe.wait_ge(hn_done, 4)
                        end(nc.tensor.matmul(o[:, 0:NM], cqpad[:, h, qt * P:(qt + 1) * P], ckn[:, pr, :], start=True, stop=True))
                    else:
                        pe.wait_ge(hn_done, 8)
                        w_ = P * (qt + 1)
                        end(nc.tensor.matmul(o[:, 0:w_], qpad[:, h, qt * P:(qt + 1) * P], kn[:, pr, 0:w_], start=True, stop=True))
                elif kind == "turn":
                    which, pr, qt, hh = arg
                    u = unit_index[arg]
                    o = begin(st)
                    pe.wait_ge(p_ready, u + 1)
                    for kt in range(MT if which == "mem" else qt + 1):
                        ins = nc.tensor.transpose(o[:, kt * P:(kt + 1) * P], p_sb[:, u % 2, kt * P:(kt + 1) * P], C("ident"))
                    end(ins)
                elif kind == "values":
                    which, pr, qt = arg
                    o = begin(st)
                    nk = MT if which == "mem" else qt + 1
                    if which == "mem":
                        for t in range(MT):
                            taken(pe, ("proj", "cv", t))
                    else:
                        for t in range(qt + 1):
                            taken(pe, ("proj", "mv", t))
                    for hh in range(2):
                        taken(pe, ("turn", which, pr, qt, hh))
                        for kt in range(nk):
                            v = (cvpad if which == "mem" else vpad)[:, kt, 2 * pr + hh, :]
                            ins = nc.tensor.matmul(o[:, 0:P], v, pT[:, hh, kt, :], start=(hh == 0 and kt == 0),
                                                   stop=(hh == 1 and kt == nk - 1))
                    end(ins)
                elif kind == "gate":
                    pr = arg[0]
                    o = begin(st)
                    pe.wait_ge(ld["wgk"], 16)
                    taken(pe, ("proj", "lr", 0))
                    end(nc.tensor.matmul(o, w_gk[0:RANK, pr * P:(pr + 1) * P], lrT[0:RANK, :], start=True, stop=True))
                elif kind == "turn_keys":
                    pr = arg[0]
                    o = begin(st)
                    pe.wait_ge(qk_ready, pr + 1)
                    for t in range(TT):
                        ins = nc.tensor.transpose(o[:, t * P:(t + 1) * P], kend_f[:, t * P:(t + 1) * P], C("ident"))
                    end(ins)
                elif kind == "intra":
                    pr, hh = arg
                    o = begin(st)
                    for t in range(TT):
                        ins = nc.tensor.matmul(o[:, t * P:(t + 1) * P], kinv[:, 2 * pr + hh, t * P:(t + 1) * P],
                                               qdec[:, pr, t * P:(t + 1) * P], start=True, stop=True)
                    end(ins)
                elif kind == "chunk_state":
                    pr, g = arg
                    o = begin(st)
                    taken(pe, ("turn_keys", pr))
                    taken(pe, ("proj", "gv", g))
                    for s_ in range(2):
                        ins = nc.tensor.matmul(o[:, s_ * 256:s_ * 256 + 256], kend[:, s_, g, :],
                                               gv[:, g, pr * 256:pr * 256 + 256], start=True, stop=True)
                    end(ins)
                elif kind == "gla_out":
                    pr, hh = arg
                    o = begin(st)
                    h = 2 * pr + hh
                    taken(pe, ("intra", pr, hh))
                    for t in range(TT):
                        ins = nc.tensor.matmul(o[:, t * P:(t + 1) * P], gv[:, t, h * P:(h + 1) * P], at_sb[:, hh, t, :],
                                               start=True, stop=False, skip_group_check=True)
                        for c in (2 * t, 2 * t + 1):
                            if c:
                                pe.wait_ge(st_done, 14 * pr + 2 * c)
                                ins = nc.tensor.matmul(o[:, c * CH:(c + 1) * CH], state[:, c, hh * P:(hh + 1) * P],
                                                       qdec[:, pr, c * CH:(c + 1) * CH], start=False, stop=True,
                                                       skip_group_check=True)
                    end(ins)
                elif kind == "gla_sum":
                    o = begin(st)
                    taken(pe, ("gla_out", *arg))
                    end(nc.tensor.matmul(o, C("ones"), osq, start=True, stop=True))
                elif kind == "router":
                    o = begin(st)
                    pe.wait_ge(ld["router"], 16)
                    for t in range(TT):
                        for k in range(KD):
                            pe.wait_ge(h_ready, 8 + k + 1)
                            ins = nc.tensor.matmul(o[:, t * 36:(t + 1) * 36], hT[:, k, t * P:(t + 1) * P], w_router[:, k, :],
                                                   start=(k == 0), stop=(k == KD - 1))
                    end(ins)
                elif kind == "turn_h":
                    t, half = arg
                    o = begin(st)
                    for j in range(4):
                        ins = nc.tensor.transpose(o[:, j * P:(j + 1) * P], hT[:, 4 * half + j, t * P:(t + 1) * P], C("ident"))
                    end(ins)
                elif kind == "rank":
                    o = begin(st)
                    pe.wait_ge(r_m, 1)
                    for t in range(TT):
                        for u in range(t + 1):
                            nc.tensor.matmul(o[:, t * 32:(t + 1) * 32], C("before") if u == t else C("ones"), M[:, u, :],
                                             start=(u == 0), stop=(u == t))
                    for u in range(TT):
                        ins = nc.tensor.matmul(o[:, P:P + 32], C("ones"), M[:, u, :], start=(u == 0), stop=(u == TT - 1))
                    end(ins)
                elif kind == "moe":
                    taken(pe, ("rank",))
                    for t in range(TT):
                        for half in range(2):
                            taken(pe, ("turn_h", t, half))
                    pe.wait_ge(std_done, 2)

                    def turn(b, s):
                        pe.sem_inc(passed["pe"], 1)
                        for k in range(KD):
                            ins = nc.tensor.transpose(ps_[:, 4 * b, k * CAP:(k + 1) * CAP], xg[b][0:CAP, k * P:(k + 1) * P],
                                                      C("ident")[0:CAP, 0:CAP])
                        ins.then_inc(s, 1)

                    def gate_up(b, s):
                        for j in range(2):
                            w = slot[2 * b + j][:, :].rearrange("p (k n) -> p k n", k=KD)
                            for f in range(4):
                                for k in range(KD):
                                    ins = nc.tensor.matmul(
                                        ps_[:, 4 * b + 1, j * 256 + f * CAP:j * 256 + (f + 1) * CAP],
                                        w[:, k, f * P:(f + 1) * P], xgT[b][:, k, :], start=(k == 0), stop=(k == KD - 1))
                        ins.then_inc(s, 1)

                    def down(b, s):
                        w = slot[4 + b][:, :].rearrange("p (k n) -> p k n", k=4)
                        for half in range(2):
                            for k in range(4):
                                ins = nc.tensor.matmul(ps_[0:CAP, 4 * b + 2 + half, :], hid[b][:, k, :],
                                                       w[:, k, half * 512:(half + 1) * 512], start=(k == 0), stop=(k == 3))
                        ins.then_inc(s, 1)

                    def pair(i):
                        for b in range(2):
                            pe.wait_ge(m_x[b], 16 * i + 16)
                            free(pe, m_xT[b], i)
                            turn(b, m_turned[b])
                        for b in range(2):
                            pe.wait_ge(m_xT[b], i + 1)
                            free(pe, m_hid[b], i)
                            pe.wait_ge(m_w[2 * b], 16 * i + 16)
                            pe.wait_ge(m_w[2 * b + 1], 16 * i + 16)
                            gate_up(b, m_gu[b])
                        for b in range(2):
                            pe.wait_ge(m_hid[b], i + 1)
                            free(pe, m_y[b], i)
                            pe.wait_ge(m_w[4 + b], 16 * i + 16)
                            down(b, m_down[b])

                    def over(i):
                        pe.wait_ge(o_x, 16 * i + 16)
                        turn(0, o_turned)
                        pe.wait_ge(o_xT, i + 1)
                        pe.wait_ge(o_w, 48 * i + 48)
                        gate_up(0, o_gu)
                        pe.wait_ge(o_hid, i + 1)
                        down(0, o_down)
                        pe.wait_ge(o_st, 16 * i + 16)

                    pairs(pe, pair)
                    for b in range(2):
                        pe.wait_ge(m_y[b], NE // 2)
                    pe.wait_ge(r_dest, 1)
                    n_over = nc.tensor.value_load(over_i[0:1, NOVER:NOVER + 1], min_val=0, max_val=NOVER)
                    overflow(pe, n_over, over)
                elif kind == "turn_y":
                    t, half = arg
                    o = begin(st)
                    pe.wait_ge(y_mixed, t + 1)
                    for j in range(4):
                        ins = nc.tensor.transpose(o[:, j * P:(j + 1) * P],
                                                  yg[2 * t][:, (4 * half + j) * P:(4 * half + j + 1) * P], C("ident"))
                    end(ins)
                elif kind == "lru_gate":
                    which, n = arg
                    o = begin(st)
                    pe.wait_ge(conv_done, n + 1)
                    j = int(which == "i")
                    pe.wait_ge(ld_bd[j], 16 * (n + 1))
                    end(nc.tensor.matmul(o, w_bd[:, j, :], lc[:, n % 2, :], start=True, stop=True))
                elif kind == "stick":
                    for name in jobs[J[("proj", "v2", 15)] - 6:J[("proj", "v2", 15)] + 1]:
                        taken(pe, name)
                    pe.wait_ge(std_done, 3)

                    def scores(h):
                        pr, lo = h // 2, CH * (h % 2)
                        b0 = 3 * (h % 2)
                        if h >= 2:
                            pe.wait_ge(att_done, h - 1)
                        for kt, (c, w_) in enumerate(SEG):
                            o = ps_[:, b0 + c // 512, c % 512:c % 512 + w_]
                            nc.tensor.matmul(o, k2[lo:lo + CH, pr, kt * P:(kt + 1) * P], q2[lo:lo + CH, pr, kt * P:S],
                                             start=(kt != 3), stop=False, skip_group_check=True)
                            ins = nc.tensor.matmul(ps_[:, b0 + c // 512, c % 512:c % 512 + P], C("ident"), C("stickbias"),
                                                   start=False, stop=False, skip_group_check=True)
                        ins.then_inc(z_done, 1)

                    def suffix(h):
                        b0 = 3 * (h % 2)
                        pe.wait_ge(sp_done, h + 1)
                        for jt, (c, w_) in enumerate(SEG):
                            for kt in range(jt, TT):
                                ck_, wk = SEG[kt]
                                o = c + (kt - jt) * P
                                ins = nc.tensor.matmul(ps_[:, b0 + o // 512, o % 512:o % 512 + wk],
                                                       C("negtri") if kt == jt else C("negones"), Lb[h % 2][:, ck_:ck_ + wk],
                                                       start=False, stop=False, skip_group_check=True)
                        ins.then_inc(tri_done, 1)

                    def head_values(h):
                        pr = h // 2
                        pe.wait_ge(att_done, h + 1)
                        if h >= 2:
                            pe.wait_ge(pv_out, h - 1)
                        for kt, (c, w_) in enumerate(SEG):
                            ins = nc.tensor.matmul(ps_[:, 6 + h % 2, kt * P:S], v2[:, kt, pr * P:(pr + 1) * P],
                                                   att[h % 2][:, c:c + w_], start=(kt == 0), stop=(kt == TT - 1),
                                                   skip_group_check=True)
                        ins.then_inc(pv_done, 1)

                    scores(0)
                    scores(1)
                    for h in range(HB + 1):
                        if h < HB:
                            suffix(h)
                        if h >= 1:
                            head_values(h - 1)
                        if h + 2 < HB:
                            scores(h + 2)
                    pe.wait_ge(att_done, HB)
                    pe.wait_ge(pv_out, HB)

        @block.scalar
        def _(act):
            chain = [0]

            def link(ins):
                chain[0] += 1
                ins.then_inc(act_chain, 1)
                act.wait_ge(act_chain, chain[0])

            one, eps = C("one"), C("eps")

            def fn(dst, src, f, **kw):
                return nc.scalar.activation(dst, src, f, **kw)

            act.wait_ge(ld["cst"], 16)
            act.wait_ge(ld["prm"], 16)
            for st in steps:
                kind, arg = st[0], st[1:]
                if kind == "mem_norm":
                    act.wait_ge(mem_sum, 1)
                    fn(std[:, 0:NM], ps_[:, 7, 0:NM], ACT.Sqrt, scale=1.0 / D, bias=eps).then_inc(mem_std, 1)
                    link(fn(lw[0], prm[:, GAINS["lru_lambda_2"][0]:GAINS["lru_lambda_2"][1]], ACT.Abs))
                    fn(lw[1], lw[0], ACT.Exp, scale=-1.0).then_inc(lam_exp, 1)
                    act.wait_ge(ld["x"], 16)
                    for n in range(KD):
                        fn(hT[:, n, :], xT[:, n, :], ACT.Square).then_inc(squared, 1)
                elif kind == "square":
                    norm, n = arg
                    if norm == 5:
                        act.wait_ge(x_new, n + 1)
                    else:
                        taken(act, {1: ("proj", "out", n), 3: ("proj", "out2", n), 4: ("proj", "dn", 3 * KD + n)}[norm])
                    if n == 0:
                        act.wait_ge(std_done, norm)
                        fn(acc, xT[:, n, :], ACT.Square).then_inc(squared, 1)
                    else:
                        if n == 1:
                            norm_used(act, norm)
                        else:
                            act.wait_ge(acc_done, 7 * SQUARED.index(norm) + n - 1)
                        fn(sq, xT[:, n, :], ACT.Square).then_inc(squared, 1)
                elif kind == "y_square":
                    t = arg[0]
                    for half in range(2):
                        taken(act, ("turn_y", t, half))
                    fn(hT[:, :, t * P:(t + 1) * P], xT[:, :, t * P:(t + 1) * P], ACT.Square).then_inc(y_squared, 1)
                elif kind == "norm":
                    norm = arg[0]
                    act.wait_ge(summed, norm + 1)
                    if norm == 0:
                        act.wait_ge(mem_h, 8)
                    if norm == 2:
                        norm_used(act, 2)
                    fn(std, ps_[:, 7, :], ACT.Sqrt, scale=1.0 / D, bias=eps).then_inc(std_done, 1)
                elif kind == "split":
                    s_ = arg[0]
                    if s_ in split_old:
                        finished(act, split_old[s_])
                    for k in range(KD):
                        if s_ == 1:
                            act.wait_ge(yl_done, k + 1)
                        elif s_ == 2:
                            act.wait_ge(pv_out, HB)
                        elif s_ == 3:
                            act.wait_ge(merge_done, k + 1)
                        else:
                            act.wait_ge(tmp_done, KD * {0: 0, 4: 1, 5: 2}[s_] + k + 1)
                        fn(HH[:, k, :], split_src(s_, k), ACT.Copy).then_inc(high_done, 1)
                elif kind == "weights":
                    g = arg[0]
                    _, s_, v_ = panel_at(PANELS2[g // 2])
                    act.wait_ge(s_, v_)
                    if g in STICK_HALVES:
                        act.wait_ge(pv_done, HB)
                    half_free(act, g)
                    fn(WH[g % 2], raw_half(g), ACT.Copy).then_inc(w_high, 1)
                elif kind == "proj":
                    name, n = arg
                    job = st
                    o = None if name in ("out", "bl", "ba", "out2", "dn", "ple") else bank(job)
                    if o is not None:
                        finished(act, job)
                    if name in ("ck", "cq", "mq", "mk"):
                        i = hn_index[arg]
                        w_ = NM if name == "ck" else S
                        if i == 0:
                            act.wait_ge(mem_h, 8)
                        if i >= 2:
                            act.wait_ge(hn_done, i - 1)
                        fn(hn_raw[:, i % 2, 0:w_], o[:, 0:w_], ACT.Copy)
                        link(fn(hn_sq[:, i % 2, 0:w_], o[:, 0:w_], ACT.Square))
                        act.sem_inc(hn_in, 1)
                        act.sem_inc(bank_free[J[job] % JB], 1)
                    elif name in ("cv", "mv"):
                        dst = (cvpad if name == "cv" else vpad)[:, n, :, :]
                        act.wait_ge(zeroed, 3)
                        src = o[:, 0:256].rearrange("p (a b d) -> p a b d", a=2, b=2)
                        d4 = dst.rearrange("p (a b) d -> p a b d", a=2)
                        fn(d4[:, :, 0, 0:CH], src[:, :, 0, :], ACT.Copy)
                        frees(fn(d4[:, :, 1, CH:P], src[:, :, 1, :], ACT.Copy), job)
                    elif name in ("gq", "gk"):
                        frees(fn((gq if name == "gq" else gk)[:, n, :], o, ACT.Copy), job)
                    elif name == "lr":
                        frees(fn(lrT[0:RANK, :], o[0:RANK, :], ACT.Copy), job)
                    elif name == "gv":
                        frees(fn(gv[:, n, :], o, ACT.Copy), job)
                    elif name == "r":
                        act.wait_ge(zeros_stored, 32)
                        frees(fn(rs[:, n, :], o, ACT.Silu), job)
                    elif name == "ux":
                        if n == 0:
                            act.wait_ge(pad_zero, 1)
                        if n >= 2:
                            act.wait_ge(conv_done, n - 1)
                        frees(fn(uxp[:, n % 2, 3:3 + S], o, ACT.Copy), job)
                    elif name == "ug":
                        if n >= 2:
                            act.wait_ge(yl_done, n - 1)
                        elif n == 0:
                            act.wait_ge(lru_done, KD)
                        frees(fn(lt[:, n % 2, :], o, ACT.Gelu_apprx_tanh), job)
                    elif name == "q2":
                        frees(fn(q2[:, n, :], o, ACT.Copy, scale=0.125), job)
                    elif name == "k2":
                        if n == 0:
                            act.wait_ge(yl_done, KD)
                        frees(fn(k2[:, n, :], o, ACT.Copy), job)
                    elif name == "v2":
                        q4, t = n // TT, n % TT
                        if n == 0:
                            act.wait_ge(lru_done, KD)
                        frees(fn(v2[:, t, q4 * 256:q4 * 256 + 256], o[:, 0:256], ACT.Copy), job)
                    elif name in ("gl", "ga"):
                        if name == "gl" and n == 0:
                            act.wait_ge(pv_done, HB)
                        frees(fn(sig[name][:, n, :], o, ACT.Sigmoid), job)
                    elif name == "up":
                        if n >= 2:
                            act.wait_ge(hid_low, n - 1)
                        frees(fn(relu[:, n % 2, :], o, ACT.Relu), job)
                        c = n // KD
                        if c == 0:
                            finished(act, ("proj", "out2", 7))
                        elif c >= 2:
                            finished(act, ("proj", "dn", (c - 2) * KD + 7))
                        act.wait_ge(relu_sq, n + 1)
                        fn(HC[c % 2][0][:, n % KD, :], relu[:, n % 2, :], ACT.Copy).then_inc(hid_high, 1)
                    elif name == "pg":
                        frees(fn(pgs[:, n, :], o, ACT.Sigmoid), job)
                elif kind == "headsum":
                    i = hn_index[arg]
                    w_ = NM if arg[0] == "ck" else S
                    finished(act, st)
                    frees(fn(hn_sq[:, i % 2, 0:w_], bank(st)[:, 0:w_], ACT.Sqrt, scale=1.0 / CH, bias=eps), st)
                elif kind == "softmax":
                    u = unit_index[arg]
                    which, pr, qt, hh = arg
                    act.wait_ge(neg_ready, u + 1)
                    if u >= 2:
                        finished(act, ("turn", *prev_unit(u - 2)))
                    if which == "mem":
                        ins = fn(p_sb[:, u % 2, 0:NM], bank(("score", *arg))[:, 0:NM], ACT.Exp, scale=0.125,
                                 bias=row_neg[:, u % 2:u % 2 + 1], accum_out=row_sum[:, u % 2:u % 2 + 1])
                    else:
                        w_ = P * (qt + 1)
                        ins = fn(p_sb[:, u % 2, 0:w_], s_sb[:, u % 2, 0:w_], ACT.Exp,
                                 bias=row_neg[:, u % 2:u % 2 + 1], accum_out=row_sum[:, u % 2:u % 2 + 1])
                    ins.then_inc(exp_done, 1)
                elif kind == "turn":
                    which, pr, qt, hh = arg
                    finished(act, st)
                    nk = MT if which == "mem" else qt + 1
                    first = unit_index[arg]
                    if first >= 2:
                        pu = prev_unit(2 * (first // 2) - 2)
                        finished(act, ("values", *pu[:3]))
                    frees(fn(pT[:, hh, 0:nk, :], bank(st)[:, 0:nk * P].rearrange("p (k q) -> p k q", q=P), ACT.Copy), st)
                elif kind == "values":
                    which, pr, qt = arg
                    finished(act, st)
                    tile = (6 if which == "mem" else 4) + pr
                    frees(fn(mixT[:, tile, qt * P:(qt + 1) * P], bank(st)[:, 0:P], ACT.Copy), st)
                elif kind == "gate":
                    pr = arg[0]
                    finished(act, st)
                    frees(fn(zb[:, pr, :], bank(st), ACT.Identity, bias=G("b_gla_gk", pr)), st)
                elif kind == "gla_begin":
                    finished(act, ("values", "moba", 1, TT - 1))
                    act.wait_ge(exp_done, 32)
                elif kind == "decay":
                    pr = arg[0]
                    if pr:
                        act.wait_ge(qk_ready, pr)
                    taken(act, ("gate", pr))
                    link(fn(t1, zb[:, pr, :], ACT.Abs))
                    link(fn(t1, t1, ACT.Exp, scale=-1.0))
                    fn(t1, t1, ACT.Ln, bias=one).then_inc(lsig, 1)
                    act.wait_ge(cum_done, 2 * pr + 2)
                    i16 = 1.0 / 16.0
                    fn(ecum, cum, ACT.Exp, scale=i16)
                    fn(einv, cum, ACT.Exp, scale=-i16)
                    fn(eend, t1, ACT.Exp, scale=i16)
                    fn(dec[pr], cum.rearrange("p (c l) -> p c l", l=CH)[:, :, CH - 1], ACT.Exp, scale=i16).then_inc(dec_exp, 1)
                elif kind == "gla_out":
                    h = 2 * arg[0] + arg[1]
                    finished(act, st)
                    if h:
                        act.wait_ge(o_done, h)
                        finished(act, ("gla_sum", (h - 1) // 2, (h - 1) % 2))
                    fn(ogn, bank(st), ACT.Copy)
                    frees(fn(osq, bank(st), ACT.Square), st)
                elif kind == "gla_sum":
                    finished(act, st)
                    frees(fn(ostd, bank(st), ACT.Sqrt, scale=1.0 / P, bias=eps), st)
                elif kind == "turn_h":
                    t, half = arg
                    finished(act, st)
                    frees(fn(htok[:, t, half * 512:half * 512 + 512], bank(st), ACT.Copy), st)
                    if half == 1:
                        taken(act, st)
                        act.dma_start(h_dram[t * P:(t + 1) * P, :], htok[:, t, :]).then_inc(h_stored, 16)
                elif kind == "route":
                    act.wait_ge(r_gd, 1)
                    fn(w4b, w4, ACT.Exp).then_inc(r_exp, 1)
                    act.wait_ge(r_e2in, 1)
                    fn(col[5], col[4], ACT.Exp).then_inc(r_e2, 1)
                elif kind == "moe":
                    def silu(b, s_gu, s_silu, i):
                        act.wait_ge(s_gu, i + 1)
                        fn(sg[b], ps_[:, 4 * b + 1, 0:256].rearrange("p (f c) -> p f c", c=CAP), ACT.Silu).then_inc(s_silu, 1)

                    def rows_out(b, first, s_down, s_y, s_st, i):
                        act.wait_ge(s_down, i + 1)
                        free(act, s_st, 16 * i)
                        fn(yout[b][0:CAP, :], ps_[0:CAP, 4 * b + 2:4 * b + 4, :].rearrange("p a n -> p (a n)"),
                           ACT.Copy).then_inc(s_y, 1)
                        act.wait_ge(s_y, i + 1)
                        act.dma_start(y_dram[bass.ds(first, CAP), :], yout[b][0:CAP, :]).then_inc(s_st, 16)

                    def pair(i):
                        for b in range(2):
                            free(act, m_hid[b], i)
                            silu(b, m_gu[b], m_silu[b], i)
                        for b in range(2):
                            rows_out(b, (2 * i + b) * CAP, m_down[b], m_y[b], m_st[b], i)

                    def over(i):
                        silu(0, o_gu, o_silu, i)
                        rows_out(0, (NE + i) * CAP, o_down, o_y, o_st, i)

                    pairs(act, pair)
                    for b in range(2):
                        act.wait_ge(m_st[b], 16 * (NE // 2))
                    act.wait_ge(r_dest, 1)
                    n_over = nc.scalar.value_load(over_i[0:1, NOVER:NOVER + 1], min_val=0, max_val=NOVER)
                    overflow(act, n_over, over)
                elif kind == "lru_gate":
                    which, n = arg
                    if n >= 2:
                        act.wait_ge(lru_done, n - n % 2)
                    finished(act, st)
                    dst, b_ = (lr_, "b_rgate_2") if which == "r" else (li, "b_igate_2")
                    frees(fn(dst[:, n % 2, :], bank(st), ACT.Sigmoid, bias=G(b_, n)), st)
                elif kind == "lru":
                    g = arg[0]
                    if g == 0:
                        act.wait_ge(lam_done, 1)
                    taken(act, ("lru_gate", "r", 2 * g))
                    taken(act, ("lru_gate", "r", 2 * g + 1))
                    for m in (2 * g, 2 * g + 1):
                        fn(la[:, m % 2, :], lr_[:, m % 2, :], ACT.Exp, scale=nsp8[:, m:m + 1])
                        ins = fn(lt[:, m % 2, :], lr_[:, m % 2, :], ACT.Tanh, scale=sp8[:, m:m + 1])
                    ins.then_inc(lru_exp, 1)
                    act.wait_ge(lru_m2, g + 1)
                    fn(lt, lt, ACT.Sqrt).then_inc(lru_mult, 1)
                elif kind == "stick":
                    finished(act, ("proj", "v2", 15))

                    def softplus(h):
                        act.wait_ge(z_done, h + 1)
                        if h >= 2:
                            act.wait_ge(tri_done, h - 1)
                        link(fn(Lb[h % 2], flat(h), ACT.Abs))
                        link(fn(Lb[h % 2], Lb[h % 2], ACT.Exp, scale=-1.0))
                        fn(Lb[h % 2], Lb[h % 2], ACT.Ln, bias=one).then_inc(sp_log, 1)

                    def weights(h):
                        act.wait_ge(tri_done, h + 1)
                        if h >= 2:
                            act.wait_ge(pv_done, h - 1)
                        fn(att[h % 2], flat(h), ACT.Exp).then_inc(att_done, 1)

                    softplus(0)
                    softplus(1)
                    for h in range(HB):
                        weights(h)
                        if h + 2 < HB:
                            softplus(h + 2)

        @block.vector
        def _(dve):
            chain = [0]

            def link(ins):
                chain[0] += 1
                ins.then_inc(dve_chain, 1)
                dve.wait_ge(dve_chain, chain[0])

            v = nc.vector
            dve.wait_ge(ld["cst"], 16)
            dve.wait_ge(ld["prm"], 16)
            lam = prm[:, GAINS["lru_lambda_2"][0]:GAINS["lru_lambda_2"][1]]
            dve.wait_ge(ld["mem"], 16)
            v.tensor_tensor(memh, memT, memT, ALU.mult).then_inc(mem_sq, 1)
            dve.wait_ge(lam_exp, 1)
            link(v.tensor_scalar(lw[2], lw[1], 2.0, None, ALU.add))
            link(v.reciprocal(lw[2], lw[2]))
            link(v.tensor_tensor(lw[3], lw[1], lw[2], ALU.mult))
            link(v.tensor_tensor(lw[4], lw[3], lw[3], ALU.mult))
            link(v.tensor_scalar(lw[5], lw[4], 1.0 / 17, 1.0 / 15, ALU.mult, ALU.add))
            for d in (13, 11, 9, 7, 5, 3, 1):
                link(v.tensor_tensor(lw[5], lw[5], lw[4], ALU.mult))
                link(v.tensor_scalar(lw[5], lw[5], 1.0 / d, None, ALU.add))
            link(v.scalar_tensor_tensor(out=lw[5], in0=lw[5], scalar=2.0, in1=lw[3], op0=ALU.mult, op1=ALU.mult))
            link(v.tensor_scalar(lw[0], lam, -1.0, 0.0, ALU.mult, ALU.max))
            link(v.tensor_tensor(lw[5], lw[5], lw[0], ALU.add))
            v.tensor_scalar(nsp8, lw[5], -8.0, None, ALU.mult)
            v.tensor_scalar(sp8, lw[5], 8.0, None, ALU.mult).then_inc(lam_done, 1)

            def add_x(n, job):
                finished(dve, job)
                frees(v.tensor_tensor(xT[:, n, :], bank(job), xT[:, n, :], ALU.add), job)

            def low_part(s_, k):
                dve.wait_ge(high_done, KD * s_ + k + 1)
                v.tensor_tensor(HL[:, k, :], split_src(s_, k), HH[:, k, :].bitcast(F32), ALU.subtract).then_inc(low_done, 1)

            def pick_first(dst, cond, first, tmp, mx):
                link(v.tensor_tensor(tmp, cond, first, ALU.mult))
                link(v.tensor_reduce(mx, tmp, AX, ALU.max))
                link(v.tensor_tensor(dst, tmp, mx.unsqueeze(2).to_broadcast(list(tmp.shape)), ALU.is_equal))

            def rows(x):
                return x.unsqueeze(1).to_broadcast([P, TT, x.shape[1]])

            def each(x, n):
                return x.unsqueeze(2).to_broadcast([P, x.shape[1], n])

            for st in steps:
                kind, arg = st[0], st[1:]
                if kind == "mem_norm":
                    dve.wait_ge(mem_std, 1)
                    link(v.reciprocal(std[:, 0:NM], std[:, 0:NM]))
                    for k in range(KD):
                        v.scalar_tensor_tensor(out=memh[:, k, :], in0=memT[:, k, :], scalar=G("mem_norm_g", k),
                                               in1=std[:, 0:NM], op0=ALU.mult, op1=ALU.mult).then_inc(mem_h, 1)
                elif kind == "norm":
                    norm = arg[0]
                    gain = ["attn_norm_g", "ffn_norm_g", "norm_mix_g_2", "norm_mlp_g_2", "norm_ple_g_2",
                            "norm_final_g_2"][norm]
                    if norm in (1, 5):
                        finished(dve, ("proj", "r", 3) if norm == 1 else ("proj", "pg", 7))
                    dve.wait_ge(std_done, norm + 1)
                    link(v.reciprocal(std, std))
                    if norm in (2, 3, 4):
                        low = {2: 0, 3: 4, 4: 5}[norm]

                        def normed(k):
                            if k >= 4:
                                dve.wait_ge(low_done, KD * low + k - 3)
                            v.scalar_tensor_tensor(out=tmp[:, k % 4, :], in0=xT[:, k, :], scalar=G(gain, k), in1=std,
                                                   op0=ALU.mult, op1=ALU.mult).then_inc(tmp_done, 1)

                        for k in range(KD + 2):
                            if k < KD:
                                normed(k)
                            if k >= 2:
                                low_part(low, k - 2)
                        if norm == 2:
                            v.memset(uxp[:, :, 0:3], 0.0).then_inc(pad_zero, 1)
                        continue
                    for k in range(KD):
                        v.scalar_tensor_tensor(out=hT[:, k, :], in0=xT[:, k, :], scalar=G(gain, k), in1=std,
                                               op0=ALU.mult, op1=ALU.mult).then_inc(h_ready, 1)
                elif kind == "split":
                    if arg[0] in (1, 2, 3):
                        for k in range(KD):
                            low_part(arg[0], k)
                elif kind == "weights":
                    g = arg[0]
                    dve.wait_ge(w_high, g + 1)
                    v.tensor_tensor(WL[g % 2], raw_half(g), WH[g % 2].bitcast(F32), ALU.subtract).then_inc(w_low, 1)
                elif kind == "square":
                    norm, n = arg
                    if n:
                        dve.wait_ge(squared, 8 + 8 * SQUARED.index(norm) + n + 1)
                        v.tensor_tensor(acc, acc, sq, ALU.add).then_inc(acc_done, 1)
                elif kind == "proj":
                    name, n = arg
                    if name == "dn":
                        add_x(n % KD, st)
                    elif name in ("out", "out2"):
                        add_x(n, st)
                    elif name == "ug":
                        taken(dve, st)
                        v.tensor_tensor(yl[:, n, :], yl[:, n, :], lt[:, n % 2, :], ALU.mult).then_inc(yl_done, 1)
                    elif name in ("bl", "ba"):
                        sg_ = sig["gl" if name == "bl" else "ga"][:, n, :]
                        taken(dve, ("proj", "gl" if name == "bl" else "ga", n))
                        finished(dve, st)
                        if name == "bl":
                            frees(v.tensor_tensor(merged[:, n, :], bank(st), sg_, ALU.mult), st)
                        else:
                            if n:
                                dve.wait_ge(merge_done, n)
                            frees(v.tensor_tensor(prod["ba"], bank(st), sg_, ALU.mult), st)
                            taken(dve, st)
                            v.tensor_tensor(merged[:, n, :], merged[:, n, :], prod["ba"], ALU.add).then_inc(merge_done, 1)
                    elif name == "up":
                        taken(dve, st)
                        v.tensor_tensor(relu[:, n % 2, :], relu[:, n % 2, :], relu[:, n % 2, :], ALU.mult).then_inc(relu_sq, 1)
                        dve.wait_ge(hid_high, n + 1)
                        high, low = HC[n // KD % 2]
                        v.tensor_tensor(low[:, n % KD, :], relu[:, n % 2, :], high[:, n % KD, :].bitcast(F32),
                                        ALU.subtract).then_inc(hid_low, 1)
                    elif name == "ple":
                        taken(dve, ("proj", "pg", n))
                        finished(dve, st)
                        if n:
                            dve.wait_ge(x_new, n)
                        frees(v.tensor_tensor(prod["ple"], bank(st), pgs[:, n, :], ALU.mult), st)
                        taken(dve, st)
                        v.tensor_tensor(xT[:, n, :], xT[:, n, :], prod["ple"], ALU.add).then_inc(x_new, 1)
                elif kind == "headsum":
                    name, n = arg
                    i = hn_index[arg]
                    w_ = NM if name == "ck" else S
                    taken(dve, st)
                    dve.wait_ge(hn_in, i + 1)
                    dve.wait_ge(zeroed, 3)
                    inv = hn_sq[:, i % 2, 0:w_]
                    link(v.reciprocal(inv, inv))
                    gain = G({"mq": "moba_q_norm_g", "mk": "moba_k_norm_g", "cq": "mem_q_norm_g", "ck": "mem_k_norm_g"}[name])
                    parts = [(0, P, {"mk": kn, "ck": ckn}[name][:, n, :])] if name in ("mk", "ck") else [
                        (lo, lo + CH, {"mq": qpad, "cq": cqpad}[name][lo:lo + CH, 2 * n + lo // CH, :]) for lo in (0, CH)]
                    for lo, hi, dst in parts:
                        ins = v.scalar_tensor_tensor(out=dst, in0=hn_raw[lo:hi, i % 2, 0:w_], scalar=gain[lo:hi, :],
                                                     in1=hn_sq[lo:hi, i % 2, 0:w_], op0=ALU.mult, op1=ALU.mult)
                    ins.then_inc(hn_done, 1)
                elif kind == "softmax":
                    u = unit_index[arg]
                    which, pr, qt, hh = arg
                    j = u % 2
                    h = 2 * pr + hh
                    finished(dve, ("score", *arg))
                    if u >= 2:
                        dve.wait_ge(exp_done, u - 1)
                    o = bank(("score", *arg))
                    if which == "mem":
                        w_ = NM
                        link(v.tensor_reduce(row_max[:, j:j + 1], o[:, 0:w_], AX, ALU.max))
                        v.tensor_scalar(row_neg[:, j:j + 1], row_max[:, j:j + 1], -0.125, None, ALU.mult).then_inc(neg_ready, 1)
                    else:
                        w_ = P * (qt + 1)
                        link(v.tensor_scalar(slope_b[:, 0:w_], C("alibi")[:, S - w_:S], 2.0 ** (-2 * (h + 1)), None, ALU.mult))
                        link(v.scalar_tensor_tensor(out=s_sb[:, j, 0:w_], in0=o[:, 0:w_], scalar=0.125,
                                                    in1=slope_b[:, 0:w_], op0=ALU.mult, op1=ALU.add))
                        link(v.tensor_reduce(row_max[:, j:j + 1], s_sb[:, j, 0:w_], AX, ALU.max))
                        v.tensor_scalar(row_neg[:, j:j + 1], row_max[:, j:j + 1], -1.0, None, ALU.mult).then_inc(neg_ready, 1)
                    dve.wait_ge(exp_done, u + 1)
                    dve.sem_inc(bank_free[J[("score", *arg)] % JB], 1)
                    link(v.reciprocal(row_inv[:, j:j + 1], row_sum[:, j:j + 1]))
                    v.tensor_scalar(p_sb[:, j, 0:w_], p_sb[:, j, 0:w_], row_inv[:, j:j + 1], None, ALU.mult).then_inc(p_ready, 1)
                elif kind == "gla_begin":
                    finished(dve, ("values", "moba", 1, TT - 1))
                    dve.wait_ge(state_zero, 1)
                elif kind == "decay":
                    pr = arg[0]
                    for nm in ("gq", "gk"):
                        taken(dve, ("proj", nm, pr))
                    dve.wait_ge(lsig, pr + 1)
                    if pr:
                        dve.wait_ge(dec_exp, pr)
                    link(v.scalar_tensor_tensor(out=t1, in0=zb[:, pr, :], scalar=0.0, in1=t1, op0=ALU.min, op1=ALU.subtract))
                    v.tensor_tensor_scan(cum, C("reset"), t1, 0.0, ALU.mult, ALU.add).then_inc(cum_done, 1)
                    dve.wait_ge(cum_done, 2 * pr + 1)
                    c3 = cum.rearrange("p (c l) -> p c l", l=CH)
                    v.tensor_tensor(t1.rearrange("p (c l) -> p c l", l=CH), c3[:, :, CH - 1:CH].to_broadcast([P, 8, CH]), c3,
                                    ALU.subtract).then_inc(cum_done, 1)
                    dve.wait_ge(dec_exp, pr + 1)
                    if pr:
                        finished(dve, ("turn_keys", pr - 1))
                    v.scalar_tensor_tensor(out=qdec[:, pr, :], in0=gq[:, pr, :], scalar=0.125, in1=ecum, op0=ALU.mult, op1=ALU.mult)
                    for lo in (0, CH):
                        v.tensor_tensor(kinv[lo:lo + CH, 2 * pr + lo // CH, :], gk[lo:lo + CH, pr, :], einv[lo:lo + CH, :], ALU.mult)
                    v.tensor_tensor(kend_f, gk[:, pr, :], eend, ALU.mult).then_inc(qk_ready, 1)
                elif kind == "turn_keys":
                    pr = arg[0]
                    finished(dve, st)
                    if pr:
                        finished(dve, ("chunk_state", pr - 1, 3))
                    for s_ in range(2):
                        ins = v.tensor_scalar(kend[:, s_, :, :], bank(st).rearrange("p (t f) -> p t f", t=TT),
                                              C("half")[:, s_:s_ + 1], None, ALU.mult)
                    frees(ins, st)
                elif kind == "intra":
                    pr, hh = arg
                    finished(dve, st)
                    if pr:
                        finished(dve, ("gla_out", pr - 1, hh))
                    frees(v.tensor_tensor(at_sb[:, hh, :, :], bank(st).rearrange("p (t f) -> p t f", t=TT),
                                          C("chunkmask").unsqueeze(1).to_broadcast([P, TT, P]), ALU.mult), st)
                elif kind == "chunk_state":
                    pr, g = arg
                    finished(dve, st)
                    if pr and g == 0:
                        finished(dve, ("gla_out", pr - 1, 1))
                    for s_ in range(2):
                        c = 2 * g + s_
                        if c == 7:
                            break
                        if c:
                            dve.wait_ge(st_done, 14 * pr + 2 * c)
                        for lo in (0, CH):
                            cs = slice(lo // CH * P, lo // CH * P + P)
                            d_ = state[lo:lo + CH, c + 1, cs]
                            u_ = bank(st)[lo:lo + CH, s_ * 256 + cs.start:s_ * 256 + cs.stop]
                            if c == 0:
                                v.tensor_copy(d_, u_).then_inc(st_done, 1)
                            else:
                                v.scalar_tensor_tensor(out=d_, in0=state[lo:lo + CH, c, cs], scalar=dec[pr][lo:lo + CH, c:c + 1],
                                                       in1=u_, op0=ALU.mult, op1=ALU.add).then_inc(st_done, 1)
                    dve.wait_ge(st_done, 14 * pr + 2 * min(2 * g + 2, 7))
                    dve.sem_inc(bank_free[J[st] % JB], 1)
                elif kind == "gla_sum":
                    h = 2 * arg[0] + arg[1]
                    taken(dve, st)
                    link(v.reciprocal(ostd, ostd))
                    link(v.scalar_tensor_tensor(out=ogn, in0=ogn, scalar=G("gla_out_norm_g"), in1=ostd, op0=ALU.mult, op1=ALU.mult))
                    taken(dve, ("proj", "r", h))
                    v.tensor_tensor(mixT[:, h, :], ogn, rs[:, h, :], ALU.mult).then_inc(o_done, 1)
                    dve.wait_ge(o_done, h + 1)
                elif kind == "router":
                    finished(dve, st)
                    lo, hi = GAINS["router_bias"]
                    frees(v.tensor_tensor(lg, bank(st)[:, 0:TT * 36].rearrange("p (t n) -> p t n", t=TT),
                                          rows(prm[:, lo:hi]), ALU.add), st)
                    taken(dve, st)
                elif kind == "route":
                    link(v.tensor_reduce(col[0], lg[:, :, 0:4], AX, ALU.max))
                    v.tensor_tensor(w4, lg[:, :, 0:4], each(col[0], 4), ALU.subtract).then_inc(r_gd, 1)
                    dve.wait_ge(r_exp, 1)
                    link(v.tensor_reduce(col[1], w4b, AX, ALU.add))
                    link(v.reciprocal(col[1], col[1]))
                    link(v.tensor_scalar(w4, w4, 0.0, None, ALU.is_ge))
                    pick_first(w4b, w4, rows(C("first4")), w4, col[2])
                    link(v.tensor_scalar(w4b, w4b, -1.0, BIG, ALU.add, ALU.mult))
                    link(v.tensor_tensor(wk32.rearrange("p t (g e) -> p t g e", g=4),
                                         lg[:, :, 4:36].rearrange("p t (g e) -> p t g e", g=4),
                                         w4b.unsqueeze(3).to_broadcast([P, TT, 4, 8]), ALU.add))
                    for k in range(2):
                        link(v.tensor_reduce(col[2 + k], wk32, AX, ALU.max))
                        link(v.tensor_tensor(wk32b, wk32, each(col[2 + k], 32), ALU.is_ge))
                        pick_first(oh[k], wk32b, rows(C("first32")), wk32b, col[6])
                        if k == 0:
                            link(v.scalar_tensor_tensor(out=wk32, in0=oh[0], scalar=-100.0 * BIG, in1=wk32, op0=ALU.mult, op1=ALU.add))
                    v.tensor_tensor(M, oh[0], oh[1], ALU.add).then_inc(r_m, 1)
                    v.tensor_tensor(col[4], col[3], col[2], ALU.subtract).then_inc(r_e2in, 1)
                    dve.wait_ge(r_e2, 1)
                    link(v.tensor_scalar(col[7], col[5], 1.0, None, ALU.add))
                    link(v.reciprocal(col[7], col[7]))
                    link(v.tensor_tensor(gate_w[:, 0, :], col[7], col[1], ALU.mult))
                    link(v.tensor_tensor(gate_w[:, 1, :], gate_w[:, 0, :], col[5], ALU.mult))
                elif kind == "place":
                    rk = ("rank",)
                    finished(dve, rk)
                    o = bank(rk)
                    link(v.tensor_copy(cnt, o[:, P:P + 32]))
                    link(v.tensor_tensor(cmp, cnt.unsqueeze(2).to_broadcast([P, 32, 7]),
                                         C("thresholds").unsqueeze(1).to_broadcast([P, 32, 7]), ALU.is_gt))
                    link(v.tensor_reduce(nb, cmp, AX, ALU.add))
                    link(v.tensor_tensor_scan(obend, C("ones")[:, 0:32], nb, 0.0, ALU.mult, ALU.add))
                    link(v.tensor_tensor(dd, obend, nb, ALU.subtract))
                    link(v.tensor_tensor(dd, dd, C("expert"), ALU.subtract))
                    link(v.tensor_scalar(dd, dd, float(CAP), float((NE - 1) * CAP), ALU.mult, ALU.add))
                    rank = o[:, 0:P].rearrange("p (t e) -> p t e", t=TT)
                    link(v.tensor_scalar(wk32, rank, float(CAP), None, ALU.is_ge))
                    link(v.tensor_tensor(wk32, wk32, rows(dd), ALU.mult))
                    link(v.tensor_tensor(wk32, wk32, rank, ALU.add))
                    link(v.tensor_scalar(dd, C("expert"), float(CAP), None, ALU.mult))
                    link(v.tensor_tensor(dest, wk32, rows(dd), ALU.add))
                    for k in range(2):
                        link(v.tensor_tensor(wk32, dest, oh[k], ALU.mult))
                        link(v.tensor_reduce(col[8 + k], wk32, AX, ALU.add))
                        link(v.tensor_copy(dest_i[:, k * TT:(k + 1) * TT], col[8 + k]))
                    link(v.tensor_tensor(cmp2, obend.unsqueeze(1).to_broadcast([P, NOVER, 32]),
                                         C("overblock").unsqueeze(2).to_broadcast([P, NOVER, 32]), ALU.is_le))
                    link(v.tensor_reduce(otab, cmp2, AX, ALU.add))
                    link(v.tensor_scalar(otab, otab, float(NE - 1), None, ALU.min))
                    link(v.tensor_copy(over_i[:, 0:NOVER], otab))
                    link(v.tensor_copy(over_i[:, NOVER:NOVER + 1], obend[:, 31:32]))
                    dve.sem_inc(r_dest, 1)
                    dve.sem_inc(bank_free[J[rk] % JB], 1)
                elif kind == "moe":
                    def rows_in(b, s_turned, s_xT, i):
                        dve.wait_ge(s_turned, i + 1)
                        v.tensor_copy(xgT[b], ps_[:, 4 * b, :].rearrange("p (k c) -> p k c", k=KD)).then_inc(s_xT, 1)

                    def gated(b, s_silu, s_hid, i):
                        dve.wait_ge(s_silu, i + 1)
                        v.tensor_tensor(hid[b], ps_[:, 4 * b + 1, 256:512].rearrange("p (f c) -> p f c", c=CAP), sg[b],
                                        ALU.mult).then_inc(s_hid, 1)

                    def pair(i):
                        for b in range(2):
                            free(dve, m_gu[b], i)
                            rows_in(b, m_turned[b], m_xT[b], i)
                        for b in range(2):
                            free(dve, m_down[b], i)
                            gated(b, m_silu[b], m_hid[b], i)

                    def over(i):
                        free(dve, o_st, 16 * i)
                        rows_in(0, o_turned, o_xT, i)
                        gated(0, o_silu, o_hid, i)

                    pairs(dve, pair)
                    for b in range(2):
                        dve.wait_ge(m_st[b], 16 * (NE // 2))
                    n_over = nc.vector.value_load(over_i[0:1, NOVER:NOVER + 1], min_val=0, max_val=NOVER)
                    overflow(dve, n_over, over)
                    for t in range(TT):
                        dve.wait_ge(y_got[t], 32)
                        link(v.tensor_scalar(yg[2 * t], yg[2 * t], gate_w[:, 0, t:t + 1], None, ALU.mult))
                        v.scalar_tensor_tensor(out=yg[2 * t], in0=yg[2 * t + 1], scalar=gate_w[:, 1, t:t + 1], in1=yg[2 * t],
                                               op0=ALU.mult, op1=ALU.add).then_inc(y_mixed, 1)
                elif kind == "turn_y":
                    t, half = arg
                    finished(dve, st)
                    xs = xT[:, 4 * half:4 * half + 4, t * P:(t + 1) * P]
                    frees(v.tensor_tensor(xs, bank(st).rearrange("p (k q) -> p k q", q=P), xs, ALU.add), st)
                elif kind == "conv":
                    g = arg[0]
                    for m in (2 * g, 2 * g + 1):
                        taken(dve, ("proj", "ux", m))
                        dve.wait_ge(pad_zero, 1)
                        c_, u_ = lc[:, m % 2, :], uxp[:, m % 2, :]
                        link(v.tensor_scalar(c_, u_[:, 3:3 + S], G("conv_w_2", 24 + m), G("conv_b_2", m), ALU.mult, ALU.add))
                        for tap in (2, 1, 0):
                            ins = v.scalar_tensor_tensor(out=c_, in0=u_[:, tap:tap + S], scalar=G("conv_w_2", 8 * tap + m), in1=c_,
                                                         op0=ALU.mult, op1=ALU.add)
                            if tap:
                                link(ins)
                        ins.then_inc(conv_done, 1)
                elif kind == "lru":
                    g = arg[0]
                    dve.wait_ge(lru_exp, g + 1)
                    taken(dve, ("lru_gate", "i", 2 * g))
                    taken(dve, ("lru_gate", "i", 2 * g + 1))
                    dve.wait_ge(conv_done, 2 * g + 2)
                    link(v.tensor_scalar(lr_, lt, 1.0, None, ALU.add))
                    link(v.reciprocal(lr_, lr_))
                    v.scalar_tensor_tensor(out=lt, in0=lt, scalar=2.0, in1=lr_, op0=ALU.mult, op1=ALU.mult).then_inc(lru_m2, 1)
                    link(v.tensor_tensor(li, li, lc, ALU.mult))
                    dve.wait_ge(lru_mult, g + 1)
                    link(v.tensor_tensor(lt, lt, li, ALU.mult))
                    for m in (2 * g, 2 * g + 1):
                        v.tensor_tensor_scan(yl[:, m, :], la[:, m % 2, :], lt[:, m % 2, :], 0.0, ALU.mult, ALU.add).then_inc(lru_done, 1)
                    dve.wait_ge(lru_done, 2 * g + 2)
                elif kind == "stick":
                    def log_sum(h):
                        dve.wait_ge(sp_log, h + 1)
                        v.scalar_tensor_tensor(out=Lb[h % 2], in0=flat(h), scalar=0.0, in1=Lb[h % 2], op0=ALU.max,
                                               op1=ALU.add).then_inc(sp_done, 1)

                    dve.wait_ge(yl_done, KD)
                    log_sum(0)
                    log_sum(1)
                    for h in range(HB + 1):
                        if h >= 1:
                            lo = CH * ((h - 1) % 2)
                            dve.wait_ge(pv_done, h)
                            v.tensor_copy(q2[lo:lo + CH, (h - 1) // 2, :], ps_[lo:lo + CH, 6 + (h - 1) % 2, :]).then_inc(pv_out, 1)
                        if h + 2 < HB:
                            log_sum(h + 2)


def constants():
    c = np.zeros((P, NCONST), np.float32)

    def put(name, x):
        lo, hi = CONST[name]
        c[:, lo:hi] = x

    r, q = np.arange(P)[:, None], np.arange(P)[None, :]
    put("ident", r == q)
    put("ones", 1)
    put("blk", r // 64 == q // 64)
    put("before", r < q)
    put("chunkmask", (r // CH == q // CH) & (r <= q))
    put("negtri", -1.0 * (r >= q))
    put("negones", -1)
    put("stickbias", np.where(r >= q, -BIG, 0))
    dist = r + (S - P) - np.arange(S)[None, :]
    put("alibi", np.where(dist >= 0, -dist, -BIG))
    put("reset", (np.arange(S) % CH != 0)[None, :])
    put("half", np.arange(P)[:, None] // CH == np.arange(2)[None, :])
    put("thresholds", CAP * np.arange(1, 8)[None, :])
    put("first32", 32 - np.arange(32)[None, :])
    put("first4", 4 - np.arange(4)[None, :])
    put("expert", np.arange(32)[None, :])
    put("overblock", np.arange(NOVER)[None, :])
    put("token", np.arange(TT)[None, :] * P + r)
    put("eps", EPS)
    put("one", 1)
    return c


def gains(x):
    g = np.zeros((P, NGAIN), np.float32)
    for name, (lo, hi) in GAINS.items():
        if name == "router_bias":
            g[:, lo:hi] = np.concatenate([x["b_router_group"][0], x["b_router_expert"][0].reshape(-1)])[None, :]
            continue
        w = np.asarray(x[name]).reshape(-1)
        if w.size == 64:
            w = np.concatenate([w, w])
        g[:, lo:hi] = w.reshape(hi - lo, P).T
    return g


BIGS = ["w_in", "w_gla_gk", "w_mem_kv", "w_out", "w_gate", "w_up", "w_down", "w_in_2", "w_br_lru_2", "w_br_att_2",
        "w_out_2", "w_mlp_up_2", "w_mlp_down_2", "w_ple_gate_2", "w_ple_2"]


def kernel(**inputs):
    import concourse.bacc as bacc
    from concourse.bass_utils import run_bass_kernel_spmd

    x = {k: np.asarray(v) for k, v in inputs.items()}
    arrays = {k: np.ascontiguousarray(x[k]) for k in BIGS}
    arrays["xT"] = np.ascontiguousarray(x["x"][0].T)
    arrays["memT"] = np.ascontiguousarray(x["mem"][0].T)
    arrays["pT"] = np.ascontiguousarray(x["p_2"][0, 0].T)
    arrays["consts"] = constants()
    arrays["gains"] = gains(x)
    router = np.concatenate([x["w_router_group"][0], x["w_router_expert"][0].transpose(1, 0, 2).reshape(D, 32)], axis=1)
    arrays["w_router"] = np.ascontiguousarray(router.reshape(KD, P, 36).transpose(1, 0, 2))
    blocks = np.zeros((2 * KD, P, P), np.float32)
    for j, name in enumerate(("w_rgate_2", "w_igate_2")):
        for n in range(2 * KD):
            lo = 64 * (n % 2)
            blocks[2 * (n // 2) + j, lo:lo + 64, lo:lo + 64] = x[name][0, n]
    arrays["gate_blocks"] = blocks
    nc = bacc.Bacc("TRN2", target_bir_lowering=False, num_devices=1)
    a = {k: nc.dram_tensor(k, v.shape, mybir.dt.from_np(v.dtype), kind="ExternalInput").ap() for k, v in arrays.items()}
    out = nc.dram_tensor("outT", (D, S), F32, kind="ExternalOutput").ap()
    build(nc, a, out)
    r = run_bass_kernel_spmd(nc, [arrays], core_ids=[0])
    return np.ascontiguousarray(r.results[0]["outT"].T)[None]
```

```python
from contextlib import ExitStack

import concourse.bass as bass
from concourse import mybir
import numpy as np

F32 = mybir.dt.float32
F32R = mybir.dt.float32r
BF16 = mybir.dt.bfloat16
I32 = mybir.dt.int32
ALU = mybir.AluOpType
ACT = mybir.ActivationFunctionType
AX = mybir.AxisListType.X

P = 128
S = 512
D = 1024
KD = D // P
TT = S // P
NM = 256
MT = NM // P
PAN = KD * 512
RANK = 16
CH = 64
NE, FF = 32, 512
CAP = 64
NOVER = 2 * S // CAP - 1
NROWS = (NE + NOVER) * CAP
EPS = 1e-6
BIG = 1e30
JB = 7
HB = 16


def columns(widths):
    at, out = 0, {}
    for name, w in widths:
        out[name] = (at, at + w)
        at += w
    return out, at


CONST, NCONST = columns([
    ("ident", P), ("ones", P), ("blk", P), ("before", P), ("chunkmask", P), ("negtri", P), ("negones", P),
    ("stickbias", P), ("alibi", S), ("reset", S), ("half", 2), ("thresholds", 7), ("first32", 32), ("first4", 4),
    ("expert", 32), ("overblock", NOVER), ("column", P), ("eps", 1), ("one", 1)])

GAINS, NGAIN = columns([
    ("attn_norm_g", 8), ("mem_norm_g", 8), ("ffn_norm_g", 8), ("norm_mix_g_2", 8), ("norm_mlp_g_2", 8),
    ("norm_ple_g_2", 8), ("norm_final_g_2", 8), ("b_gla_gk", 2), ("gla_out_norm_g", 1), ("moba_q_norm_g", 1),
    ("moba_k_norm_g", 1), ("mem_q_norm_g", 1), ("mem_k_norm_g", 1), ("conv_w_2", 32), ("conv_b_2", 8),
    ("b_rgate_2", 8), ("b_igate_2", 8), ("lru_lambda_2", 8), ("router_bias", 36)])


def plan():
    steps, jobs = [], []

    def step(kind, *args):
        steps.append((kind, *args))

    def job(kind, *args):
        jobs.append((kind, *args))
        steps.append((kind, *args))

    def attention(which, fill):
        units = [(which, pr, qt, hh) for pr in range(2) for qt in range(TT) for hh in range(2)]
        fill = list(fill)
        for u in range(len(units) + 3):
            if u < len(units):
                job("score", *units[u])
            if u >= 3 and (u - 3) % 2 == 1:
                job("values", *units[u - 3][:3])
            if 2 <= u < len(units) + 2:
                job("turn", *units[u - 2])
            if fill and u % 2 == 0:
                for f in fill.pop(0):
                    emit(f)
            if u < len(units):
                step("softmax", *units[u])
        if (len(units) - 1) % 2 == 1 and ("values", *units[-1][:3]) not in jobs:
            job("values", *units[-1][:3])
        for fs in fill:
            for f in fs:
                emit(f)

    def emit(f):
        (step if f[0] in STEPS_ONLY else job)(*f)
        if f[0] == "proj" and f[1] in ("mq", "mk", "cq", "ck"):
            job("headsum", f[1], f[2])

    step("mem_norm")
    step("norm", 0)
    for n in range(2):
        emit(("proj", "ck", n))
    for n in range(MT):
        emit(("proj", "cv", n))
    for n in range(2):
        emit(("proj", "cq", n))
    attention("mem", [[("proj", "mv", t)] for t in range(TT)] + [[("proj", "mq", n)] for n in range(2)]
              + [[("proj", "mk", n)] for n in range(2)])
    attention("moba", [[("proj", "gq", 0)], [("proj", "gq", 1)], [("proj", "gk", 0)], [("proj", "gk", 1)],
                       [("proj", "lr", 0), ("gate", 0), ("gate", 1)]] + [[("proj", "gv", t)] for t in range(TT)])
    step("gla_begin")
    step("decay", 0)
    job("proj", "r", 0)
    job("proj", "r", 1)
    for pr in range(2):
        job("turn_keys", pr)
        for hh in range(2):
            job("intra", pr, hh)
        for g in range(4):
            job("chunk_state", pr, g)
        if pr == 0:
            job("proj", "r", 2)
            job("proj", "r", 3)
        for hh in range(2):
            job("gla_out", pr, hh)
            job("gla_sum", pr, hh)
        if pr == 0:
            step("decay", 1)
    for n in range(KD):
        job("proj", "out", n)
        step("square", 1, n)
    step("norm", 1)
    job("router")
    for t in range(TT):
        for half in range(2):
            job("turn_h", t, half)
    step("route")
    job("rank")
    step("place")
    step("moe")
    for t in range(TT):
        for half in range(2):
            job("turn_y", t, half)
        if t:
            step("y_square", t - 1)
    step("weights", 0)
    step("y_square", TT - 1)
    step("norm", 2)
    step("split", 0)

    halves = [(name, h) for name in PANELS2[:-1] for h in range(2)]
    ahead = [1]

    def half_jobs(g):
        name, h = halves[g]
        while ahead[0] <= min(g + 1, len(halves) - 1):
            if ahead[0] > g and name == "v21" and h == 1:
                break
            step("weights", ahead[0])
            ahead[0] += 1
        base, n = name[:-1], int(name[-1])
        if base == "v2":
            return [("proj", "v2", (2 * n + h) * TT + t) for t in range(TT)]
        return [("proj", base, 4 * n + 2 * h + j) for j in range(2)]

    for g, (name, h) in enumerate(halves):
        if (name, h) == ("gl0", 0):
            step("stick")
        if (name, h) == ("bl0", 0):
            step("split", 1)
        if (name, h) == ("ba0", 0):
            step("split", 2)
        if (name, h) == ("out20", 0):
            step("split", 3)
        if (name, h) == ("up0", 0):
            step("norm", 3)
            step("split", 4)
        if (name, h) == ("pg0", 0):
            step("norm", 4)
            step("split", 5)
        for jb in half_jobs(g):
            job(*jb)
            n = jb[2]
            if jb[1] in ("ux", "ug"):
                pair = n // 2 - 1 + (4 if jb[1] == "ug" else 0)
                if 0 <= pair < 4:
                    if n % 2 == 0:
                        for m in (2 * pair, 2 * pair + 1):
                            job("lru_gate", "r", m)
                            job("lru_gate", "i", m)
                    elif jb[1] == "ug":
                        step("lru", pair)
                if jb[1] == "ux" and n % 2:
                    step("conv", n // 2)
                    if pair >= 0:
                        step("lru", pair)
            if jb[1] == "out2":
                step("square", 3, n)
            if jb[1] == "dn" and n >= 3 * KD:
                step("square", 4, n - 3 * KD)
    for n in range(KD):
        job("proj", "ple", n)
        step("square", 5, n)
    step("norm", 5)
    return steps, jobs


SQUARED = (1, 3, 4, 5)
STICK_HALVES = (20, 21)
STEPS_ONLY = ("softmax",)
PHASE2 = ("ux", "ug", "q2", "k2", "v2", "gl", "ga", "bl", "ba", "out2", "up", "dn", "pg")

PANELS1 = ["memkv", "mvcq", "mqk", "gqk", "gv", "r", "out0", "out1"]
PANELS2 = ["ux0", "ux1", "ug0", "ug1", "q20", "q21", "k20", "k21", "v20", "v21", "gl0", "gl1", "ga0", "ga1",
           "bl0", "bl1", "ba0", "ba1", "out20", "out21", "up0", "up1", "up2", "up3", "dn0", "dn1", "up4", "up5",
           "dn2", "dn3", "up6", "up7", "dn4", "dn5", "dn6", "dn7", "pg0", "pg1", "ple"]
SLOTS1, SLOTS2 = 4, 3
SPLITS = ("mixed input", "lru", "attention", "merged", "mlp input", "ple input")
NORM_SPLITS = tuple(SPLITS.index(x) for x in ("mixed input", "mlp input", "ple input"))


def build(nc, a, out):
    steps, jobs = plan()
    J = {name: n for n, name in enumerate(jobs)}
    hn_index = {n[1:]: i for i, n in enumerate(x for x in jobs if x[0] == "headsum")}
    unit_index = {n[1:]: i for i, n in enumerate(x for x in steps if x[0] == "softmax")}

    with ExitStack() as ctx:
        def sb(name, n, dt=F32):
            return ctx.enter_context(nc.sbuf_tensor("sb_" + name, [P, n], dt))

        def sem(name):
            return ctx.enter_context(nc.semaphore(name))

        def dram(name, shape, dt):
            return nc.dram_tensor(name, shape, dt, kind="Internal").ap()

        slot = [sb(f"slot{i}", PAN) for i in range(3)]
        xT_ = sb("xT", KD * S)
        F = sb("F", 1024)
        cst = sb("cst", NCONST)
        prm = sb("prm", NGAIN)
        small = sb("small", 288)
        table_i = sb("table_i", 32, I32)
        with ExitStack() as first:
            def fb(name, n):
                return first.enter_context(nc.sbuf_tensor("sb_" + name, [P, n], F32))

            slot += [fb(f"slot{i}", PAN) for i in range(3, 6)]
            hT_ = fb("hT", KD * S)
            R = fb("R", 4 * KD * S)
        WP = sb("w_parts", 2 * PAN, F32R)
        HH_, HL_ = sb("h_high", KD * S, F32R), sb("h_low", KD * S, F32R)
        HC_ = [[sb(f"hidden_{part}{i}", KD * S, F32R) for part in ("high", "low")] for i in range(2)]
        ps_ = ctx.enter_context(nc.psum_tensor("ps", [P, 8, 512], F32))

        def C(name):
            lo, hi = CONST[name]
            return cst[:, lo:hi]

        def G(name, i=0):
            lo = GAINS[name][0] + i
            return prm[:, lo:lo + 1]

        def view(t, at, *dims):
            n = int(np.prod(dims))
            v = t[:, at:at + n]
            if len(dims) == 2:
                return v.rearrange("p (a b) -> p a b", a=dims[0])
            if len(dims) == 3:
                return v.rearrange("p (a b c) -> p a b c", a=dims[0], b=dims[1])
            return v

        xT, hT = view(xT_, 0, KD, S), view(hT_, 0, KD, S)
        acc = view(F, 0, S)
        sq = view(F, 512, S)
        std = view(F, 512, S)
        mixT = view(R, 0, KD, S)
        qpad = view(R, 4096, 4, S)
        kn = view(R, 6144, 2, S)
        vpad = view(R, 7168, TT, 4, P)
        cqpad = view(R, 9216, 4, S)
        ckn = view(R, 11264, 2, NM)
        cvpad = view(R, 11776, MT, 4, P)
        s_sb = view(R, 13312, 2, S)
        p_sb = view(R, 14336, 2, S)
        pT = view(R, 15360, 2, TT, P)
        memT = view(slot[5], 0, KD, NM)
        memh = view(slot[5], 2048, KD, NM)
        hn_raw = view(slot[5], 0, 2, S)
        hn_sq = view(slot[5], 1024, 2, S)
        gq = view(slot[4], 0, 2, S)
        gk = view(slot[4], 1024, 2, S)
        lrT = view(slot[4], 2048, S)
        zb = view(slot[4], 2560, 2, S)
        slope_b = view(slot[4], 3584, S)
        gv = view(R, 9216, TT, S)
        rs = view(R, 11264, 4, S)
        t1 = view(R, 4096, S)
        cum = view(R, 4608, S)
        ecum = view(R, 5120, S)
        einv = view(R, 5632, S)
        eend = view(R, 6144, S)
        kend_f = view(R, 6656, S)
        kend = view(R, 7168, 2, TT, P)
        osq = view(R, 8192, S)
        ogn = view(R, 8704, S)
        qdec = view(R, 13312, 2, S)
        ostd = view(R, 14336, S)
        at_sb = view(R, 14848, 2, TT, P)
        kinv = view(slot[5], 0, 4, S)
        state = view(slot[5], 2048, 8, 2 * P)
        htok = view(R, 0, TT, D)
        chosen, chosen2 = (view(R, 4096 + 512 * i, TT, P) for i in range(2))
        yout = view(R, 6144, D)
        xgT = view(R, 7168, KD, 2 * CAP)
        sg, hid = view(R, 8192, FF), view(R, 8704, FF)
        hidT = view(R, 9216, FF // P, 2 * CAP)
        lg = view(R, 10240, TT, 36)
        wk32 = view(R, 10400, TT, 32)
        wk32b = view(R, 10528, TT, 32)
        oh = [view(R, 10656 + 128 * k, TT, 32) for k in range(2)]
        M = view(R, 10912, TT, 32)
        dest = view(R, 11040, TT, 32)
        w4 = view(R, 11168, TT, 4)
        w4b = view(R, 11184, TT, 4)
        w4c, w4e = (view(R, 12096 + 16 * i, TT, 4) for i in range(2))
        row = view(R, 12128, 2, TT)
        cmp = view(R, 11200, 32, 7)
        cmp2 = view(R, 11424, NOVER, 32)
        cnt, nb, obend, dd = (view(R, 11904 + 32 * i, 32) for i in range(4))
        otab = view(R, 12032, NOVER)
        w_router = view(R, 9728, KD, 36)
        col = [view(R, 12144 + 4 * i, TT) for i in range(8)]
        gate_slots = [slot[0], slot[1], hT_[:, :], R[:, 12288:16384]]
        gate_w = view(small, 0, 2, TT)
        dest_i = table_i[:, 0:8]
        over_i = table_i[:, 12:12 + NOVER + 1]
        yg = [view(R, 1024 * i, D) for i in range(2 * TT)]
        q2, k2, v2, yl = (view(R, 4096 * i, KD, S) for i in range(4))
        v2 = view(R, 8192, TT, D)
        lc = view(R, 8192, 4, S)
        lr_, li, la, lt, gel = (view(R, at, 2, S) for at in (0, 1024, 10240, 5136, 6160))
        uxp = view(R, 4096, 2, S + 4)
        w_bd = view(R, 2048, KD, 2, P)
        sp8 = view(small, 16, KD)
        nsp8 = view(small, 24, KD)
        lw = [view(small, 32 + 8 * i, KD) for i in range(6)]
        row_max, row_neg, row_sum, row_inv = (view(small, 96 + 2 * i, 2) for i in range(4))
        dec = [view(small, 112 + 8 * i, 8) for i in range(2)]
        w_lr = view(R, 0, KD * RANK)
        w_gk = view(R, 128, 2 * P)
        SEG = [(0, 512), (512, 384), (1024, 256), (896, 128)]
        WH = [view(WP, PAN // 2 * i, KD, 256) for i in range(2)]
        WL = [view(WP, PAN + PAN // 2 * i, KD, 256) for i in range(2)]
        Lb = [view(slot[3], 1280 * i, 1280) for i in range(2)]
        Llow = [WP[:, 1280 * i:1280 * i + 1280] for i in range(2)]
        Lhigh = [WP[:, 2560 + 1280 * i:3840 + 1280 * i] for i in range(2)]
        att = [view(slot[4], 5120 - PAN + 1280 * i, 1280) for i in range(2)]
        tri_r, ones_r = WP[:, 7680:7808], WP[:, 7808:7936]
        ident_b, bias_b = (slot[4][:, 7936 - PAN + 64 * i:8000 - PAN + 64 * i].bitcast(BF16) for i in range(2))
        HH, HL = (w[:, :].rearrange("p (k n) -> p k n", k=KD) for w in (HH_, HL_))
        HC = [[w[:, :].rearrange("p (k n) -> p k n", k=KD) for w in pair] for pair in HC_]
        tmp = view(R, 8192, KD, S)
        relu = view(F, 0, 2, S)
        sig = {"gl": view(R, 4096, KD, S), "ga": view(R, 8192, KD, S)}
        merged = yl
        prod = {"ba": view(F, 0, S), "ple": view(R, 5120, S)}
        pgs = view(R, 0, KD, S)
        pT2 = view(R, 4096, 2, S)

        y_dram = dram("y_rows", (NROWS, D), F32)

        pe_done = sem("pe_done")
        bank_free = [sem(f"bank_free{b}") for b in range(JB)]
        ld = {n: sem(f"ld_{n}") for n in ("cst", "prm", "mem", "x", "wlr", "wgk", "router", "p", "blocks")}
        pan1 = [sem(f"pan1_{i}") for i in range(SLOTS1)]
        pan2 = [sem(f"pan2_{i}") for i in range(SLOTS2)]
        act_chain, dve_chain = sem("act_chain"), sem("dve_chain")
        mem_sq, mem_sum, mem_std, mem_h = sem("mem_sq"), sem("mem_sum"), sem("mem_std"), sem("mem_h")
        squared, summed, std_done, h_ready = sem("squared"), sem("summed"), sem("std_done"), sem("h_ready")
        x_new, acc_done, tmp_done = sem("x_new"), sem("acc_done"), sem("tmp_done")
        high_done, low_done, low_first, w_high, w_low = sem("high_done"), sem("low_done"), sem("low_first"), sem("w_high"), sem("w_low")
        relu_sq, hid_high, hid_low = sem("relu_sq"), sem("hid_high"), sem("hid_low")
        zeroed = sem("zeroed")
        hn_in, hn_std, hn_done = sem("hn_in"), sem("hn_std"), sem("hn_done")
        neg_ready, exp_done, p_ready = sem("neg_ready"), sem("exp_done"), sem("p_ready")
        state_zero = sem("state_zero")
        lsig, cum_done, dec_exp, qk_ready = sem("lsig"), sem("cum_done"), sem("dec_exp"), sem("qk_ready")
        st_done = sem("st_done")
        o_done = sem("o_done")
        r_exp, r_gd, r_m, r_dest = sem("r_exp"), sem("r_gd"), sem("r_m"), sem("r_dest")
        r_e2in, r_e2 = sem("r_e2in"), sem("r_e2")
        zeros_set, zeros_stored = sem("zeros_set"), sem("zeros_stored")
        m_gate_w, m_w = [sem(f"m_gate_w{i}") for i in range(4)], [sem(f"m_w{i}") for i in range(2, 6)]
        FLOW = ("equal", "chosen", "row", "x", "xT", "gate", "up", "silu", "hid", "hturned", "hidT", "down", "y", "st")
        m_ = {n: sem("m_" + n) for n in FLOW}
        o_ = {n: sem("o_" + n) for n in FLOW}
        o_w = sem("o_w")
        y_squared = sem("y_squared")
        y_got, y_mixed = [sem(f"y_got{t}") for t in range(TT)], sem("y_mixed")
        pad_zero, conv_done, lru_exp, lru_m2, lru_mult, lru_done = (
            sem(n) for n in ("pad_zero", "conv_done", "lru_exp", "lru_m2", "lru_mult", "lru_done"))
        lam_exp, lam_done = sem("lam_exp"), sem("lam_done")
        gelu_done, yl_done = sem("gelu_done"), sem("yl_done")
        z_done, sp_log, sp_done, sp_low, stick_set, tri_done, att_done, pv_done, pv_out = (
            sem(n) for n in ("z_done", "sp_log", "sp_done", "sp_low", "stick_set", "tri_done", "att_done", "pv_done", "pv_out"))
        merge_done = sem("merge_done")
        stored = sem("stored")
        passed = {e: sem(f"passed_{e}") for e in ("pool", "pe", "sp")}

        def bank(name):
            return ps_[:, J[name] % JB, :]

        def finished(eng, name):
            eng.wait_ge(pe_done, J[name] + 1)

        def taken(eng, name):
            eng.wait_ge(bank_free[J[name] % JB], J[name] // JB + 1)

        def frees(ins, name):
            return ins.then_inc(bank_free[J[name] % JB], 1)

        w_in, w_in2 = a["w_in"], a["w_in_2"]

        def panel_src(name):
            def cols(w, lo):
                return w[0, :, lo:lo + 512].rearrange("(k p) n -> p k n", p=P)
            if name == "memkv":
                return cols(a["w_mem_kv"], 0)
            if name in ("gqk", "gv", "r", "mqk", "mvcq"):
                return cols(w_in, {"gqk": 0, "gv": 512, "r": 1024, "mqk": 1552, "mvcq": 2064}[name])
            if name in ("out0", "out1"):
                return cols(a["w_out"], 512 * int(name[-1]))
            base, n = name[:-1], name[-1]
            if base in ("ux", "ug", "q2", "k2", "v2", "gl", "ga"):
                return cols(w_in2, ["ux", "ug", "q2", "k2", "v2", "gl", "ga"].index(base) * D + 512 * int(n))
            if base in ("bl", "ba", "out2", "up", "pg"):
                w = a[{"bl": "w_br_lru_2", "ba": "w_br_att_2", "out2": "w_out_2", "up": "w_mlp_up_2",
                       "pg": "w_ple_gate_2"}[base]]
                return cols(w, 512 * int(n))
            if base == "dn":
                c, half = int(n) // 2, int(n) % 2
                return a["w_mlp_down_2"][0, D * c:D * c + D, 512 * half:512 * half + 512].rearrange(
                    "(k p) n -> p k n", p=P)
            return a["w_ple_2"][0].rearrange("(k p) n -> p k n", p=P)

        def where(name, n):
            if name in ("ck", "cv"):
                return "memkv", (0 if name == "ck" else 256)
            if name in ("cq", "mv"):
                return "mvcq", (256 if name == "cq" else 0)
            if name in ("mq", "mk"):
                return "mqk", (0 if name == "mq" else 256)
            if name in ("gq", "gk"):
                return "gqk", (0 if name == "gq" else 256)
            if name in ("gv", "r"):
                return name, 0
            if name == "out":
                return f"{name}{n // 4}", 0
            return name, 0

        def last_use(panel):
            return next(nm for nm in reversed(jobs) if nm[0] == "proj" and nm[1] not in PHASE2 + ("lr",)
                        and where(nm[1], nm[2])[0] == panel)

        def half_of(name, n):
            p, h = (n // 8, n // 4 % 2) if name == "v2" else (n // 4, n % 4 // 2)
            return 2 * PANELS2.index(f"{name}{p}") + h

        half_last = {}
        for nm in jobs:
            if nm[0] == "proj" and nm[1] in PHASE2:
                half_last[half_of(*nm[1:])] = nm

        def half_free(eng, g):
            if g >= 2:
                finished(eng, half_last[g - 2])

        def split_src(s, k):
            return {1: yl, 2: q2, 3: merged}[s][:, k, :] if s in (1, 2, 3) else tmp[:, k, :]

        split_old = {1: ("proj", "ga", 7), 2: ("proj", "bl", 7), 3: ("proj", "ba", 7), 4: ("proj", "out2", 7),
                     5: ("proj", "up", 31)}

        def low_ready(eng, s, k):
            if s in NORM_SPLITS and k < 4:
                eng.wait_ge(low_first, 4 * NORM_SPLITS.index(s) + k + 1)
            else:
                before = 8 * s - 4 * sum(x < s for x in NORM_SPLITS)
                eng.wait_ge(low_done, before + (k - 4 if s in NORM_SPLITS else k) + 1)

        def norm_used(eng, norm):
            if norm <= 2:
                eng.wait_ge(h_ready, 8 * norm)
            else:
                eng.wait_ge(tmp_done, 8 * (norm - 2))

        def panel_at(name):
            if name in PANELS1:
                n = PANELS1.index(name)
                return slot[n % SLOTS1], pan1[n % SLOTS1], 16 * (n // SLOTS1 + 1)
            n = PANELS2.index(name)
            return slot[n % SLOTS2], pan2[n % SLOTS2], 16 * (n // SLOTS2 + 1)

        def raw_half(g):
            t = panel_at(PANELS2[g // 2])[0][:, :].rearrange("p (k n) -> p k n", k=KD)
            return t[:, :, 256 * (g % 2):256 * (g % 2) + 256]

        def expert_src(name, e):
            w = a[name][0, e]
            return w.rearrange("(k p) n -> p k n", p=P)

        def pairs(eng, body):
            body(0)
            with eng.Fori(1, NE // 4) as i:
                body(i)

        def overflow(eng, n_over, body):
            with eng.If(n_over > 0):
                body(0)
                with eng.Fori(1, NOVER) as i:
                    with eng.If(i < n_over):
                        body(i)

        def free(eng, s, v):
            if type(v) is not int or v > 0:
                eng.wait_ge(s, v)

        def prev_unit(u):
            return next(n for n, i in unit_index.items() if i == u)

        def flat(h):
            b0 = 3 * (h % 2)
            return ps_[:, b0:b0 + 3, :].rearrange("p a b -> p (a b)")[:, 0:1280]

        block = ctx.enter_context(nc.Block())

        @block.sync
        def _(sp):
            def load(dst, src, s):
                sp.dma_start(dst, src).then_inc(s, 16)

            load(cst[:, :], a["consts"], ld["cst"])
            load(prm[:, :], a["gains"], ld["prm"])
            load(memT, a["memT"].rearrange("(k p) n -> p k n", p=P), ld["mem"])
            load(slot[0][:, :].rearrange("p (k n) -> p k n", k=KD), panel_src("memkv"), pan1[0])
            load(xT, a["xT"].rearrange("(k p) n -> p k n", p=P), ld["x"])
            load(w_lr.rearrange("p (k n) -> p k n", k=KD),
                 w_in[0, :, 1536:1536 + RANK].rearrange("(k p) n -> p k n", p=P), ld["wlr"])
            load(w_gk[0:RANK, :], a["w_gla_gk"][0], ld["wgk"])
            for n, name in enumerate(PANELS1):
                if n == 0:
                    continue
                if n >= SLOTS1:
                    finished(sp, last_use(PANELS1[n - SLOTS1]))
                load(slot[n % SLOTS1][:, :].rearrange("p (k n) -> p k n", k=KD), panel_src(name), pan1[n % SLOTS1])

            def pair_load(n, part, odd=0):
                for b in range(2):
                    src = expert_src(("w_gate", "w_up", "w_down")[part], 2 * n + b)
                    if part == 0:
                        dst, s = gate_slots[2 * odd + b], m_gate_w[2 * odd + b]
                    else:
                        dst, s = slot[2 * part + b], m_w[2 * part - 2 + b]
                    load(dst[:, :].rearrange("p (k n) -> p k n", k=(KD, KD, 4)[part]), src, s)

            def up_down_load(n):
                for part, used in ((1, "up"), (2, "down")):
                    sp.wait_ge(m_[used], n)
                    pair_load(n, part)

            finished(sp, ("gla_sum", 1, 1))
            sp.wait_ge(st_done, 14 * 2)
            sp.wait_ge(qk_ready, 2)
            load(w_router, a["w_router"], ld["router"])
            pair_load(0, 2)
            for part in range(2):
                for n in (4 + 2 * part, 5 + 2 * part):
                    finished(sp, last_use(PANELS1[n]))
                pair_load(0, part)
            finished(sp, ("turn_h", TT - 1, 1))
            pair_load(1, 0, 1)
            with sp.Fori(0, NE // 4 - 1) as i:
                for odd in (1, 0):
                    n = 2 * i + 2 - odd
                    up_down_load(n)
                    sp.wait_ge(m_["gate"], n)
                    pair_load(n + 1, 0, 1 - odd)
            up_down_load(NE // 2 - 1)
            for used in ("gate", "up", "down"):
                sp.wait_ge(m_[used], NE // 2)
            sp.wait_ge(r_dest, 1)
            n_over = sp.value_load(over_i[0:1, NOVER:NOVER + 1], min_val=0, max_val=NOVER)

            def over_load(i):
                e = sp.value_load(over_i[0:1, bass.ds(i, 1)], min_val=0, max_val=NE - 1)
                for part, name in enumerate(("w_gate", "w_up", "w_down")):
                    load(slot[2 * part][:, :].rearrange("p (k n) -> p k n", k=(KD, KD, 4)[part]), expert_src(name, e), o_w)
                sp.wait_ge(o_["st"], 16 * i + 16)
                sp.sem_inc(passed["sp"], 1)

            overflow(sp, n_over, over_load)
            for t in range(TT):
                sp.wait_ge(y_got[t], 32)
            for n, name in enumerate(PANELS2):
                if n >= SLOTS2:
                    sp.wait_ge(w_low, 2 * (n - SLOTS2) + 2)
                dst = slot[n % SLOTS2]
                if name == "ple":
                    finished(sp, ("proj", "dn", 31))
                    load(pT2, a["pT"].rearrange("(k p) n -> p k n", p=P), ld["p"])
                    load(dst[:, 0:2 * D].rearrange("p (k n) -> p k n", k=2), panel_src(name), pan2[n % SLOTS2])
                else:
                    load(dst[:, :].rearrange("p (k n) -> p k n", k=KD), panel_src(name), pan2[n % SLOTS2])
            for k in range(KD):
                sp.wait_ge(h_ready, 8 * 2 + k + 1)
                sp.dma_start(out[k * P:(k + 1) * P, :], hT[:, k, :]).then_inc(stored, 16)
            sp.wait_ge(stored, 16 * KD)

        @block.gpsimd
        def _(pool):
            nc.gpsimd.memset(R[:, 4096:6144], 0.0).then_inc(zeroed, 1)
            nc.gpsimd.memset(R[:, 7168:11264], 0.0).then_inc(zeroed, 1)
            nc.gpsimd.memset(R[:, 11776:12800], 0.0).then_inc(zeroed, 1)
            nc.gpsimd.memset(R[:, 12800:13312], 0.0).then_inc(zeros_set, 1)
            pool.wait_ge(zeros_set, 1)
            zp = NOVER * CAP // 8
            pool.dma_start(y_dram[NE * CAP:NROWS, :].rearrange("(z r) (c n) -> z (r c) n", z=zp, c=2),
                           R[0:zp, 12800:13312].unsqueeze(1).to_broadcast([zp, 16, 512])).then_inc(zeros_stored, 16)
            finished(pool, ("values", "moba", 1, TT - 1))
            pool.wait_ge(hn_done, 8)
            nc.gpsimd.memset(slot[5][:, :], 0.0).then_inc(state_zero, 1)
            pool.wait_ge(r_dest, 1)
            pool.wait_ge(m_["st"], 16 * (NE // 2))
            n_over = nc.gpsimd.value_load(over_i[0:1, NOVER:NOVER + 1], min_val=0, max_val=NOVER)

            def over_stored(i):
                pool.wait_ge(o_["st"], 16 * i + 16)
                pool.sem_inc(passed["pool"], 1)

            overflow(pool, n_over, over_stored)
            for t in range(TT):
                for k in range(2):
                    nc.gpsimd.indirect_dma_start(
                        yg[2 * t + k], None, y_dram,
                        bass.IndirectOffsetOnAxis(ap=dest_i[:, k * TT + t:k * TT + t + 1], axis=0)
                    ).then_inc(y_got[t], 16)
            finished(pool, ("turn_y", TT - 1, 1))
            pool.dma_start(w_bd.rearrange("p n j c -> p (n j) c"), a["gate_blocks"].rearrange("m p c -> p m c")
                           ).then_inc(ld["blocks"], 16)
            for st in steps:
                if st[0] == "stick":
                    for h in range(HB):
                        pool.wait_ge(sp_done, h + 1)
                        for c, w_ in ((0, 896), (1024, 256)):
                            ins = nc.gpsimd.tensor_tensor(Llow[h % 2][:, c:c + w_], Lb[h % 2][:, c:c + w_],
                                                          Lhigh[h % 2][:, c:c + w_].bitcast(F32), ALU.subtract)
                        ins.then_inc(sp_low, 1)
                if st[0] == "split" and st[1] in NORM_SPLITS:
                    for k in range(4):
                        pool.wait_ge(high_done, KD * st[1] + k + 1)
                        nc.gpsimd.tensor_tensor(HL[:, k, :], split_src(st[1], k), HH[:, k, :].bitcast(F32),
                                                ALU.subtract).then_inc(low_first, 1)
                if st[0] == "weights":
                    g = st[1]
                    pool.wait_ge(w_high, g + 1)
                    nc.gpsimd.tensor_tensor(WL[g % 2], raw_half(g), WH[g % 2].bitcast(F32), ALU.subtract).then_inc(w_low, 1)

        @block.tensor
        def _(pe):
            def begin(name):
                n = J[name]
                if n >= JB:
                    pe.wait_ge(bank_free[n % JB], n // JB)
                return bank(name)

            def end(ins):
                ins.then_inc(pe_done, 1)

            def panel(name):
                t, s, v = panel_at(name)
                pe.wait_ge(s, v)
                return t[:, :].rearrange("p (k n) -> p k n", k=KD)

            tok_major = ("mv", "cv", "gv")

            def project2(name, n):
                o = begin(("proj", name, n))
                g = half_of(name, n)
                if name == "dn":
                    c = n // KD
                    high, low = HC[c % 2]
                else:
                    s = {"bl": 1, "ba": 2, "out2": 3, "up": 4, "pg": 5}.get(name, 0)
                    high, low = HH, HL
                for i, (w, h) in enumerate(((WH, high), (WL, high), (WH, low))):
                    if i < 2:
                        pe.wait_ge(w_low if i else w_high, g + 1)
                    for k in range(KD):
                        if i != 1:
                            if name == "dn":
                                pe.wait_ge(hid_low if i else hid_high, c * KD + k + 1)
                            else:
                                low_ready(pe, s, k) if i else pe.wait_ge(high_done, KD * s + k + 1)
                        first, last = i == 0 and k == 0, i == 2 and k == KD - 1
                        if name == "v2":
                            t = n % TT
                            ins = nc.tensor.matmul(o[:, 0:256], h[:, k, t * P:(t + 1) * P], w[g % 2][:, k, :], start=first, stop=last)
                        else:
                            ins = nc.tensor.matmul(o, w[g % 2][:, k, n % 2 * P:(n % 2 + 1) * P], h[:, k, :], start=first, stop=last)
                end(ins)

            def project(name, n):
                if name in PHASE2:
                    return project2(name, n)
                o = begin(("proj", name, n))
                if name == "lr":
                    pe.wait_ge(ld["wlr"], 16)
                    w = w_lr.rearrange("p (k n) -> p k n", k=KD)
                    for k in range(KD):
                        ins = nc.tensor.matmul(o[0:RANK, :], w[:, k, :], hT[:, k, :], start=(k == 0), stop=(k == KD - 1))
                    end(ins)
                    return
                pn, off = where(name, n)
                w = panel(pn)
                if name == "ple":
                    w = panel_at(pn)[0][:, 0:2 * D].rearrange("p (k n) -> p k n", k=2)
                    pe.wait_ge(ld["p"], 16)
                    for k in range(2):
                        ins = nc.tensor.matmul(o, w[:, k, n * P:(n + 1) * P], pT2[:, k, :], start=(k == 0), stop=(k == 1))
                    end(ins)
                    return
                src = hT
                if name in ("ck", "cv"):
                    src = memh
                elif name == "out":
                    src = mixT
                for k in range(KD):
                    if name in ("ck", "cv"):
                        pe.wait_ge(mem_h, k + 1)
                    elif name == "out" and k < 4:
                        pe.wait_ge(o_done, k + 1)
                    elif name == "out":
                        if k == 4 and n == 0:
                            for w_ in ("mem", "moba"):
                                for pr in range(2):
                                    for qt in range(TT):
                                        taken(pe, ("values", w_, pr, qt))
                    elif name != "out":
                        pe.wait_ge(h_ready, k + 1)
                    if name in tok_major:
                        t = n % TT
                        width = {"mv": 256, "cv": 256, "gv": 512}[name]
                        ins = nc.tensor.matmul(o[:, 0:width], src[:, k, t * P:(t + 1) * P], w[:, k, off:off + width],
                                               start=(k == 0), stop=(k == KD - 1))
                    else:
                        c = off + (n % 4) * P
                        width = NM if name == "ck" else S
                        ins = nc.tensor.matmul(o[:, 0:width], w[:, k, c:c + P], src[:, k, :],
                                               start=(k == 0), stop=(k == KD - 1))
                end(ins)

            def norm_sum(norm):
                pe.wait_ge(std_done, norm)
                pe.wait_ge(acc_done, 7 * SQUARED.index(norm) + 7)
                nc.tensor.matmul(ps_[:, 7, :], C("ones"), acc, start=True, stop=True).then_inc(summed, 1)

            for st in steps:
                kind, arg = st[0], st[1:]
                if kind == "mem_norm":
                    pe.wait_ge(ld["cst"], 16)
                    pe.wait_ge(mem_sq, 1)
                    for k in range(KD):
                        ins = nc.tensor.matmul(ps_[:, 7, 0:NM], C("ones"), memh[:, k, :], start=(k == 0), stop=(k == KD - 1))
                    ins.then_inc(mem_sum, 1)
                elif kind == "norm":
                    norm = arg[0]
                    if norm == 0:
                        pe.wait_ge(mem_std, 1)
                        for n in range(KD):
                            pe.wait_ge(squared, n + 1)
                            ins = nc.tensor.matmul(ps_[:, 7, :], C("ones"), hT[:, n, :], start=(n == 0), stop=(n == KD - 1))
                        ins.then_inc(summed, 1)
                    elif norm != 2:
                        norm_sum(norm)
                elif kind == "y_square":
                    t = arg[0]
                    pe.wait_ge(std_done, 2)
                    pe.wait_ge(y_squared, t + 1)
                    for k in range(KD):
                        ins = nc.tensor.matmul(ps_[:, 7, t * P:(t + 1) * P], C("ones"), hT[:, k, t * P:(t + 1) * P],
                                               start=(k == 0), stop=(k == KD - 1))
                    if t == TT - 1:
                        ins.then_inc(summed, 1)
                elif kind == "proj":
                    project(*arg)
                elif kind == "headsum":
                    o = begin(st)
                    i = hn_index[arg]
                    pe.wait_ge(hn_in, i + 1)
                    width = NM if arg[0] == "ck" else S
                    end(nc.tensor.matmul(o[:, 0:width], C("blk"), hn_sq[:, i % 2, 0:width], start=True, stop=True))
                elif kind == "score":
                    which, pr, qt, hh = arg
                    o = begin(st)
                    h = 2 * pr + hh
                    if which == "mem":
                        pe.wait_ge(hn_done, 4)
                        end(nc.tensor.matmul(o[:, 0:NM], cqpad[:, h, qt * P:(qt + 1) * P], ckn[:, pr, :], start=True, stop=True))
                    else:
                        pe.wait_ge(hn_done, 8)
                        w_ = P * (qt + 1)
                        end(nc.tensor.matmul(o[:, 0:w_], qpad[:, h, qt * P:(qt + 1) * P], kn[:, pr, 0:w_], start=True, stop=True))
                elif kind == "turn":
                    which, pr, qt, hh = arg
                    u = unit_index[arg]
                    o = begin(st)
                    pe.wait_ge(p_ready, u + 1)
                    for kt in range(MT if which == "mem" else qt + 1):
                        ins = nc.tensor.transpose(o[:, kt * P:(kt + 1) * P], p_sb[:, u % 2, kt * P:(kt + 1) * P], C("ident"))
                    end(ins)
                elif kind == "values":
                    which, pr, qt = arg
                    o = begin(st)
                    nk = MT if which == "mem" else qt + 1
                    if which == "mem":
                        for t in range(MT):
                            taken(pe, ("proj", "cv", t))
                    else:
                        for t in range(qt + 1):
                            taken(pe, ("proj", "mv", t))
                    for hh in range(2):
                        taken(pe, ("turn", which, pr, qt, hh))
                        for kt in range(nk):
                            v = (cvpad if which == "mem" else vpad)[:, kt, 2 * pr + hh, :]
                            ins = nc.tensor.matmul(o[:, 0:P], v, pT[:, hh, kt, :], start=(hh == 0 and kt == 0),
                                                   stop=(hh == 1 and kt == nk - 1))
                    end(ins)
                elif kind == "gate":
                    pr = arg[0]
                    o = begin(st)
                    pe.wait_ge(ld["wgk"], 16)
                    taken(pe, ("proj", "lr", 0))
                    end(nc.tensor.matmul(o, w_gk[0:RANK, pr * P:(pr + 1) * P], lrT[0:RANK, :], start=True, stop=True))
                elif kind == "turn_keys":
                    pr = arg[0]
                    o = begin(st)
                    pe.wait_ge(qk_ready, pr + 1)
                    for t in range(TT):
                        ins = nc.tensor.transpose(o[:, t * P:(t + 1) * P], kend_f[:, t * P:(t + 1) * P], C("ident"))
                    end(ins)
                elif kind == "intra":
                    pr, hh = arg
                    o = begin(st)
                    for t in range(TT):
                        ins = nc.tensor.matmul(o[:, t * P:(t + 1) * P], kinv[:, 2 * pr + hh, t * P:(t + 1) * P],
                                               qdec[:, pr, t * P:(t + 1) * P], start=True, stop=True)
                    end(ins)
                elif kind == "chunk_state":
                    pr, g = arg
                    o = begin(st)
                    taken(pe, ("turn_keys", pr))
                    taken(pe, ("proj", "gv", g))
                    for s_ in range(2):
                        ins = nc.tensor.matmul(o[:, s_ * 256:s_ * 256 + 256], kend[:, s_, g, :],
                                               gv[:, g, pr * 256:pr * 256 + 256], start=True, stop=True)
                    end(ins)
                elif kind == "gla_out":
                    pr, hh = arg
                    o = begin(st)
                    h = 2 * pr + hh
                    taken(pe, ("intra", pr, hh))
                    for t in range(TT):
                        ins = nc.tensor.matmul(o[:, t * P:(t + 1) * P], gv[:, t, h * P:(h + 1) * P], at_sb[:, hh, t, :],
                                               start=True, stop=False, skip_group_check=True)
                        for c in (2 * t, 2 * t + 1):
                            if c:
                                pe.wait_ge(st_done, 14 * pr + 2 * c)
                                ins = nc.tensor.matmul(o[:, c * CH:(c + 1) * CH], state[:, c, hh * P:(hh + 1) * P],
                                                       qdec[:, pr, c * CH:(c + 1) * CH], start=False, stop=True,
                                                       skip_group_check=True)
                    end(ins)
                elif kind == "gla_sum":
                    o = begin(st)
                    taken(pe, ("gla_out", *arg))
                    end(nc.tensor.matmul(o, C("ones"), osq, start=True, stop=True))
                elif kind == "router":
                    o = begin(st)
                    pe.wait_ge(ld["router"], 16)
                    for t in range(TT):
                        for k in range(KD):
                            pe.wait_ge(h_ready, 8 + k + 1)
                            ins = nc.tensor.matmul(o[:, t * 36:(t + 1) * 36], hT[:, k, t * P:(t + 1) * P], w_router[:, k, :],
                                                   start=(k == 0), stop=(k == KD - 1))
                    end(ins)
                elif kind == "turn_h":
                    t, half = arg
                    o = begin(st)
                    for j in range(4):
                        ins = nc.tensor.transpose(o[:, j * P:(j + 1) * P], hT[:, 4 * half + j, t * P:(t + 1) * P], C("ident"))
                    end(ins)
                elif kind == "rank":
                    o = begin(st)
                    pe.wait_ge(r_m, 1)
                    for t in range(TT):
                        for u in range(t + 1):
                            nc.tensor.matmul(o[:, t * 32:(t + 1) * 32], C("before") if u == t else C("ones"), M[:, u, :],
                                             start=(u == 0), stop=(u == t))
                    for u in range(TT):
                        ins = nc.tensor.matmul(o[:, P:P + 32], C("ones"), M[:, u, :], start=(u == 0), stop=(u == TT - 1))
                    end(ins)
                elif kind == "moe":
                    taken(pe, ("rank",))
                    for t in range(TT):
                        for half in range(2):
                            taken(pe, ("turn_h", t, half))
                    pe.wait_ge(std_done, 2)

                    def gather(rows_, s):
                        for k in range(KD):
                            for t in range(TT):
                                ins = nc.tensor.matmul(ps_[:, k // 4, k % 4 * P:k % 4 * P + rows_], htok[:, t, k * P:(k + 1) * P],
                                                       chosen[:, t, 0:rows_], start=(t == 0), stop=(t == TT - 1))
                        ins.then_inc(s, 1)

                    def turn(rows_, s):
                        pe.sem_inc(passed["pe"], 1)
                        for k in range(4):
                            ins = nc.tensor.transpose(ps_[:, 4, k * P:k * P + rows_], hid[0:rows_, k * P:(k + 1) * P],
                                                      C("ident")[0:rows_, 0:rows_])
                        ins.then_inc(s, 1)

                    def product(xT_op, part, experts, halves, bank0, s, odd=0):
                        tiles = (KD, KD, 4)[part]
                        ws = [(slot[2 * part + b] if part else gate_slots[2 * odd + b])[:, :].rearrange("p (k n) -> p k n", k=tiles) for b in range(experts)]
                        for half in range(halves):
                            for k in range(tiles):
                                for b in range(experts):
                                    ins = nc.tensor.matmul(ps_[b * CAP:(b + 1) * CAP, bank0 + half, :],
                                                           xT_op[:, k, b * CAP:(b + 1) * CAP],
                                                           ws[b][:, k, half * 512:(half + 1) * 512],
                                                           start=(k == 0), stop=(k == tiles - 1))
                        ins.then_inc(s, 1)

                    def loaded(part, n):
                        for b in range(2):
                            pe.wait_ge(m_w[2 * part - 2 + b], 16 * n + 16)

                    def pair(i):
                        for b in range(2):
                            n = 2 * i + b
                            pe.wait_ge(m_["chosen"], n + 1)
                            gather(2 * CAP, m_["x"])
                            pe.wait_ge(m_["xT"], n + 1)
                            for s_ in m_gate_w[2 * b:2 * b + 2]:
                                pe.wait_ge(s_, 16 * i + 16)
                            product(xgT, 0, 2, 1, 2, m_["gate"], b)
                            loaded(1, n)
                            product(xgT, 1, 2, 1, 3, m_["up"])
                            pe.wait_ge(m_["hid"], n + 1)
                            turn(2 * CAP, m_["hturned"])
                            pe.wait_ge(m_["hidT"], n + 1)
                            free(pe, m_["y"], n)
                            loaded(2, n)
                            product(hidT, 2, 2, 2, 5, m_["down"])

                    def over(i):
                        pe.wait_ge(o_["chosen"], i + 1)
                        gather(CAP, o_["x"])
                        pe.wait_ge(o_["xT"], i + 1)
                        pe.wait_ge(o_w, 48 * i + 48)
                        product(xgT, 0, 1, 1, 2, o_["gate"])
                        product(xgT, 1, 1, 1, 3, o_["up"])
                        pe.wait_ge(o_["hid"], i + 1)
                        turn(CAP, o_["hturned"])
                        pe.wait_ge(o_["hidT"], i + 1)
                        product(hidT, 2, 1, 2, 5, o_["down"])
                        pe.wait_ge(o_["st"], 16 * i + 16)

                    pairs(pe, pair)
                    pe.wait_ge(m_["y"], NE // 2)
                    pe.wait_ge(r_dest, 1)
                    n_over = nc.tensor.value_load(over_i[0:1, NOVER:NOVER + 1], min_val=0, max_val=NOVER)
                    overflow(pe, n_over, over)
                elif kind == "turn_y":
                    t, half = arg
                    o = begin(st)
                    pe.wait_ge(y_mixed, t + 1)
                    for j in range(4):
                        ins = nc.tensor.transpose(o[:, j * P:(j + 1) * P],
                                                  yg[2 * t][:, (4 * half + j) * P:(4 * half + j + 1) * P], C("ident"))
                    end(ins)
                elif kind == "lru_gate":
                    which, n = arg
                    o = begin(st)
                    pe.wait_ge(conv_done, n + 1)
                    j = int(which == "i")
                    pe.wait_ge(ld["blocks"], 16)
                    end(nc.tensor.matmul(o, w_bd[:, n, j, :], lc[:, n % 4, :], start=True, stop=True))
                elif kind == "stick":
                    for name in jobs[J[("proj", "v2", 15)] - 6:J[("proj", "v2", 15)] + 1]:
                        taken(pe, name)
                    pe.wait_ge(std_done, 3)
                    pe.wait_ge(stick_set, 1)

                    def scores(h):
                        pr, lo = h // 2, CH * (h % 2)
                        b0 = 3 * (h % 2)
                        if h >= 2:
                            pe.wait_ge(att_done, h - 1)
                        for kt, (c, w_) in enumerate(SEG):
                            o = ps_[:, b0 + c // 512, c % 512:c % 512 + w_]
                            nc.tensor.matmul(o, k2[lo:lo + CH, pr, kt * P:(kt + 1) * P], q2[lo:lo + CH, pr, kt * P:S],
                                             start=(kt != 3), stop=False, skip_group_check=True)
                            ins = nc.tensor.matmul(ps_[:, b0 + c // 512, c % 512:c % 512 + P], ident_b, bias_b,
                                                   start=False, stop=False, skip_group_check=True)
                        ins.then_inc(z_done, 1)

                    def suffix(h):
                        b0 = 3 * (h % 2)

                        def sums(tri, ones, L, kts):
                            for jt, (c, w_) in enumerate(SEG):
                                for kt in kts:
                                    if kt >= jt:
                                        ck_, wk = SEG[kt]
                                        o = c + (kt - jt) * P
                                        ins = nc.tensor.matmul(ps_[:, b0 + o // 512, o % 512:o % 512 + wk], tri if kt == jt else ones,
                                                               L[h % 2][:, ck_:ck_ + wk], start=False, stop=False, skip_group_check=True)
                            return ins

                        pe.wait_ge(sp_done, h + 1)
                        sums(tri_r, ones_r, Lhigh, (0, 1, 2))
                        sums(C("negtri"), C("negones"), Lb, (3,))
                        pe.wait_ge(sp_low, h + 1)
                        ins = sums(tri_r, ones_r, Llow, (0, 1, 2))
                        ins.then_inc(tri_done, 1)

                    def head_values(h):
                        pr = h // 2
                        pe.wait_ge(att_done, h + 1)
                        if h >= 2:
                            pe.wait_ge(pv_out, h - 1)
                        for kt, (c, w_) in enumerate(SEG):
                            ins = nc.tensor.matmul(ps_[:, 6 + h % 2, kt * P:S], v2[:, kt, pr * P:(pr + 1) * P],
                                                   att[h % 2][:, c:c + w_], start=(kt == 0), stop=(kt == TT - 1),
                                                   skip_group_check=True)
                        ins.then_inc(pv_done, 1)

                    scores(0)
                    scores(1)
                    for h in range(HB + 1):
                        if h < HB:
                            suffix(h)
                        if h >= 1:
                            head_values(h - 1)
                        if h + 2 < HB:
                            scores(h + 2)
                    pe.wait_ge(att_done, HB)
                    pe.wait_ge(pv_out, HB)

        @block.scalar
        def _(act):
            chain = [0]

            def link(ins):
                chain[0] += 1
                ins.then_inc(act_chain, 1)
                act.wait_ge(act_chain, chain[0])

            one, eps = C("one"), C("eps")

            def fn(dst, src, f, **kw):
                return nc.scalar.activation(dst, src, f, **kw)

            def root(dst, sums, n):
                return fn(dst, sums, ACT.Sqrt, scale=1.0 / n, bias=eps)

            act.wait_ge(ld["cst"], 16)
            act.wait_ge(ld["prm"], 16)
            for st in steps:
                kind, arg = st[0], st[1:]
                if kind == "mem_norm":
                    act.wait_ge(mem_sum, 1)
                    root(std[:, 0:NM], ps_[:, 7, 0:NM], D).then_inc(mem_std, 1)
                    link(fn(lw[0], prm[:, GAINS["lru_lambda_2"][0]:GAINS["lru_lambda_2"][1]], ACT.Abs))
                    fn(lw[1], lw[0], ACT.Exp, scale=-1.0).then_inc(lam_exp, 1)
                    act.wait_ge(ld["x"], 16)
                    for n in range(KD):
                        fn(hT[:, n, :], xT[:, n, :], ACT.Square).then_inc(squared, 1)
                elif kind == "square":
                    norm, n = arg
                    if norm == 5:
                        act.wait_ge(x_new, n + 1)
                    else:
                        taken(act, {1: ("proj", "out", n), 3: ("proj", "out2", n), 4: ("proj", "dn", 3 * KD + n)}[norm])
                    if n == 0:
                        act.wait_ge(std_done, norm)
                        fn(acc, xT[:, n, :], ACT.Square).then_inc(squared, 1)
                    else:
                        if n == 1:
                            norm_used(act, norm)
                        else:
                            act.wait_ge(acc_done, 7 * SQUARED.index(norm) + n - 1)
                        fn(sq, xT[:, n, :], ACT.Square).then_inc(squared, 1)
                elif kind == "y_square":
                    t = arg[0]
                    for half in range(2):
                        taken(act, ("turn_y", t, half))
                    fn(hT[:, :, t * P:(t + 1) * P], xT[:, :, t * P:(t + 1) * P], ACT.Square).then_inc(y_squared, 1)
                elif kind == "norm":
                    norm = arg[0]
                    act.wait_ge(summed, norm + 1)
                    if norm == 0:
                        act.wait_ge(mem_h, 8)
                    if norm == 2:
                        norm_used(act, 2)
                    root(std, ps_[:, 7, :], D).then_inc(std_done, 1)
                elif kind == "split":
                    s_ = arg[0]
                    if s_ in split_old:
                        finished(act, split_old[s_])
                    for k in range(KD):
                        if s_ == 1:
                            act.wait_ge(yl_done, k + 1)
                        elif s_ == 2:
                            act.wait_ge(pv_out, HB)
                        elif s_ == 3:
                            act.wait_ge(merge_done, k + 1)
                        else:
                            act.wait_ge(tmp_done, KD * {0: 0, 4: 1, 5: 2}[s_] + k + 1)
                        fn(HH[:, k, :], split_src(s_, k), ACT.Copy).then_inc(high_done, 1)
                elif kind == "weights":
                    g = arg[0]
                    _, s_, v_ = panel_at(PANELS2[g // 2])
                    act.wait_ge(s_, v_)
                    if g in STICK_HALVES:
                        act.wait_ge(pv_done, HB)
                    half_free(act, g)
                    fn(WH[g % 2], raw_half(g), ACT.Copy).then_inc(w_high, 1)
                elif kind == "proj":
                    name, n = arg
                    job = st
                    o = None if name in ("out", "bl", "ba", "out2", "dn", "ple") else bank(job)
                    if o is not None:
                        finished(act, job)
                    if name in ("ck", "cq", "mq", "mk"):
                        i = hn_index[arg]
                        w_ = NM if name == "ck" else S
                        if i == 0:
                            act.wait_ge(mem_h, 8)
                        if i >= 2:
                            act.wait_ge(hn_done, i - 1)
                        fn(hn_raw[:, i % 2, 0:w_], o[:, 0:w_], ACT.Copy)
                        link(fn(hn_sq[:, i % 2, 0:w_], o[:, 0:w_], ACT.Square))
                        act.sem_inc(hn_in, 1)
                        act.sem_inc(bank_free[J[job] % JB], 1)
                    elif name in ("cv", "mv"):
                        dst = (cvpad if name == "cv" else vpad)[:, n, :, :]
                        act.wait_ge(zeroed, 3)
                        src = o[:, 0:256].rearrange("p (a b d) -> p a b d", a=2, b=2)
                        d4 = dst.rearrange("p (a b) d -> p a b d", a=2)
                        fn(d4[:, :, 0, 0:CH], src[:, :, 0, :], ACT.Copy)
                        frees(fn(d4[:, :, 1, CH:P], src[:, :, 1, :], ACT.Copy), job)
                    elif name in ("gq", "gk"):
                        frees(fn((gq if name == "gq" else gk)[:, n, :], o, ACT.Copy), job)
                    elif name == "lr":
                        frees(fn(lrT[0:RANK, :], o[0:RANK, :], ACT.Copy), job)
                    elif name == "gv":
                        frees(fn(gv[:, n, :], o, ACT.Copy), job)
                    elif name == "r":
                        act.wait_ge(zeros_stored, 16)
                        frees(fn(rs[:, n, :], o, ACT.Silu), job)
                    elif name == "ux":
                        if n == 0:
                            act.wait_ge(pad_zero, 1)
                        if n >= 2:
                            act.wait_ge(conv_done, n - 1)
                        frees(fn(uxp[:, n % 2, 3:3 + S], o, ACT.Copy), job)
                    elif name == "ug":
                        if n >= 2:
                            act.wait_ge(yl_done, n - 1)
                        frees(fn(gel[:, n % 2, :], o, ACT.Gelu_apprx_tanh), job)
                    elif name == "q2":
                        if n == 0:
                            act.wait_ge(lru_done, KD)
                        frees(fn(q2[:, n, :], o, ACT.Copy, scale=0.125), job)
                    elif name == "k2":
                        if n == 0:
                            act.wait_ge(yl_done, KD)
                        frees(fn(k2[:, n, :], o, ACT.Copy), job)
                    elif name == "v2":
                        q4, t = n // TT, n % TT
                        if n == 0:
                            act.wait_ge(lru_done, KD)
                        frees(fn(v2[:, t, q4 * 256:q4 * 256 + 256], o[:, 0:256], ACT.Copy), job)
                    elif name in ("gl", "ga"):
                        if name == "gl" and n == 0:
                            act.wait_ge(pv_done, HB)
                        frees(fn(sig[name][:, n, :], o, ACT.Sigmoid), job)
                    elif name == "up":
                        if n >= 2:
                            act.wait_ge(hid_low, n - 1)
                        frees(fn(relu[:, n % 2, :], o, ACT.Relu), job)
                        c = n // KD
                        if c == 0:
                            finished(act, ("proj", "out2", 7))
                        elif c >= 2:
                            finished(act, ("proj", "dn", (c - 2) * KD + 7))
                        act.wait_ge(relu_sq, n + 1)
                        fn(HC[c % 2][0][:, n % KD, :], relu[:, n % 2, :], ACT.Copy).then_inc(hid_high, 1)
                    elif name == "pg":
                        frees(fn(pgs[:, n, :], o, ACT.Sigmoid), job)
                elif kind == "headsum":
                    i = hn_index[arg]
                    w_ = NM if arg[0] == "ck" else S
                    finished(act, st)
                    frees(root(hn_sq[:, i % 2, 0:w_], bank(st)[:, 0:w_], CH), st)
                elif kind == "softmax":
                    u = unit_index[arg]
                    which, pr, qt, hh = arg
                    act.wait_ge(neg_ready, u + 1)
                    if u >= 2:
                        finished(act, ("turn", *prev_unit(u - 2)))
                    if which == "mem":
                        ins = fn(p_sb[:, u % 2, 0:NM], bank(("score", *arg))[:, 0:NM], ACT.Exp, scale=0.125,
                                 bias=row_neg[:, u % 2:u % 2 + 1], accum_out=row_sum[:, u % 2:u % 2 + 1])
                    else:
                        w_ = P * (qt + 1)
                        ins = fn(p_sb[:, u % 2, 0:w_], s_sb[:, u % 2, 0:w_], ACT.Exp,
                                 bias=row_neg[:, u % 2:u % 2 + 1], accum_out=row_sum[:, u % 2:u % 2 + 1])
                    ins.then_inc(exp_done, 1)
                elif kind == "turn":
                    which, pr, qt, hh = arg
                    finished(act, st)
                    nk = MT if which == "mem" else qt + 1
                    first = unit_index[arg]
                    if first >= 2:
                        pu = prev_unit(2 * (first // 2) - 2)
                        finished(act, ("values", *pu[:3]))
                    frees(fn(pT[:, hh, 0:nk, :], bank(st)[:, 0:nk * P].rearrange("p (k q) -> p k q", q=P), ACT.Copy), st)
                elif kind == "values":
                    which, pr, qt = arg
                    finished(act, st)
                    tile = (6 if which == "mem" else 4) + pr
                    frees(fn(mixT[:, tile, qt * P:(qt + 1) * P], bank(st)[:, 0:P], ACT.Copy), st)
                elif kind == "gate":
                    pr = arg[0]
                    finished(act, st)
                    frees(fn(zb[:, pr, :], bank(st), ACT.Identity, bias=G("b_gla_gk", pr)), st)
                elif kind == "gla_begin":
                    finished(act, ("values", "moba", 1, TT - 1))
                    act.wait_ge(exp_done, 32)
                elif kind == "decay":
                    pr = arg[0]
                    if pr:
                        act.wait_ge(qk_ready, pr)
                    taken(act, ("gate", pr))
                    nc.scalar.preload_act_table_set("natural_log_exp_and_others")
                    link(fn(t1, zb[:, pr, :], ACT.Abs))
                    link(fn(t1, t1, ACT.Exp, scale=-1.0))
                    fn(t1, t1, ACT.Ln, bias=one).then_inc(lsig, 1)
                    act.wait_ge(cum_done, 2 * pr + 2)
                    i16 = 1.0 / 16.0
                    fn(ecum, cum, ACT.Exp, scale=i16)
                    fn(einv, cum, ACT.Exp, scale=-i16)
                    fn(eend, t1, ACT.Exp, scale=i16)
                    fn(dec[pr], cum.rearrange("p (c l) -> p c l", l=CH)[:, :, CH - 1], ACT.Exp, scale=i16).then_inc(dec_exp, 1)
                elif kind == "gla_out":
                    h = 2 * arg[0] + arg[1]
                    finished(act, st)
                    if h:
                        act.wait_ge(o_done, h)
                        finished(act, ("gla_sum", (h - 1) // 2, (h - 1) % 2))
                    fn(ogn, bank(st), ACT.Copy)
                    frees(fn(osq, bank(st), ACT.Square), st)
                elif kind == "gla_sum":
                    finished(act, st)
                    frees(root(ostd, bank(st), P), st)
                elif kind == "turn_h":
                    t, half = arg
                    finished(act, st)
                    frees(fn(htok[:, t, half * 512:half * 512 + 512], bank(st), ACT.Copy), st)
                elif kind == "route":
                    act.wait_ge(r_gd, 1)
                    fn(w4e, w4, ACT.Exp).then_inc(r_exp, 1)
                    act.wait_ge(r_e2in, 1)
                    fn(col[5], col[4], ACT.Exp).then_inc(r_e2, 1)
                elif kind == "moe":
                    def silu(f, rows_, n):
                        act.wait_ge(f["gate"], n + 1)
                        fn(sg[0:rows_, :], ps_[0:rows_, 2, :], ACT.Silu).then_inc(f["silu"], 1)

                    def rows_out(f, first, rows_, n):
                        act.wait_ge(f["down"], n + 1)
                        free(act, f["st"], 16 * n)
                        fn(yout[0:rows_, :], ps_[0:rows_, 5:7, :].rearrange("p a n -> p (a n)"),
                           ACT.Copy).then_inc(f["y"], 1)
                        act.wait_ge(f["y"], n + 1)
                        act.dma_start(y_dram[bass.ds(first, rows_), :], yout[0:rows_, :]).then_inc(f["st"], 16)

                    def pair(i):
                        for n in (2 * i, 2 * i + 1):
                            free(act, m_["hid"], n)
                            silu(m_, 2 * CAP, n)
                            rows_out(m_, n * 2 * CAP, 2 * CAP, n)

                    def over(i):
                        silu(o_, CAP, i)
                        rows_out(o_, (NE + i) * CAP, CAP, i)

                    pairs(act, pair)
                    act.wait_ge(m_["st"], 16 * (NE // 2))
                    act.wait_ge(zeros_stored, 16)
                    act.wait_ge(r_dest, 1)
                    n_over = nc.scalar.value_load(over_i[0:1, NOVER:NOVER + 1], min_val=0, max_val=NOVER)
                    overflow(act, n_over, over)
                elif kind == "lru_gate":
                    which, n = arg
                    if n >= 2:
                        act.wait_ge(lru_done, n - n % 2)
                    finished(act, st)
                    dst, b_ = (lr_, "b_rgate_2") if which == "r" else (li, "b_igate_2")
                    frees(fn(dst[:, n % 2, :], bank(st), ACT.Sigmoid, bias=G(b_, n)), st)
                elif kind == "lru":
                    g = arg[0]
                    if g == 0:
                        act.wait_ge(lam_done, 1)
                    taken(act, ("lru_gate", "r", 2 * g))
                    taken(act, ("lru_gate", "r", 2 * g + 1))
                    for m in (2 * g, 2 * g + 1):
                        fn(la[:, m % 2, :], lr_[:, m % 2, :], ACT.Exp, scale=nsp8[:, m:m + 1])
                        ins = fn(lt[:, m % 2, :], lr_[:, m % 2, :], ACT.Tanh, scale=sp8[:, m:m + 1])
                    ins.then_inc(lru_exp, 1)
                    act.wait_ge(lru_m2, g + 1)
                    fn(lt, lt, ACT.Sqrt).then_inc(lru_mult, 1)
                elif kind == "stick":
                    finished(act, ("proj", "v2", 15))

                    def softplus(h):
                        act.wait_ge(z_done, h + 1)
                        if h >= 2:
                            act.wait_ge(tri_done, h - 1)
                        link(fn(Lb[h % 2], flat(h), ACT.Abs))
                        link(fn(Lb[h % 2], Lb[h % 2], ACT.Exp, scale=-1.0))
                        fn(Lb[h % 2], Lb[h % 2], ACT.Ln, bias=one).then_inc(sp_log, 1)

                    def weights(h):
                        act.wait_ge(tri_done, h + 1)
                        if h >= 2:
                            act.wait_ge(pv_done, h - 1)
                        fn(att[h % 2], flat(h), ACT.Exp).then_inc(att_done, 1)

                    nc.scalar.preload_act_table_set("natural_log_exp_and_others")
                    softplus(0)
                    softplus(1)
                    for h in range(HB):
                        weights(h)
                        if h + 2 < HB:
                            softplus(h + 2)

        @block.vector
        def _(dve):
            chain = [0]

            def link(ins):
                chain[0] += 1
                ins.then_inc(dve_chain, 1)
                dve.wait_ge(dve_chain, chain[0])

            v = nc.vector
            dve.wait_ge(ld["cst"], 16)
            dve.wait_ge(ld["prm"], 16)
            lam = prm[:, GAINS["lru_lambda_2"][0]:GAINS["lru_lambda_2"][1]]
            dve.wait_ge(ld["mem"], 16)
            v.tensor_tensor(memh, memT, memT, ALU.mult).then_inc(mem_sq, 1)
            dve.wait_ge(lam_exp, 1)
            link(v.tensor_scalar(lw[2], lw[1], 2.0, None, ALU.add))
            link(v.reciprocal(lw[2], lw[2]))
            link(v.tensor_tensor(lw[3], lw[1], lw[2], ALU.mult))
            link(v.tensor_tensor(lw[4], lw[3], lw[3], ALU.mult))
            link(v.tensor_scalar(lw[5], lw[4], 1.0 / 17, 1.0 / 15, ALU.mult, ALU.add))
            for d in (13, 11, 9, 7, 5, 3, 1):
                link(v.tensor_tensor(lw[5], lw[5], lw[4], ALU.mult))
                link(v.tensor_scalar(lw[5], lw[5], 1.0 / d, None, ALU.add))
            link(v.scalar_tensor_tensor(out=lw[5], in0=lw[5], scalar=2.0, in1=lw[3], op0=ALU.mult, op1=ALU.mult))
            link(v.tensor_scalar(lw[0], lam, -1.0, 0.0, ALU.mult, ALU.max))
            link(v.tensor_tensor(lw[5], lw[5], lw[0], ALU.add))
            v.tensor_scalar(nsp8, lw[5], -8.0, None, ALU.mult)
            v.tensor_scalar(sp8, lw[5], 8.0, None, ALU.mult).then_inc(lam_done, 1)

            def add_x(n, job):
                finished(dve, job)
                frees(v.tensor_tensor(xT[:, n, :], bank(job), xT[:, n, :], ALU.add), job)

            def low_part(s_, k):
                dve.wait_ge(high_done, KD * s_ + k + 1)
                v.tensor_tensor(HL[:, k, :], split_src(s_, k), HH[:, k, :].bitcast(F32), ALU.subtract).then_inc(low_done, 1)

            def pick_first(dst, cond, first, tmp, mx):
                link(v.tensor_tensor(tmp, cond, first, ALU.mult))
                link(v.tensor_reduce(mx, tmp, AX, ALU.max))
                link(v.tensor_tensor(dst, tmp, mx.unsqueeze(2).to_broadcast(list(tmp.shape)), ALU.is_equal))

            def rows(x):
                return x.unsqueeze(1).to_broadcast([P, TT, x.shape[1]])

            def each(x, n):
                return x.unsqueeze(2).to_broadcast([P, x.shape[1], n])

            for st in steps:
                kind, arg = st[0], st[1:]
                if kind == "mem_norm":
                    dve.wait_ge(mem_std, 1)
                    link(v.reciprocal(std[:, 0:NM], std[:, 0:NM]))
                    for k in range(KD):
                        v.scalar_tensor_tensor(out=memh[:, k, :], in0=memT[:, k, :], scalar=G("mem_norm_g", k),
                                               in1=std[:, 0:NM], op0=ALU.mult, op1=ALU.mult).then_inc(mem_h, 1)
                elif kind == "norm":
                    norm = arg[0]
                    gain = ["attn_norm_g", "ffn_norm_g", "norm_mix_g_2", "norm_mlp_g_2", "norm_ple_g_2",
                            "norm_final_g_2"][norm]
                    if norm in (1, 5):
                        finished(dve, ("proj", "r", 3) if norm == 1 else ("proj", "pg", 7))
                    dve.wait_ge(std_done, norm + 1)
                    link(v.reciprocal(std, std))
                    if norm in (2, 3, 4):
                        low = {2: 0, 3: 4, 4: 5}[norm]
                        for k in range(KD):
                            v.scalar_tensor_tensor(out=tmp[:, k, :], in0=xT[:, k, :], scalar=G(gain, k), in1=std,
                                                   op0=ALU.mult, op1=ALU.mult).then_inc(tmp_done, 1)
                        for k in range(4, KD):
                            low_part(low, k)
                        if norm == 2:
                            v.memset(uxp[:, :, 0:3], 0.0).then_inc(pad_zero, 1)
                        continue
                    for k in range(KD):
                        v.scalar_tensor_tensor(out=hT[:, k, :], in0=xT[:, k, :], scalar=G(gain, k), in1=std,
                                               op0=ALU.mult, op1=ALU.mult).then_inc(h_ready, 1)
                elif kind == "split":
                    if arg[0] in (1, 2, 3):
                        for k in range(KD):
                            low_part(arg[0], k)
                elif kind == "square":
                    norm, n = arg
                    if n:
                        dve.wait_ge(squared, 8 + 8 * SQUARED.index(norm) + n + 1)
                        v.tensor_tensor(acc, acc, sq, ALU.add).then_inc(acc_done, 1)
                elif kind == "proj":
                    name, n = arg
                    if name == "dn":
                        add_x(n % KD, st)
                    elif name in ("out", "out2"):
                        add_x(n, st)
                    elif name == "ug":
                        taken(dve, st)
                        v.tensor_tensor(yl[:, n, :], yl[:, n, :], gel[:, n % 2, :], ALU.mult).then_inc(yl_done, 1)
                    elif name in ("bl", "ba"):
                        sg_ = sig["gl" if name == "bl" else "ga"][:, n, :]
                        taken(dve, ("proj", "gl" if name == "bl" else "ga", n))
                        finished(dve, st)
                        if name == "bl":
                            frees(v.tensor_tensor(merged[:, n, :], bank(st), sg_, ALU.mult), st)
                        else:
                            if n:
                                dve.wait_ge(merge_done, n)
                            frees(v.tensor_tensor(prod["ba"], bank(st), sg_, ALU.mult), st)
                            taken(dve, st)
                            v.tensor_tensor(merged[:, n, :], merged[:, n, :], prod["ba"], ALU.add).then_inc(merge_done, 1)
                    elif name == "up":
                        taken(dve, st)
                        v.tensor_tensor(relu[:, n % 2, :], relu[:, n % 2, :], relu[:, n % 2, :], ALU.mult).then_inc(relu_sq, 1)
                        dve.wait_ge(hid_high, n + 1)
                        high, low = HC[n // KD % 2]
                        v.tensor_tensor(low[:, n % KD, :], relu[:, n % 2, :], high[:, n % KD, :].bitcast(F32),
                                        ALU.subtract).then_inc(hid_low, 1)
                    elif name == "ple":
                        taken(dve, ("proj", "pg", n))
                        finished(dve, st)
                        if n:
                            dve.wait_ge(x_new, n)
                        frees(v.tensor_tensor(prod["ple"], bank(st), pgs[:, n, :], ALU.mult), st)
                        taken(dve, st)
                        v.tensor_tensor(xT[:, n, :], xT[:, n, :], prod["ple"], ALU.add).then_inc(x_new, 1)
                elif kind == "headsum":
                    name, n = arg
                    i = hn_index[arg]
                    w_ = NM if name == "ck" else S
                    taken(dve, st)
                    dve.wait_ge(hn_in, i + 1)
                    dve.wait_ge(zeroed, 3)
                    link(v.reciprocal(hn_sq[:, i % 2, 0:w_], hn_sq[:, i % 2, 0:w_]))
                    gain = G({"mq": "moba_q_norm_g", "mk": "moba_k_norm_g", "cq": "mem_q_norm_g", "ck": "mem_k_norm_g"}[name])
                    parts = [(0, P, {"mk": kn, "ck": ckn}[name][:, n, :])] if name in ("mk", "ck") else [
                        (lo, lo + CH, {"mq": qpad, "cq": cqpad}[name][lo:lo + CH, 2 * n + lo // CH, :]) for lo in (0, CH)]
                    for lo, hi, dst in parts:
                        ins = v.scalar_tensor_tensor(out=dst, in0=hn_raw[lo:hi, i % 2, 0:w_], scalar=gain[lo:hi, :],
                                                     in1=hn_sq[lo:hi, i % 2, 0:w_], op0=ALU.mult, op1=ALU.mult)
                    ins.then_inc(hn_done, 1)
                elif kind == "softmax":
                    u = unit_index[arg]
                    which, pr, qt, hh = arg
                    j = u % 2
                    h = 2 * pr + hh
                    finished(dve, ("score", *arg))
                    if u >= 2:
                        dve.wait_ge(exp_done, u - 1)
                    o = bank(("score", *arg))
                    if which == "mem":
                        w_ = NM
                        link(v.tensor_reduce(row_max[:, j:j + 1], o[:, 0:w_], AX, ALU.max))
                        v.tensor_scalar(row_neg[:, j:j + 1], row_max[:, j:j + 1], -0.125, None, ALU.mult).then_inc(neg_ready, 1)
                    else:
                        w_ = P * (qt + 1)
                        link(v.tensor_scalar(slope_b[:, 0:w_], C("alibi")[:, S - w_:S], 2.0 ** (-2 * (h + 1)), None, ALU.mult))
                        link(v.scalar_tensor_tensor(out=s_sb[:, j, 0:w_], in0=o[:, 0:w_], scalar=0.125,
                                                    in1=slope_b[:, 0:w_], op0=ALU.mult, op1=ALU.add))
                        link(v.tensor_reduce(row_max[:, j:j + 1], s_sb[:, j, 0:w_], AX, ALU.max))
                        v.tensor_scalar(row_neg[:, j:j + 1], row_max[:, j:j + 1], -1.0, None, ALU.mult).then_inc(neg_ready, 1)
                    dve.wait_ge(exp_done, u + 1)
                    dve.sem_inc(bank_free[J[("score", *arg)] % JB], 1)
                    link(v.reciprocal(row_inv[:, j:j + 1], row_sum[:, j:j + 1]))
                    v.tensor_scalar(p_sb[:, j, 0:w_], p_sb[:, j, 0:w_], row_inv[:, j:j + 1], None, ALU.mult).then_inc(p_ready, 1)
                elif kind == "gla_begin":
                    finished(dve, ("values", "moba", 1, TT - 1))
                    dve.wait_ge(state_zero, 1)
                elif kind == "decay":
                    pr = arg[0]
                    for nm in ("gq", "gk"):
                        taken(dve, ("proj", nm, pr))
                    dve.wait_ge(lsig, pr + 1)
                    if pr:
                        dve.wait_ge(dec_exp, pr)
                    link(v.scalar_tensor_tensor(out=t1, in0=zb[:, pr, :], scalar=0.0, in1=t1, op0=ALU.min, op1=ALU.subtract))
                    v.tensor_tensor_scan(cum, C("reset"), t1, 0.0, ALU.mult, ALU.add).then_inc(cum_done, 1)
                    dve.wait_ge(cum_done, 2 * pr + 1)
                    c3 = cum.rearrange("p (c l) -> p c l", l=CH)
                    v.tensor_tensor(t1.rearrange("p (c l) -> p c l", l=CH), c3[:, :, CH - 1:CH].to_broadcast([P, 8, CH]), c3,
                                    ALU.subtract).then_inc(cum_done, 1)
                    dve.wait_ge(dec_exp, pr + 1)
                    if pr:
                        finished(dve, ("turn_keys", pr - 1))
                    v.scalar_tensor_tensor(out=qdec[:, pr, :], in0=gq[:, pr, :], scalar=0.125, in1=ecum, op0=ALU.mult, op1=ALU.mult)
                    for lo in (0, CH):
                        v.tensor_tensor(kinv[lo:lo + CH, 2 * pr + lo // CH, :], gk[lo:lo + CH, pr, :], einv[lo:lo + CH, :], ALU.mult)
                    v.tensor_tensor(kend_f, gk[:, pr, :], eend, ALU.mult).then_inc(qk_ready, 1)
                elif kind == "turn_keys":
                    pr = arg[0]
                    finished(dve, st)
                    if pr:
                        finished(dve, ("chunk_state", pr - 1, 3))
                    for s_ in range(2):
                        ins = v.tensor_scalar(kend[:, s_, :, :], bank(st).rearrange("p (t f) -> p t f", t=TT),
                                              C("half")[:, s_:s_ + 1], None, ALU.mult)
                    frees(ins, st)
                elif kind == "intra":
                    pr, hh = arg
                    finished(dve, st)
                    if pr:
                        finished(dve, ("gla_out", pr - 1, hh))
                    frees(v.tensor_tensor(at_sb[:, hh, :, :], bank(st).rearrange("p (t f) -> p t f", t=TT),
                                          C("chunkmask").unsqueeze(1).to_broadcast([P, TT, P]), ALU.mult), st)
                elif kind == "chunk_state":
                    pr, g = arg
                    finished(dve, st)
                    if pr and g == 0:
                        finished(dve, ("gla_out", pr - 1, 1))
                    for s_ in range(2):
                        c = 2 * g + s_
                        if c == 7:
                            break
                        if c:
                            dve.wait_ge(st_done, 14 * pr + 2 * c)
                        for lo in (0, CH):
                            cs = slice(lo // CH * P, lo // CH * P + P)
                            d_ = state[lo:lo + CH, c + 1, cs]
                            u_ = bank(st)[lo:lo + CH, s_ * 256 + cs.start:s_ * 256 + cs.stop]
                            if c == 0:
                                v.tensor_copy(d_, u_).then_inc(st_done, 1)
                            else:
                                v.scalar_tensor_tensor(out=d_, in0=state[lo:lo + CH, c, cs], scalar=dec[pr][lo:lo + CH, c:c + 1],
                                                       in1=u_, op0=ALU.mult, op1=ALU.add).then_inc(st_done, 1)
                    dve.wait_ge(st_done, 14 * pr + 2 * min(2 * g + 2, 7))
                    dve.sem_inc(bank_free[J[st] % JB], 1)
                elif kind == "gla_sum":
                    h = 2 * arg[0] + arg[1]
                    taken(dve, st)
                    link(v.reciprocal(ostd, ostd))
                    link(v.scalar_tensor_tensor(out=ogn, in0=ogn, scalar=G("gla_out_norm_g"), in1=ostd, op0=ALU.mult, op1=ALU.mult))
                    taken(dve, ("proj", "r", h))
                    v.tensor_tensor(mixT[:, h, :], ogn, rs[:, h, :], ALU.mult).then_inc(o_done, 1)
                    dve.wait_ge(o_done, h + 1)
                elif kind == "router":
                    finished(dve, st)
                    lo, hi = GAINS["router_bias"]
                    frees(v.tensor_tensor(lg, bank(st)[:, 0:TT * 36].rearrange("p (t n) -> p t n", t=TT),
                                          rows(prm[:, lo:hi]), ALU.add), st)
                    taken(dve, st)
                elif kind == "route":
                    link(v.tensor_reduce(col[0], lg[:, :, 0:4], AX, ALU.max))
                    v.tensor_tensor(w4, lg[:, :, 0:4], each(col[0], 4), ALU.subtract).then_inc(r_gd, 1)
                    dve.wait_ge(r_gd, 1)
                    link(v.tensor_scalar(w4c, w4, 0.0, None, ALU.is_ge))
                    pick_first(w4b, w4c, rows(C("first4")), w4c, col[2])
                    link(v.tensor_scalar(w4b, w4b, -1.0, BIG, ALU.add, ALU.mult))
                    link(v.tensor_tensor(wk32.rearrange("p t (g e) -> p t g e", g=4),
                                         lg[:, :, 4:36].rearrange("p t (g e) -> p t g e", g=4),
                                         w4b.unsqueeze(3).to_broadcast([P, TT, 4, 8]), ALU.add))
                    for k in range(2):
                        link(v.tensor_reduce(col[2 + k], wk32, AX, ALU.max))
                        link(v.tensor_tensor(wk32b, wk32, each(col[2 + k], 32), ALU.is_ge))
                        pick_first(oh[k], wk32b, rows(C("first32")), wk32b, col[6])
                        if k == 0:
                            link(v.scalar_tensor_tensor(out=wk32, in0=oh[0], scalar=-100.0 * BIG, in1=wk32, op0=ALU.mult, op1=ALU.add))
                    v.tensor_tensor(M, oh[0], oh[1], ALU.add).then_inc(r_m, 1)
                    v.tensor_tensor(col[4], col[3], col[2], ALU.subtract).then_inc(r_e2in, 1)
                elif kind == "place":
                    rk = ("rank",)
                    finished(dve, rk)
                    o = bank(rk)
                    link(v.tensor_copy(cnt, o[:, P:P + 32]))
                    link(v.tensor_tensor(cmp, cnt.unsqueeze(2).to_broadcast([P, 32, 7]),
                                         C("thresholds").unsqueeze(1).to_broadcast([P, 32, 7]), ALU.is_gt))
                    link(v.tensor_reduce(nb, cmp, AX, ALU.add))
                    link(v.tensor_tensor_scan(obend, C("ones")[:, 0:32], nb, 0.0, ALU.mult, ALU.add))
                    link(v.tensor_tensor(dd, obend, nb, ALU.subtract))
                    link(v.tensor_tensor(dd, dd, C("expert"), ALU.subtract))
                    link(v.tensor_scalar(dd, dd, float(CAP), float((NE - 1) * CAP), ALU.mult, ALU.add))
                    rank = o[:, 0:P].rearrange("p (t e) -> p t e", t=TT)
                    link(v.tensor_scalar(wk32, rank, float(CAP), None, ALU.is_ge))
                    link(v.tensor_tensor(wk32, wk32, rows(dd), ALU.mult))
                    link(v.tensor_tensor(wk32, wk32, rank, ALU.add))
                    link(v.tensor_scalar(dd, C("expert"), float(CAP), None, ALU.mult))
                    link(v.tensor_tensor(dest, wk32, rows(dd), ALU.add))
                    for k in range(2):
                        link(v.tensor_tensor(wk32, dest, oh[k], ALU.mult))
                        link(v.tensor_reduce(row[:, k, :], wk32, AX, ALU.add))
                        v.tensor_copy(dest_i[:, k * TT:(k + 1) * TT], row[:, k, :])
                    dve.sem_inc(bank_free[J[rk] % JB], 1)
                elif kind == "moe":
                    def choose(f, rows_, n):
                        free(dve, f["row"], n)
                        for dst, k in ((chosen, 0), (chosen2, 1)):
                            ins = v.tensor_tensor(dst[:, :, 0:rows_], C("column")[:, 0:rows_].unsqueeze(1).to_broadcast([P, TT, rows_]),
                                                  row[:, k, :].unsqueeze(2).to_broadcast([P, TT, rows_]), ALU.is_equal)
                        ins.then_inc(f["equal"], 1)
                        dve.wait_ge(f["equal"], n + 1)
                        v.tensor_tensor(chosen[:, :, 0:rows_], chosen[:, :, 0:rows_], chosen2[:, :, 0:rows_], ALU.add).then_inc(f["chosen"], 1)
                        v.tensor_scalar(row, row, -float(rows_), None, ALU.add).then_inc(f["row"], 1)

                    def rows_in(f, rows_, n):
                        dve.wait_ge(f["x"], n + 1)
                        v.tensor_copy(xgT[:, :, 0:rows_], ps_[:, 0:2, :].rearrange("p a n -> p (a n)").rearrange(
                            "p (k c) -> p k c", k=KD)[:, :, 0:rows_]).then_inc(f["xT"], 1)

                    def gated(f, rows_, n):
                        dve.wait_ge(f["silu"], n + 1)
                        dve.wait_ge(f["up"], n + 1)
                        v.tensor_tensor(hid[0:rows_, :], ps_[0:rows_, 3, :], sg[0:rows_, :], ALU.mult).then_inc(f["hid"], 1)

                    def hidden_in(f, rows_, n):
                        dve.wait_ge(f["hturned"], n + 1)
                        v.tensor_copy(hidT[:, :, 0:rows_], ps_[:, 4, :].rearrange("p (k c) -> p k c", k=4)[:, :, 0:rows_]
                                      ).then_inc(f["hidT"], 1)

                    def pair(i):
                        for n in (2 * i, 2 * i + 1):
                            choose(m_, 2 * CAP, n)
                            free(dve, m_["up"], n)
                            rows_in(m_, 2 * CAP, n)
                            gated(m_, 2 * CAP, n)
                            free(dve, m_["down"], n)
                            hidden_in(m_, 2 * CAP, n)

                    def over(i):
                        free(dve, o_["st"], 16 * i)
                        choose(o_, CAP, i)
                        rows_in(o_, CAP, i)
                        gated(o_, CAP, i)
                        hidden_in(o_, CAP, i)

                    pairs(dve, pair)
                    link(v.tensor_tensor(cmp2, obend.unsqueeze(1).to_broadcast([P, NOVER, 32]),
                                         C("overblock").unsqueeze(2).to_broadcast([P, NOVER, 32]), ALU.is_le))
                    link(v.tensor_reduce(otab, cmp2, AX, ALU.add))
                    link(v.tensor_scalar(otab, otab, float(NE - 1), None, ALU.min))
                    v.tensor_copy(over_i[:, 0:NOVER], otab)
                    v.tensor_copy(over_i[:, NOVER:NOVER + 1], obend[:, 31:32]).then_inc(r_dest, 1)
                    dve.wait_ge(r_exp, 1)
                    link(v.tensor_reduce(col[1], w4e, AX, ALU.add))
                    link(v.reciprocal(col[1], col[1]))
                    dve.wait_ge(r_e2, 1)
                    link(v.tensor_scalar(col[7], col[5], 1.0, None, ALU.add))
                    link(v.reciprocal(col[7], col[7]))
                    link(v.tensor_tensor(gate_w[:, 0, :], col[7], col[1], ALU.mult))
                    link(v.tensor_tensor(gate_w[:, 1, :], gate_w[:, 0, :], col[5], ALU.mult))
                    dve.wait_ge(r_dest, 1)
                    dve.wait_ge(m_["row"], NE // 2)
                    dve.wait_ge(m_["st"], 16 * (NE // 2))
                    n_over = nc.vector.value_load(over_i[0:1, NOVER:NOVER + 1], min_val=0, max_val=NOVER)
                    overflow(dve, n_over, over)
                    for t in range(TT):
                        dve.wait_ge(y_got[t], 32)
                        link(v.tensor_scalar(yg[2 * t], yg[2 * t], gate_w[:, 0, t:t + 1], None, ALU.mult))
                        v.scalar_tensor_tensor(out=yg[2 * t], in0=yg[2 * t + 1], scalar=gate_w[:, 1, t:t + 1], in1=yg[2 * t],
                                               op0=ALU.mult, op1=ALU.add).then_inc(y_mixed, 1)
                elif kind == "turn_y":
                    t, half = arg
                    finished(dve, st)
                    xs = xT[:, 4 * half:4 * half + 4, t * P:(t + 1) * P]
                    frees(v.tensor_tensor(xs, bank(st).rearrange("p (k q) -> p k q", q=P), xs, ALU.add), st)
                elif kind == "conv":
                    g = arg[0]
                    for m in (2 * g, 2 * g + 1):
                        taken(dve, ("proj", "ux", m))
                        dve.wait_ge(pad_zero, 1)
                        c_, u_ = lc[:, m % 4, :], uxp[:, m % 2, :]
                        link(v.tensor_scalar(c_, u_[:, 3:3 + S], G("conv_w_2", 24 + m), G("conv_b_2", m), ALU.mult, ALU.add))
                        for tap in (2, 1, 0):
                            ins = v.scalar_tensor_tensor(out=c_, in0=u_[:, tap:tap + S], scalar=G("conv_w_2", 8 * tap + m), in1=c_,
                                                         op0=ALU.mult, op1=ALU.add)
                            if tap:
                                link(ins)
                        ins.then_inc(conv_done, 1)
                elif kind == "lru":
                    g = arg[0]
                    dve.wait_ge(lru_exp, g + 1)
                    taken(dve, ("lru_gate", "i", 2 * g))
                    taken(dve, ("lru_gate", "i", 2 * g + 1))
                    dve.wait_ge(conv_done, 2 * g + 2)
                    link(v.tensor_tensor(lr_, la, la, ALU.mult))
                    v.scalar_tensor_tensor(out=lt, in0=lr_, scalar=1.0, in1=lt, op0=ALU.add, op1=ALU.mult).then_inc(lru_m2, 1)
                    link(v.tensor_tensor(li, li, lc[:, 2 * g % 4:2 * g % 4 + 2, :], ALU.mult))
                    dve.wait_ge(lru_mult, g + 1)
                    link(v.tensor_tensor(lt, lt, li, ALU.mult))
                    for m in (2 * g, 2 * g + 1):
                        v.tensor_tensor_scan(yl[:, m, :], la[:, m % 2, :], lt[:, m % 2, :], 0.0, ALU.mult, ALU.add).then_inc(lru_done, 1)
                    dve.wait_ge(lru_done, 2 * g + 2)
                elif kind == "stick":
                    def log_sum(h):
                        dve.wait_ge(sp_log, h + 1)
                        link(v.scalar_tensor_tensor(out=Lb[h % 2], in0=flat(h), scalar=0.0, in1=Lb[h % 2], op0=ALU.max, op1=ALU.add))
                        v.tensor_copy(Lhigh[h % 2], Lb[h % 2]).then_inc(sp_done, 1)

                    finished(dve, ("proj", "v2", 15))
                    for dst, name in ((ident_b, "ident"), (bias_b, "stickbias"), (tri_r, "negtri"), (ones_r, "negones")):
                        ins = v.tensor_copy(dst, C(name))
                    ins.then_inc(stick_set, 1)
                    dve.wait_ge(yl_done, KD)
                    log_sum(0)
                    log_sum(1)
                    for h in range(HB + 1):
                        if h >= 1:
                            lo = CH * ((h - 1) % 2)
                            dve.wait_ge(pv_done, h)
                            v.tensor_copy(q2[lo:lo + CH, (h - 1) // 2, :], ps_[lo:lo + CH, 6 + (h - 1) % 2, :]).then_inc(pv_out, 1)
                        if h + 2 < HB:
                            log_sum(h + 2)


def constants():
    c = np.zeros((P, NCONST), np.float32)

    def put(name, x):
        lo, hi = CONST[name]
        c[:, lo:hi] = x

    r, q = np.arange(P)[:, None], np.arange(P)[None, :]
    put("ident", r == q)
    put("ones", 1)
    put("blk", r // 64 == q // 64)
    put("before", r < q)
    put("chunkmask", (r // CH == q // CH) & (r <= q))
    put("negtri", -1.0 * (r >= q))
    put("negones", -1)
    put("stickbias", np.where(r >= q, -2.0 ** 100, 0))
    dist = r + (S - P) - np.arange(S)[None, :]
    put("alibi", np.where(dist >= 0, -dist, -BIG))
    put("reset", (np.arange(S) % CH != 0)[None, :])
    put("half", np.arange(P)[:, None] // CH == np.arange(2)[None, :])
    put("thresholds", CAP * np.arange(1, 8)[None, :])
    put("first32", 32 - np.arange(32)[None, :])
    put("first4", 4 - np.arange(4)[None, :])
    put("expert", np.arange(32)[None, :])
    put("overblock", np.arange(NOVER)[None, :])
    put("column", q)
    put("eps", EPS)
    put("one", 1)
    return c


def gains(x):
    g = np.zeros((P, NGAIN), np.float32)
    for name, (lo, hi) in GAINS.items():
        if name == "router_bias":
            g[:, lo:hi] = np.concatenate([x["b_router_group"][0], x["b_router_expert"][0].reshape(-1)])[None, :]
            continue
        w = np.asarray(x[name]).reshape(-1)
        if w.size == 64:
            w = np.concatenate([w, w])
        g[:, lo:hi] = w.reshape(hi - lo, P).T
    return g


BIGS = ["w_in", "w_gla_gk", "w_mem_kv", "w_out", "w_gate", "w_up", "w_down", "w_in_2", "w_br_lru_2", "w_br_att_2",
        "w_out_2", "w_mlp_up_2", "w_mlp_down_2", "w_ple_gate_2", "w_ple_2"]


def kernel(**inputs):
    import concourse.bacc as bacc
    from concourse.bass_utils import run_bass_kernel_spmd

    x = {k: np.asarray(v) for k, v in inputs.items()}
    arrays = {k: np.ascontiguousarray(x[k]) for k in BIGS}
    arrays["xT"] = np.ascontiguousarray(x["x"][0].T)
    arrays["memT"] = np.ascontiguousarray(x["mem"][0].T)
    arrays["pT"] = np.ascontiguousarray(x["p_2"][0, 0].T)
    arrays["consts"] = constants()
    arrays["gains"] = gains(x)
    router = np.concatenate([x["w_router_group"][0], x["w_router_expert"][0].transpose(1, 0, 2).reshape(D, 32)], axis=1)
    arrays["w_router"] = np.ascontiguousarray(router.reshape(KD, P, 36).transpose(1, 0, 2))
    blocks = np.zeros((2 * KD, P, P), np.float32)
    for j, name in enumerate(("w_rgate_2", "w_igate_2")):
        for n in range(2 * KD):
            lo = 64 * (n % 2)
            blocks[2 * (n // 2) + j, lo:lo + 64, lo:lo + 64] = x[name][0, n]
    arrays["gate_blocks"] = blocks
    nc = bacc.Bacc("TRN2", target_bir_lowering=False, num_devices=1)
    a = {k: nc.dram_tensor(k, v.shape, mybir.dt.from_np(v.dtype), kind="ExternalInput").ap() for k, v in arrays.items()}
    out = nc.dram_tensor("outT", (D, S), F32, kind="ExternalOutput").ap()
    build(nc, a, out)
    r = run_bass_kernel_spmd(nc, [arrays], core_ids=[0])
    return np.ascontiguousarray(r.results[0]["outT"].T)[None]
```
